# Optimizing a Trainium2 kernel written in Bass

```python
import jax, jax.numpy as jnp
from jax import lax
import numpy as np

D_MODEL = 1024
BATCH = 1
SEQ = 1024
DEPTH = 1

MIX_WIDTH = D_MODEL
RWKV_WIDTH = MIX_WIDTH // 2
RWKV_HEAD_DIM = 64
RWKV_HEADS = RWKV_WIDTH // RWKV_HEAD_DIM
RWKV_DECAY_LORA = 64
RWKV_AAA_LORA = 64
RWKV_GATE_LORA = 128
RWKV_GN_EPS = 64e-5
GLA_WIDTH = MIX_WIDTH - RWKV_WIDTH
GLA_HEADS = 4
GLA_DV = GLA_WIDTH // GLA_HEADS
GLA_DK = GLA_DV // 2
GLA_KEY_WIDTH = GLA_HEADS * GLA_DK
GLA_GATE_LORA = 16
GLA_GATE_TEMP = 16.0
GLA_CHUNK = 64
CONV_WIDTH = 3
PLE_DIM = 256
D_FF = -(-8 * D_MODEL // (3 * 256)) * 256
NORM_EPS = 1e-6

RWKV_SPLITS = (RWKV_WIDTH, 2 * RWKV_WIDTH, 3 * RWKV_WIDTH,
               3 * RWKV_WIDTH + 2 * RWKV_DECAY_LORA,
               3 * RWKV_WIDTH + 2 * RWKV_DECAY_LORA + RWKV_AAA_LORA)
RWKV_IN_WIDTH = RWKV_SPLITS[-1] + RWKV_GATE_LORA
GLA_SPLITS = (2 * GLA_KEY_WIDTH + GLA_WIDTH, 2 * GLA_KEY_WIDTH + 2 * GLA_WIDTH)
GLA_IN_WIDTH = GLA_SPLITS[-1] + 2 * GLA_GATE_LORA
IN_WIDTH = RWKV_IN_WIDTH + GLA_IN_WIDTH


def rms_norm(x, w, eps=NORM_EPS):
    xf = x.astype(jnp.float32)
    y = xf * lax.rsqrt(jnp.mean(xf * xf, axis=-1, keepdims=True) + eps)
    return (y * w.astype(jnp.float32)).astype(x.dtype)

def centred_shift(z):
    zp = jnp.pad(z, ((0, 0), (1, 1), (0, 0)))
    return 0.5 * (zp[:, :-2] + zp[:, 2:])

def centred_dwconv(z, w):
    pad = (w.shape[0] - 1) // 2
    return lax.conv_general_dilated(z, w.astype(z.dtype), window_strides=(1,),
                                    padding=[(pad, pad)],
                                    dimension_numbers=('NWC', 'WIO', 'NWC'),
                                    feature_group_count=z.shape[-1])

def rwkv7_scan(r, decay, k, v, kk, b, reverse):
    B, T, H, N = r.shape
    xs = tuple(jnp.moveaxis(t, 1, 0) for t in (r, decay, k, v, kk, b))

    def step(S, inp):
        r_t, w_t, k_t, v_t, kk_t, b_t = inp
        sa = jnp.einsum('bhij,bhj->bhi', S, -kk_t)
        S = (S * w_t[:, :, None, :] + sa[..., None] * b_t[:, :, None, :]
             + v_t[..., None] * k_t[:, :, None, :])
        return S, jnp.einsum('bhij,bhj->bhi', S, r_t)

    S0 = jnp.zeros((B, H, N, N), r.dtype)
    _, y = lax.scan(step, S0, xs, reverse=reverse)
    return jnp.moveaxis(y, 0, 1)

def rwkv7_mixer(z, w0, w_up, a0, a_up, g_up, k_k, k_a, r_k, ln_w, ln_b, out_dtype):
    B, T, _ = z.shape
    z = z.astype(jnp.float32)
    r, k, v, w_lo, a_lo, g_lo = jnp.split(z, RWKV_SPLITS, axis=-1)
    w_lo = w_lo.reshape(B, T, 2, RWKV_DECAY_LORA)
    w_log = -jax.nn.softplus(-(w0 + jnp.einsum('btdr,drc->btdc', jnp.tanh(w_lo), w_up))) - 0.5
    decay = jnp.exp(-jnp.exp(w_log))
    a = jax.nn.sigmoid(a0 + a_lo @ a_up)
    g = jax.nn.sigmoid(g_lo) @ g_up

    def heads(t):
        return t.reshape(B, T, RWKV_HEADS, RWKV_HEAD_DIM)

    kk = heads(k * k_k)
    kk = kk * lax.rsqrt(jnp.maximum(jnp.sum(kk * kk, axis=-1, keepdims=True), 1e-24))
    k = k * (1.0 + (a - 1.0) * k_a)
    r_h, k_h, v_h, a_h = heads(r), heads(k), heads(v), heads(a)
    b_h = kk * a_h
    y = (rwkv7_scan(r_h, heads(decay[:, :, 0]), k_h, v_h, kk, b_h, False)
         + rwkv7_scan(r_h, heads(decay[:, :, 1]), k_h, v_h, kk, b_h, True))
    mu = jnp.mean(y, axis=-1, keepdims=True)
    var = jnp.mean(jnp.square(y - mu), axis=-1, keepdims=True)
    y = heads(((y - mu) * lax.rsqrt(var + RWKV_GN_EPS)).reshape(B, T, RWKV_WIDTH) * ln_w + ln_b)
    bonus = jnp.sum(r_h * k_h * r_k, axis=-1, keepdims=True) * v_h
    y = (y + bonus).reshape(B, T, RWKV_WIDTH)
    return (y * g).astype(out_dtype)

def gla_chunked(q, k, v, log_a):
    B, H, T, DK = q.shape
    DV = v.shape[-1]
    nc = T // GLA_CHUNK

    def to_chunks(t):
        return t.reshape(B, H, nc, GLA_CHUNK, t.shape[-1]).transpose(2, 0, 1, 3, 4)

    qc, kc, vc = to_chunks(q), to_chunks(k), to_chunks(v)
    bc = jnp.cumsum(to_chunks(log_a), axis=-2)
    mask = jnp.tril(jnp.ones((GLA_CHUNK, GLA_CHUNK), dtype=bool))[:, :, None]

    def step(S, inp):
        q_c, k_c, v_c, b_c = inp
        o_inter = jnp.einsum('bhcd,bhde->bhce', q_c * jnp.exp(b_c), S)
        diff = b_c[:, :, :, None, :] - b_c[:, :, None, :, :]
        dmat = jnp.exp(jnp.where(mask, diff, -jnp.inf))
        scores = jnp.einsum('bhid,bhjd,bhijd->bhij', q_c, k_c, dmat)
        o_intra = jnp.einsum('bhij,bhje->bhie', scores, v_c)
        b_last = b_c[:, :, -1:, :]
        S = (S * jnp.exp(b_last[:, :, 0, :])[..., None]
             + jnp.einsum('bhcd,bhce->bhde', k_c * jnp.exp(b_last - b_c), v_c))
        return S, o_inter + o_intra

    S0 = jnp.zeros((B, H, DK, DV), q.dtype)
    _, o = lax.scan(step, S0, (qc, kc, vc, bc))
    return o.transpose(1, 2, 0, 3, 4).reshape(B, H, T, DV)

def gla_mixer(z, conv_w, a_up, a_b, norm_w, out_dtype):
    B, T, _ = z.shape
    z = z.astype(jnp.float32)
    qkv, g, a_lo = jnp.split(z, GLA_SPLITS, axis=-1)
    qkv = jax.nn.silu(centred_dwconv(qkv, conv_w))
    q, k, v = jnp.split(qkv, (GLA_KEY_WIDTH, 2 * GLA_KEY_WIDTH), axis=-1)
    a_lo = a_lo.reshape(B, T, 2, GLA_GATE_LORA)
    log_a = jax.nn.log_sigmoid(jnp.einsum('btdr,drc->btdc', a_lo, a_up) + a_b) / GLA_GATE_TEMP

    def heads(t, d):
        return t.reshape(B, T, GLA_HEADS, d).transpose(0, 2, 1, 3)

    def flip(t):
        return jnp.flip(t, axis=2)

    q_h = heads(q, GLA_DK) * GLA_DK ** -0.5
    k_h = heads(k, GLA_DK)
    v_h = heads(v, GLA_DV)
    o_f = gla_chunked(q_h, k_h, v_h, heads(log_a[:, :, 0], GLA_DK))
    o_b = flip(gla_chunked(flip(q_h), flip(k_h), flip(v_h), flip(heads(log_a[:, :, 1], GLA_DK))))
    o = (o_f + o_b).transpose(0, 2, 1, 3)
    o = rms_norm(o, norm_w) * jax.nn.silu(g.reshape(B, T, GLA_HEADS, GLA_DV))
    return o.reshape(B, T, GLA_WIDTH).astype(out_dtype)

def first_inputs(seed: int = 0) -> dict:
    key = jax.random.key(seed)
    ks = jax.random.split(key, 32)
    L = DEPTH
    f32 = jnp.float32

    def nrm(k, shape, scale):
        return jax.random.normal(k, shape, f32) * scale

    def gain(k, shape):
        return 1.0 + 0.05 * jax.random.normal(k, shape, f32)

    return {
        'x': jax.random.normal(ks[0], (BATCH, SEQ, D_MODEL), f32),
        'p': jax.random.normal(ks[1], (DEPTH, BATCH, SEQ, PLE_DIM), f32),
        'norm_mix_pre': gain(ks[2], (L, D_MODEL)),
        'norm_mix_post': gain(ks[3], (L, D_MODEL)),
        'norm_ffn_pre': gain(ks[4], (L, D_MODEL)),
        'norm_ffn_post': gain(ks[5], (L, D_MODEL)),
        'norm_ple': gain(ks[6], (L, D_MODEL)),
        'w_in': nrm(ks[7], (L, D_MODEL, IN_WIDTH), D_MODEL ** -0.5),
        'rwkv_mu': jax.random.uniform(ks[8], (L, RWKV_IN_WIDTH), f32),
        'rwkv_w0': jax.random.uniform(ks[9], (L, 2, RWKV_WIDTH), f32, -6.0, -1.0),
        'rwkv_w_up': nrm(ks[10], (L, 2, RWKV_DECAY_LORA, RWKV_WIDTH), RWKV_DECAY_LORA ** -0.5),
        'rwkv_a0': nrm(ks[11], (L, RWKV_WIDTH), 0.3),
        'rwkv_a_up': nrm(ks[12], (L, RWKV_AAA_LORA, RWKV_WIDTH), 0.5 * RWKV_AAA_LORA ** -0.5),
        'rwkv_g_up': nrm(ks[13], (L, RWKV_GATE_LORA, RWKV_WIDTH), RWKV_GATE_LORA ** -0.5),
        'rwkv_k_k': 0.85 + 0.05 * jax.random.normal(ks[14], (L, RWKV_WIDTH), f32),
        'rwkv_k_a': gain(ks[15], (L, RWKV_WIDTH)),
        'rwkv_r_k': nrm(ks[16], (L, RWKV_HEADS, RWKV_HEAD_DIM), 0.1),
        'rwkv_ln_w': gain(ks[17], (L, RWKV_WIDTH)),
        'rwkv_ln_b': nrm(ks[18], (L, RWKV_WIDTH), 0.02),
        'gla_conv': nrm(ks[19], (L, CONV_WIDTH, 1, 2 * GLA_KEY_WIDTH + GLA_WIDTH), CONV_WIDTH ** -0.5),
        'gla_a_up': nrm(ks[20], (L, 2, GLA_GATE_LORA, GLA_KEY_WIDTH), GLA_GATE_LORA ** -0.5),
        'gla_a_b': 2.0 + 0.5 * jax.random.normal(ks[21], (L, 2, GLA_KEY_WIDTH), f32),
        'gla_norm': gain(ks[22], (L, GLA_DV)),
        'w_out': nrm(ks[23], (L, MIX_WIDTH, D_MODEL), MIX_WIDTH ** -0.5),
        'ffn_gate': nrm(ks[24], (L, D_MODEL, D_FF), D_MODEL ** -0.5),
        'ffn_up': nrm(ks[25], (L, D_MODEL, D_FF), D_MODEL ** -0.5),
        'ffn_down': nrm(ks[26], (L, D_FF, D_MODEL), D_FF ** -0.5),
        'ple_proj': nrm(ks[27], (L, PLE_DIM, D_MODEL), PLE_DIM ** -0.5),
        'ple_gate': nrm(ks[28], (L, D_MODEL, D_MODEL), D_MODEL ** -0.5),
        'ple_gate_b': nrm(ks[29], (L, D_MODEL), 0.02),
    }

def first_block(x, p, norm_mix_pre, norm_mix_post, norm_ffn_pre, norm_ffn_post, norm_ple,
              w_in, rwkv_mu, rwkv_w0, rwkv_w_up, rwkv_a0, rwkv_a_up, rwkv_g_up,
              rwkv_k_k, rwkv_k_a, rwkv_r_k, rwkv_ln_w, rwkv_ln_b,
              gla_conv, gla_a_up, gla_a_b, gla_norm, w_out,
              ffn_gate, ffn_up, ffn_down, ple_proj, ple_gate, ple_gate_b):
    h = x
    for i in range(DEPTH):
        xn = rms_norm(h, norm_mix_pre[i])
        z = xn @ w_in[i]
        z_rwkv, z_gla = z[..., :RWKV_IN_WIDTH], z[..., RWKV_IN_WIDTH:]
        z_rwkv = z_rwkv + rwkv_mu[i] * (centred_shift(z_rwkv) - z_rwkv)
        y_rwkv = rwkv7_mixer(z_rwkv, rwkv_w0[i], rwkv_w_up[i], rwkv_a0[i], rwkv_a_up[i],
                             rwkv_g_up[i], rwkv_k_k[i], rwkv_k_a[i], rwkv_r_k[i],
                             rwkv_ln_w[i], rwkv_ln_b[i], h.dtype)
        y_gla = gla_mixer(z_gla, gla_conv[i], gla_a_up[i], gla_a_b[i], gla_norm[i], h.dtype)
        y = jnp.concatenate([y_rwkv, y_gla], axis=-1) @ w_out[i]
        h = h + rms_norm(y, norm_mix_post[i])
        hn = rms_norm(h, norm_ffn_pre[i])
        f = (jax.nn.silu(hn @ ffn_gate[i]) * (hn @ ffn_up[i])) @ ffn_down[i]
        h = h + rms_norm(f, norm_ffn_post[i])
        e = p[i] @ ple_proj[i]
        gate = jax.nn.sigmoid(h @ ple_gate[i] + ple_gate_b[i])
        h = h + rms_norm(gate * e, norm_ple[i])
    return h


CHUNK = 64
N_MIXERS = 2
N_HEADS = 16
HEAD_DIM = D_MODEL // N_HEADS
LEFT_CHUNKS = 8
BAND = (LEFT_CHUNKS + 1) * CHUNK
MAX_REL_DIST = 256
N_REL = 2 * MAX_REL_DIST + 1
D_FF_2 = (((8 * D_MODEL + 2) // 3 + 255) // 256) * 256
N_CONV_LAYERS = (DEPTH + N_MIXERS - 1) // N_MIXERS
N_ATTN_LAYERS = DEPTH // N_MIXERS
N_ADA = 6
RMS_EPS = 1e-6
NEG_INF = -1e30


def rms_norm_2(x, g):
    xf = x.astype(jnp.float32)
    y = xf * lax.rsqrt(jnp.mean(xf * xf, axis=-1, keepdims=True) + RMS_EPS)
    return (y * g.astype(jnp.float32)).astype(x.dtype)

def modulate(h, shift, scale):
    return h * (1.0 + scale[:, None, :]) + shift[:, None, :]

def short_conv_mixer(h, w_in, w_conv, w_out):
    d = h.shape[-1]
    bcv = h @ w_in
    gate_b, gate_c, v = jnp.split(bcv, 3, axis=-1)
    u = gate_c * v
    conv = lax.conv_general_dilated(
        u, w_conv[:, None, :].astype(u.dtype),
        window_strides=(1,), padding=[(CONV_WIDTH - 1, 0)],
        dimension_numbers=("NWC", "WIO", "NWC"), feature_group_count=d)
    return (gate_b * conv) @ w_out

def _rel_bias_index():
    qi = np.arange(CHUNK)[:, None]
    kj = np.arange(BAND)[None, :]
    dist = qi + LEFT_CHUNKS * CHUNK - kj
    return (np.clip(dist, -MAX_REL_DIST, MAX_REL_DIST) + MAX_REL_DIST).astype(np.int32)

def chunked_rel_attention(h, w_qkv, rel_bias, w_out):
    b, s, d = h.shape
    n_chunks = s // CHUNK
    qkv = (h @ w_qkv).reshape(b, s, 3, N_HEADS, HEAD_DIM)
    q = qkv[:, :, 0] * (HEAD_DIM ** -0.5)
    k = qkv[:, :, 1]
    v = qkv[:, :, 2]
    pad = ((0, 0), (LEFT_CHUNKS * CHUNK, 0), (0, 0), (0, 0))
    k_pad = jnp.pad(k, pad)
    v_pad = jnp.pad(v, pad)
    q_chunks = q.reshape(b, n_chunks, CHUNK, N_HEADS, HEAD_DIM).transpose(1, 0, 2, 3, 4)
    bias = rel_bias.astype(jnp.float32)[:, jnp.asarray(_rel_bias_index())]
    key_slot = jnp.arange(BAND)

    def one_chunk(args):
        n, qc = args
        kb = lax.dynamic_slice_in_dim(k_pad, n * CHUNK, BAND, axis=1)
        vb = lax.dynamic_slice_in_dim(v_pad, n * CHUNK, BAND, axis=1)
        scores = jnp.einsum("bqhd,bkhd->bhqk", qc, kb).astype(jnp.float32) + bias[None]
        valid = key_slot >= (LEFT_CHUNKS - n) * CHUNK
        scores = jnp.where(valid[None, None, None, :], scores, NEG_INF)
        p = jax.nn.softmax(scores, axis=-1).astype(vb.dtype)
        return jnp.einsum("bhqk,bkhd->bqhd", p, vb)

    out = lax.map(one_chunk, (jnp.arange(n_chunks, dtype=jnp.int32), q_chunks))
    out = out.transpose(1, 0, 2, 3, 4).reshape(b, s, d)
    return out @ w_out

def swiglu(h, w_gate_up, w_down):
    g, u = jnp.split(h @ w_gate_up, 2, axis=-1)
    return (jax.nn.silu(g) * u) @ w_down

def second_inputs(seed: int = 0) -> dict:
    key = jax.random.key(seed)
    ks = jax.random.split(key, 14)
    f32 = jnp.float32
    sd = D_MODEL ** -0.5
    x = jax.random.normal(ks[0], (BATCH, SEQ, D_MODEL), f32)
    c = jax.random.normal(ks[1], (BATCH, D_MODEL), f32)
    ada_w = jax.random.normal(ks[2], (DEPTH, D_MODEL, N_ADA * D_MODEL), f32) * (0.5 * sd)
    ada_b = jax.random.normal(ks[3], (DEPTH, N_ADA * D_MODEL), f32) * 0.02
    norm_gains = 1.0 + 0.02 * jax.random.normal(ks[4], (DEPTH, 4, D_MODEL), f32)
    conv_w_in = jax.random.normal(ks[5], (N_CONV_LAYERS, D_MODEL, 3 * D_MODEL), f32) * sd
    conv_w = jax.random.normal(ks[6], (N_CONV_LAYERS, CONV_WIDTH, D_MODEL), f32) * (CONV_WIDTH ** -0.5)
    conv_w_out = jax.random.normal(ks[7], (N_CONV_LAYERS, D_MODEL, D_MODEL), f32) * sd
    attn_w_qkv = jax.random.normal(ks[8], (N_ATTN_LAYERS, D_MODEL, 3 * D_MODEL), f32) * sd
    attn_rel_bias = jax.random.normal(ks[9], (N_ATTN_LAYERS, N_HEADS, N_REL), f32) * 0.1
    attn_w_out = jax.random.normal(ks[10], (N_ATTN_LAYERS, D_MODEL, D_MODEL), f32) * sd
    ffn_w_gate_up = jax.random.normal(ks[11], (DEPTH, D_MODEL, 2 * D_FF_2), f32) * sd
    ffn_w_down = jax.random.normal(ks[12], (DEPTH, D_FF_2, D_MODEL), f32) * (D_FF_2 ** -0.5)
    return {"x": x, "c": c, "ada_w": ada_w, "ada_b": ada_b, "norm_gains": norm_gains,
            "conv_w_in": conv_w_in, "conv_w": conv_w, "conv_w_out": conv_w_out,
            "attn_w_qkv": attn_w_qkv, "attn_rel_bias": attn_rel_bias, "attn_w_out": attn_w_out,
            "ffn_w_gate_up": ffn_w_gate_up, "ffn_w_down": ffn_w_down}

def second_block(x, c, ada_w, ada_b, norm_gains, conv_w_in, conv_w, conv_w_out,
              attn_w_qkv, attn_rel_bias, attn_w_out, ffn_w_gate_up, ffn_w_down):
    c_act = jax.nn.silu(c)
    for i in range(DEPTH):
        mod = c_act @ ada_w[i] + ada_b[i]
        sh_m, sc_m, g_m, sh_f, sc_f, g_f = jnp.split(mod, N_ADA, axis=-1)
        h = modulate(rms_norm_2(x, norm_gains[i, 0]), sh_m, sc_m)
        j = i // N_MIXERS
        if i % N_MIXERS == 0:
            h = short_conv_mixer(h, conv_w_in[j], conv_w[j], conv_w_out[j])
        else:
            h = chunked_rel_attention(h, attn_w_qkv[j], attn_rel_bias[j], attn_w_out[j])
        x = x + g_m[:, None, :] * rms_norm_2(h, norm_gains[i, 1])
        h = modulate(rms_norm_2(x, norm_gains[i, 2]), sh_f, sc_f)
        h = swiglu(h, ffn_w_gate_up[i], ffn_w_down[i])
        x = x + g_f[:, None, :] * rms_norm_2(h, norm_gains[i, 3])
    return x


def setup_inputs(seed=0):
    out = dict(first_inputs(seed))
    for name, value in second_inputs(seed + 1).items():
        if name != "x":
            out[name + "_2"] = value
    return out


def reference(
    x, p, norm_mix_pre, norm_mix_post, norm_ffn_pre, norm_ffn_post, norm_ple, w_in, rwkv_mu,
    rwkv_w0, rwkv_w_up, rwkv_a0, rwkv_a_up, rwkv_g_up, rwkv_k_k, rwkv_k_a, rwkv_r_k, rwkv_ln_w,
    rwkv_ln_b, gla_conv, gla_a_up, gla_a_b, gla_norm, w_out, ffn_gate, ffn_up, ffn_down,
    ple_proj, ple_gate, ple_gate_b, c_2, ada_w_2, ada_b_2, norm_gains_2, conv_w_in_2, conv_w_2,
    conv_w_out_2, attn_w_qkv_2, attn_rel_bias_2, attn_w_out_2, ffn_w_gate_up_2, ffn_w_down_2,
):
    x = first_block(
        x, p, norm_mix_pre, norm_mix_post, norm_ffn_pre, norm_ffn_post, norm_ple, w_in, rwkv_mu,
        rwkv_w0, rwkv_w_up, rwkv_a0, rwkv_a_up, rwkv_g_up, rwkv_k_k, rwkv_k_a, rwkv_r_k,
        rwkv_ln_w, rwkv_ln_b, gla_conv, gla_a_up, gla_a_b, gla_norm, w_out, ffn_gate, ffn_up,
        ffn_down, ple_proj, ple_gate, ple_gate_b,
    )
    return second_block(
        x, c_2, ada_w_2, ada_b_2, norm_gains_2, conv_w_in_2, conv_w_2, conv_w_out_2,
        attn_w_qkv_2, attn_rel_bias_2, attn_w_out_2, ffn_w_gate_up_2, ffn_w_down_2,
    )


_drawn_inputs = setup_inputs


def setup_inputs(seed=0):
    import zlib

    import numpy as np

    out = dict(_drawn_inputs(seed))
    spreads = {}
    factors = {'rwkv_ln_b': 5.726,
     'gla_a_up': 2.943,
     'ple_gate_b': 8.0,
     'ada_b_2': 3.321,
     'norm_gains_2': 7.216}
    for name, (base, spread) in spreads.items():
        noise = np.random.default_rng([zlib.crc32(name.encode()), seed]).standard_normal(out[name].shape)
        drawn = base * np.exp(spread * noise) if base else spread * noise
        out[name] = __import__('jax').numpy.asarray(drawn.astype(out[name].dtype))
    for name, factor in factors.items():
        out[name] = (out[name] * factor).astype(out[name].dtype)
    return out
```

```python
from contextlib import ExitStack

import numpy as np

import concourse.bass as bass
from concourse import mybir

P = 128
T = 1024
D = 1024
KD = D // P
HALF = 512
FF = 2816
NF = FF // P
HEAD_PAIRS = 4
BLK = 128
NBLK = T // BLK
CH = 64
NZR = 15
NZG = 13
DECAY = float(np.exp(-0.5))
LEVELS = [1, 2, 4, 8, 16, 32, 64]

F32 = mybir.dt.float32
F32R = mybir.dt.float32r
ALU = mybir.AluOpType
ACT = mybir.ActivationFunctionType
ds = bass.ds

VEC_FIELDS = [
    ("norm_mix_pre", 8), ("norm_mix_post", 8), ("norm_ffn_pre", 8), ("norm_ffn_post", 8), ("norm_ple", 8),
    ("mu", NZR), ("w0", 8), ("a0", 4), ("k_k", 4), ("k_a", 4), ("r_k", 4), ("ln_w", 4), ("ln_b", 4),
    ("conv", 24), ("a_b", 4), ("gla_norm", 1), ("ple_b", 8), ("c", 8), ("ada_b", 48), ("gains2", 32),
    ("conv2", 24),
]
VEC = {}
_at = 0
for _name, _n in VEC_FIELDS:
    VEC[_name] = _at
    _at += _n
NVEC = _at

CONST_FIELDS = [("ident", 1), ("ones", 1), ("head_ones", 1), ("eye64", 1), ("eps", 1),
                ("chunk_keep", 16), ("score_mask", 4), ("level_t", 12), ("level1_m", 2),
                ("block_keep", 16), ("gla_diag", 1), ("gla_level", 7)]
CONST = {}
_at = 0
for _name, _n in CONST_FIELDS:
    CONST[_name] = _at
    _at += _n
NCONST = _at
N_STAY = CONST["chunk_keep"]
EPS_RMS, EPS_GN, EPS_ZERO = 0, 1, 2


def constants():
    out = np.zeros((P, NCONST, P), np.float32)
    p, j = np.arange(P)[:, None], np.arange(P)[None, :]
    out[:, CONST["ident"]] = p == j
    out[:, CONST["ones"]] = 1
    out[:, CONST["head_ones"]] = p // 64 == j // 64
    out[:, CONST["eye64"]] = p % 64 == j % 64
    out[:, CONST["eps"], EPS_RMS] = 1e-6
    out[:, CONST["eps"], EPS_GN] = 64e-5
    t = np.arange(T)
    out[:, CONST["chunk_keep"]:CONST["chunk_keep"] + 8] = (t % CH != 0).reshape(8, P)[None]
    out[:, CONST["chunk_keep"] + 8:CONST["chunk_keep"] + 16] = (t % CH != CH - 1).reshape(8, P)[None]
    out[:, CONST["block_keep"]:CONST["block_keep"] + 8] = (t % BLK != 0).reshape(8, P)[None]
    out[:, CONST["block_keep"] + 8:CONST["block_keep"] + 16] = (t % BLK != BLK - 1).reshape(8, P)[None]
    same = p // CH == j // CH
    for d in range(2):
        before = (p < j) if d == 0 else (p > j)
        out[:, CONST["score_mask"] + 2 * d] = same & before
        out[:, CONST["score_mask"] + 2 * d + 1] = same & (before | (p == j))
        for n, s in enumerate(LEVELS[:6]):
            pair = (p // (2 * s) == j // (2 * s)) & (p // s != j // s)
            out[:, CONST["level_t"] + 2 * n + d] = pair & before
        out[:, CONST["level1_m"] + d] = (p // 2 == j // 2) & ((p > j) if d == 0 else (p < j))
    for n, s in enumerate(LEVELS):
        out[:, CONST["gla_level"] + n] = (p // (2 * s) == j // (2 * s)) & (p // s != j // s)
    out[:, CONST["gla_diag"]] = 2.0 * (p == j)
    return out.reshape(P, NCONST * P)


class Core:

    def __init__(self, nc, ctx):
        self.nc, self.ctx, self.sems = nc, ctx, []

    def sem(self, name):
        self.sems.append(self.nc.alloc_semaphore(name=name))
        return self.sems[-1]

    def clear_sems(self):
        self.nc.clear_and_free_semaphores(self.sems)
        self.nc.all_engine_barrier()
        self.sems = []


def cst(core, name):
    a = CONST[name] * P
    return core.const[:, a:a + P]


class Marks:

    def __init__(self, sem, names):
        self.sem, self.names, self.next = sem, names, 0

    def begin(self, engine):
        engine.sem_inc(self.sem, 1)

    def before(self, turn):
        return self.sem, turn * len(self.names) + 1
        assert len(set(names)) == len(names)

    def __call__(self, name):
        assert self.names[self.next % len(self.names)] == name, (name, self.names[self.next % len(self.names)])
        self.next += 1
        return self.sem, 1

    def by(self, name, turn=0):
        return self.sem, turn * len(self.names) + (self.names.index(name) + 2)


def eps(core, which):
    a = CONST["eps"] * P + which
    return core.const[:, a:a + 1]


def vec(core, name, n=0):
    return core.vec[:, ds(VEC[name] + n, 1)] if not isinstance(n, int) else core.vec[:, VEC[name] + n:VEC[name] + n + 1]


def tile_of(buf, n):
    if isinstance(n, int):
        return buf[:, n, :]
    return buf[:, ds(n, 1), :].rearrange("p a t -> p (a t)")


def walk(e, segments, unroll, body):
    total = segments[-1][1]
    for a, b, kind in segments:
        m = a
        while m < min(b, unroll if a == 0 else a):
            body(m, m % 6, m // 3 if kind == "third" else kind)
            m += 1
        last = b - 1 if b == total else b
        turns = max(0, (last - m) // unroll)
        if turns > 1:
            with e.Fori(0, turns) as i:
                for u in range(unroll):
                    body(i * unroll + (m + u), (m + u) % 6 if unroll == 6 else (m + u) % 2,
                         i * 2 + (m + u) // 3 if kind == "third" else kind)
            m += turns * unroll
        while m < b:
            body(m, m % 6, m // 3 if kind == "third" else kind)
            m += 1


def dense(core, name, weights, act_hi, act_lo, segments, act_epilogue, dve_epilogue=None, pool_epilogue=None,
          unroll=2, act_first=None, dve_first=None, pool_first=None):
    nc = core.nc
    total = segments[-1][1]
    kt = weights.shape[2] // P
    with ExitStack() as ctx:
        raw = ctx.enter_context(nc.sbuf_tensor(f"{name}_raw", [P, 2, kt, P], F32))
        w_hi = ctx.enter_context(nc.sbuf_tensor(f"{name}_whi", [P, 2, kt, P], F32R))
        w_lo = ctx.enter_context(nc.sbuf_tensor(f"{name}_wlo", [P, 2, kt, P], F32R))
        acc = ctx.enter_context(nc.psum_tensor(f"{name}_acc", [P, 2, T], F32))
        loaded = [core.sem(f"{name}_loaded{s}") for s in range(2)]
        hi_ready, lo_ready, filled, drained = (core.sem(f"{name}_{x}") for x in
                                               ("hi_ready", "lo_ready", "filled", "drained"))
        block = ctx.enter_context(nc.Block())

        @block.sync
        def _(sp):
            def load(m, r, kind):
                if not (isinstance(m, int) and m < 2):
                    sp.wait_ge(lo_ready, m - 1)
                src = weights[m] if isinstance(m, int) else weights[ds(m, 1)].rearrange("a p k -> (a p) k")
                sp.dma_start(raw[:, r % 2].rearrange("p k c -> p (k c)"), src).then_inc(loaded[r % 2], 16)
            walk(sp, [(0, total, None)], 2, load)

        @block.scalar
        def _(act):
            if act_first:
                act_first(act)

            def split_hi(m, slot, first):
                act.wait_ge(loaded[slot], (m - slot) * 8 + 16)
                if not first:
                    act.wait_ge(filled, m - 1)
                act.copy(w_hi[:, slot], raw[:, slot]).then_inc(hi_ready, 1)

            def body(m, r, kind):
                if not (isinstance(m, int) and m + 1 >= total):
                    split_hi(m + 1, (r + 1) % 2, isinstance(m, int) and m == 0)
                act_epilogue(act, m, r, kind, acc[:, r % 2], filled, drained)
            split_hi(0, 0, True)
            walk(act, segments, unroll, body)

        @block.vector
        def _(dve):
            if dve_first:
                dve_first(dve)

            def split_lo(m, slot):
                dve.wait_ge(hi_ready, m + 1)
                dve.tensor_tensor(w_lo[:, slot], raw[:, slot], w_hi[:, slot].bitcast(F32),
                                  ALU.subtract).then_inc(lo_ready, 1)

            def body(m, r, kind):
                if not (isinstance(m, int) and m + 1 >= total):
                    split_lo(m + 1, (r + 1) % 2)
                if dve_epilogue:
                    dve_epilogue(dve, m, r, kind, drained)
            split_lo(0, 0)
            walk(dve, segments, unroll, body)

        @block.gpsimd
        def _(pool):
            if pool_first:
                pool_first(pool)
            if pool_epilogue:
                walk(pool, segments, unroll, lambda m, r, kind: pool_epilogue(pool, m, r, kind, drained))

        @block.tensor
        def _(pe):
            def body(m, r, kind):
                slot = r % 2
                pe.wait_ge(lo_ready, m + 1)
                if not (isinstance(m, int) and m < 2):
                    pe.wait_ge(drained, m - 1)
                for k in range(kt):
                    for w, x in ((w_hi, act_hi), (w_hi, act_lo), (w_lo, act_hi)):
                        for h in range(2):
                            mm = pe.matmul(acc[:, slot, h * HALF:(h + 1) * HALF], w[:, slot, k],
                                           x[:, k, h * HALF:(h + 1) * HALF],
                                           start=(k == 0 and w is w_hi and x is act_hi),
                                           stop=(k == kt - 1 and w is w_lo))
                mm.then_inc(filled, 1)
            walk(pe, segments, unroll, body)


def joint(core, name, y, y_gain, h, gain, shift, hi, lo, store=None):
    nc = core.nc
    stages = [s for s in ("y", "h") if (s == "y" and y is not None) or (s == "h" and hi is not None and gain is not None)]
    with ExitStack() as ctx:
        sq = ctx.enter_context(nc.sbuf_tensor(f"{name}_sq", [P, 2, HALF], F32))
        rs = ctx.enter_context(nc.sbuf_tensor(f"{name}_rs", [P, 2, HALF], F32))
        tmp = ctx.enter_context(nc.sbuf_tensor(f"{name}_tmp", [P, 2, HALF], F32))
        sums = ctx.enter_context(nc.psum_tensor(f"{name}_sums", [P, 2, HALF], F32))
        sq_ready, sq_used, root_ready, recip, h_ready, normed, hi_done, tmp_ready, lo_done, stored = (
            core.sem(f"{name}_{x}") for x in ("sq_ready", "sq_used", "root_ready", "recip", "h_ready",
                                              "normed", "hi_done", "tmp_ready", "lo_done", "stored"))
        n_stages = len(stages)
        block = ctx.enter_context(nc.Block())

        def cols(hf):
            return slice(hf * HALF, (hf + 1) * HALF)

        def low_part(dve, hf, m):
            dve.wait_ge(hi_done, hf * KD + m + 1)
            src = tmp[:, m % 2] if gain is not None else h[:, m, cols(hf)]
            dve.scalar_tensor_tensor(lo[:, m, cols(hf)], src, shift[:, m:m + 1] if shift is not None else 0.0,
                                     hi[:, m, cols(hf)].bitcast(F32), ALU.add, ALU.subtract).then_inc(lo_done, 1)

        @block.scalar
        def _(act):
            count = 0
            for hf in range(2):
                for n, stage in enumerate(stages):
                    src = y if stage == "y" else h
                    for m in range(KD):
                        if count >= 2:
                            act.wait_ge(sq_used, count - 1)
                        if stage == "h" and y is not None:
                            act.wait_ge(h_ready, hf * KD + m + 1)
                        act.activation(sq[:, count % 2], src[:, m, cols(hf)], ACT.Square).then_inc(sq_ready, 1)
                        count += 1
                    act.wait_ge(sq_used, count)
                    if hf * n_stages + n >= 2:
                        act.wait_ge(h_ready if stage == "y" else normed, KD)
                    act.activation(rs[:, (hf * n_stages + n) % 2], sums[:, (hf * n_stages + n) % 2], ACT.Sqrt,
                                   bias=eps(core, EPS_RMS), scale=1.0 / D).then_inc(root_ready, 1)
                if hi is not None:
                    for m in range(KD):
                        if gain is not None:
                            act.wait_ge(normed, hf * KD + m + 1)
                            src = tmp[:, m % 2]
                        else:
                            if y is not None:
                                act.wait_ge(h_ready, hf * KD + m + 1)
                            src = h[:, m, cols(hf)]
                        act.activation(hi[:, m, cols(hf)], src, ACT.Identity,
                                       bias=shift[:, m:m + 1] if shift is not None else 0.0).then_inc(hi_done, 1)

        @block.tensor
        def _(pe):
            count = 0
            for hf in range(2):
                for n, stage in enumerate(stages):
                    if hf * n_stages + n >= 2:
                        pe.wait_ge(root_ready, hf * n_stages + n - 1)
                    for m in range(KD):
                        pe.wait_ge(sq_ready, count + 1)
                        count += 1
                        mm = pe.matmul(sums[:, (hf * n_stages + n) % 2], cst(core, "ones"), sq[:, (count - 1) % 2],
                                       start=(m == 0), stop=(m == KD - 1))
                        mm.then_inc(sq_used, 1)

        @block.vector
        def _(dve):
            tmps = 0
            for hf in range(2):
                for n, stage in enumerate(stages):
                    r = rs[:, (hf * n_stages + n) % 2]
                    dve.wait_ge(root_ready, hf * n_stages + n + 1)
                    dve.reciprocal(r, r).then_inc(recip, 1)
                    dve.wait_ge(recip, hf * n_stages + n + 1)
                    if stage == "y":
                        for m in range(KD):
                            dve.scalar_tensor_tensor(y[:, m, cols(hf)], y[:, m, cols(hf)], y_gain[:, m:m + 1], r,
                                                     ALU.mult, ALU.mult).then_inc(tmp_ready, 1)
                            dve.wait_ge(tmp_ready, hf * KD + m + 1)
                            dve.tensor_tensor(h[:, m, cols(hf)], h[:, m, cols(hf)], y[:, m, cols(hf)],
                                              ALU.add).then_inc(h_ready, 1)
                    else:
                        for m in range(KD):
                            if tmps >= 2:
                                dve.wait_ge(lo_done, tmps - 1)
                            dve.scalar_tensor_tensor(tmp[:, m % 2], h[:, m, cols(hf)], gain[:, m:m + 1], r,
                                                     ALU.mult, ALU.mult).then_inc(normed, 1)
                            tmps += 1
                            if m >= 1:
                                low_part(dve, hf, m - 1)
                        low_part(dve, hf, KD - 1)
                if hi is not None and gain is None:
                    for m in range(KD):
                        low_part(dve, hf, m)

        @block.sync
        def _(sp):
            if store is not None:
                for hf in range(2):
                    sp.wait_ge(h_ready, (hf + 1) * KD)
                    sp.dma_start(store[:, :, cols(hf)], h[:, :, cols(hf)]).then_inc(stored, 16)
                sp.wait_ge(stored, 32)


def gla_project(core, w, xn_hi, xn_lo, z, lora):
    nc = core.nc
    with ExitStack() as ctx:
        edge = ctx.enter_context(nc.sbuf_tensor("gp_edge", [P, 2, T + 2], F32))
        mix = ctx.enter_context(nc.sbuf_tensor("gp_mix", [P, T], F32))
        edged, raw_z, part, mixed, used = (core.sem(f"gp_{x}") for x in ("edged", "raw_z", "part", "mixed", "used"))
        segments = [(0, 8, "conv"), (8, 12, "gate"), (12, 13, "lora")]

        def dve_first(dve):
            dve.memset(edge[:, :, :], 0.0).then_inc(edged, 1)

        def act_first(act):
            act.wait_ge(edged, 1)

        def act_epilogue(act, m, r, kind, psum, filled, drained):
            act.wait_ge(filled, m + 1)
            if kind == "conv":
                act.copy(edge[:, r % 2, 1:T + 1], psum).then_inc(drained, 1)
                act.wait_ge(drained, m + 1)
                act.wait_ge(mixed, m + 1)
                act.activation(tile_of(z, m), mix[:, :], ACT.Silu).then_inc(used, 1)
            elif kind == "gate":
                act.activation(tile_of(z, m), psum, ACT.Silu).then_inc(drained, 1)
            else:
                act.copy(lora, psum).then_inc(drained, 1)

        def dve_epilogue(dve, m, r, kind, drained):
            if kind != "conv":
                return
            x = edge[:, r % 2]
            dve.wait_ge(drained, m + 1)
            if not (isinstance(m, int) and m == 0):
                dve.wait_ge(used, m)
            taps = [vec(core, "conv", t * 8 + m) for t in range(3)]
            dve.tensor_scalar(mix[:, :], x[:, 0:T], taps[0], None, ALU.mult).then_inc(part, 1)
            dve.wait_ge(part, m * 2 + 1)
            dve.scalar_tensor_tensor(mix[:, :], x[:, 1:T + 1], taps[1], mix[:, :], ALU.mult,
                                     ALU.add).then_inc(part, 1)
            dve.wait_ge(part, m * 2 + 2)
            dve.scalar_tensor_tensor(mix[:, :], x[:, 2:T + 2], taps[2], mix[:, :], ALU.mult,
                                     ALU.add).then_inc(mixed, 1)

        dense(core, "gp", w, xn_hi, xn_lo, segments, act_epilogue, dve_epilogue, act_first=act_first,
              dve_first=dve_first)


def gla_decay(core, dram_const, dram_a_up, lora, sums):
    nc = core.nc
    with ExitStack() as ctx:
        a_up = ctx.enter_context(nc.sbuf_tensor("gd_aup", [P, 2 * P], F32))
        keep = ctx.enter_context(nc.sbuf_tensor("gd_keep", [P, 2, T], F32))
        away = ctx.enter_context(nc.sbuf_tensor("gd_away", [P, T], F32))
        low = ctx.enter_context(nc.sbuf_tensor("gd_low", [P, 2, T], F32))
        gate = ctx.enter_context(nc.psum_tensor("gd_gate", [P, 4, T], F32))
        loaded, products, act_did, dve_did = (core.sem(f"gd_{x}") for x in ("loaded", "products", "act", "dve"))
        cases = [(d, i) for d in range(2) for i in range(2)]
        act_made = Marks(act_did, ["abs", "exp", "ln"])
        dve_made = Marks(dve_did, ["min", "log_sigmoid", "scan"])
        block = ctx.enter_context(nc.Block())

        @block.sync
        def _(sp):
            sp.dma_start(a_up[:, :], dram_a_up).then_inc(loaded, 16)
            c = CONST["block_keep"] * P
            sp.dma_start(keep[:, :, :].rearrange("p d t -> p (d t)"), dram_const[:, c:c + 2 * T]).then_inc(loaded, 16)

        @block.tensor
        def _(pe):
            pe.wait_ge(loaded, 32)
            for n, (d, i) in enumerate(cases):
                rows = slice(32 * d, 32 * d + 16)
                for h in range(2):
                    mm = pe.matmul(gate[:, n, h * HALF:(h + 1) * HALF], a_up[rows, i * P:(i + 1) * P],
                                   lora[rows, h * HALF:(h + 1) * HALF], start=True, stop=True)
                mm.then_inc(products, 1)

        @block.scalar
        def _(act):
            act_made.begin(act)
            for n, (d, i) in enumerate(cases):
                act.wait_ge(products, n + 1)
                if n:
                    act.wait_ge(*dve_made.by("log_sigmoid", n - 1))
                act.activation(away[:, :], gate[:, n], ACT.Abs, bias=vec(core, "a_b", n)).then_inc(*act_made("abs"))
                act.wait_ge(*act_made.by("abs", n))
                act.activation(away[:, :], away[:, :], ACT.Exp, scale=-1.0).then_inc(*act_made("exp"))
                act.wait_ge(*act_made.by("exp", n))
                act.activation(away[:, :], away[:, :], ACT.Ln, bias=1.0).then_inc(*act_made("ln"))

        @block.vector
        def _(dve):
            dve_made.begin(dve)
            dve.wait_ge(loaded, 32)
            for n, (d, i) in enumerate(cases):
                ls = low[:, n % 2]
                dve.wait_ge(*act_made.by("abs", n))
                dve.tensor_scalar(ls, gate[:, n], vec(core, "a_b", n), 0.0, ALU.add,
                                  ALU.min).then_inc(*dve_made("min"))
                dve.wait_ge(*dve_made.by("min", n))
                dve.wait_ge(*act_made.by("ln", n))
                dve.tensor_tensor(ls, ls, away[:, :], ALU.subtract).then_inc(*dve_made("log_sigmoid"))
                dve.wait_ge(*dve_made.by("log_sigmoid", n))
                out = sums[:, d, i]
                if d == 0:
                    dve.tensor_tensor_scan(out, keep[:, 0], ls, 0.0, ALU.mult, ALU.add).then_inc(*dve_made("scan"))
                else:
                    dve.tensor_tensor_scan(out[:, ::-1], keep[:, 1, ::-1], ls[:, ::-1], 0.0, ALU.mult,
                                           ALU.add).then_inc(*dve_made("scan"))


def gla_direction(core, dram_const, z, sums, y, d):
    nc = core.nc
    levels = range(7) if d == 0 else []
    scored = (["diag"] + [f"level{n}" for n in levels]) if d == 0 else []
    with ExitStack() as ctx:
        def sb(name, shape):
            return ctx.enter_context(nc.sbuf_tensor(f"g{d}_{name}", shape, F32))

        def psum(name, shape):
            return ctx.enter_context(nc.psum_tensor(f"g{d}_ps_{name}", shape, F32))
        mask = sb("mask", [P, 8, BLK])
        summed = sb("summed", [P, 2, 2, BLK])
        qk = sb("qk", [P, 2, 2, BLK])
        v = sb("v", [P, 4, BLK])
        diff_s = sb("diff_s", [P, 2, 2, BLK])
        grown_s = sb("grown_s", [P, 2, 2, BLK])
        qk_s = sb("qk_s", [P, 2, 2, BLK])
        diff = sb("diff", [P, 2, 2, 2, BLK])
        grown = sb("grown", [P, 2, 2, 2, BLK])
        qk_l = sb("qk_l", [P, 2, 2, 2, BLK])
        v_tok = sb("v_tok", [P, 4, BLK])
        k_tok = sb("k_tok", [P, 2, BLK])
        part = sb("part", [P, 2, 4, BLK])
        score = sb("score", [P, 4, BLK])
        state = sb("state", [P, 2, BLK])
        ps_score = psum("score", [P, 2, 2, 512])
        ps_v = psum("v", [P, 4, BLK])
        ps_k = psum("k", [P, 4, BLK])
        ps_o = psum("o", [P, 2, 512])
        loaded, zeroed = core.sem(f"g{d}_loaded"), core.sem(f"g{d}_zeroed")
        dve_steps = ["summed", "k", "diff_s", "qk_s"]
        if d == 0:
            dve_steps += ["diff_level0"]
            for n in levels:
                dve_steps += ([f"diff_level{n + 1}"] if n < 6 else []) + [f"qk_level{n}", f"part_{scored[n]}"]
            dve_steps += ["part_level6"]
        dve_steps += ["state0", "state1"] + (["y0", "y1"] if d else [])
        act_steps = ["q", "v", "exp_s", "v_tok", "k_tok"] + [f"exp_level{n}" for n in levels] + (
            ["y0", "y1"] if d == 0 else [])
        dve_made = Marks(core.sem(f"g{d}_dve"), dve_steps)
        act_made = Marks(core.sem(f"g{d}_act"), act_steps)
        pool_made = Marks(core.sem(f"g{d}_pool"), [f"sum_{r}" for r in scored[1:]] or ["none"])
        pe_made = Marks(core.sem(f"g{d}_pe"), ["v_tok", "k_tok"] + [f"score_{r}" for r in scored] + ["out", "gain"])
        block = ctx.enter_context(nc.Block())

        def tokens(j):
            return ds(j * BLK if d == 0 else (NBLK - 1) * BLK - j * BLK, BLK)

        @block.sync
        def _(sp):
            c = CONST["gla_diag"] * P
            sp.dma_start(mask[:, :, :].rearrange("p a t -> p (a t)"), dram_const[:, c:c + 8 * P]).then_inc(loaded, 16)

        @block.scalar
        def _(act):
            act_made.begin(act)
            with act.Fori(0, NBLK) as j:
                act.wait_ge(*pe_made.before(j))
                act.wait_ge(*dve_made.before(j))
                act.mul(qk[:, 0], z[:, 0:2, tokens(j)], 0.125).then_inc(*act_made("q"))
                act.copy(v[:, :, :], z[:, 4:8, tokens(j)]).then_inc(*act_made("v"))
                act.wait_ge(*dve_made.by("diff_s", j))
                act.activation(grown_s[:, :, :, :], diff_s[:, :, :, :], ACT.Exp,
                               scale=1 / 16).then_inc(*act_made("exp_s"))
                act.wait_ge(*pe_made.by("v_tok", j))
                act.copy(v_tok[:, :, :], ps_v[:, :, :]).then_inc(*act_made("v_tok"))
                act.wait_ge(*pe_made.by("k_tok", j))
                act.copy(k_tok[:, :, :], ps_k[:, 0:2]).then_inc(*act_made("k_tok"))
                for n in levels:
                    act.wait_ge(*dve_made.by(f"diff_level{n}", j))
                    if n >= 2:
                        act.wait_ge(*dve_made.by(f"qk_level{n - 2}", j))
                    act.activation(grown[:, n % 2], diff[:, n % 2], ACT.Exp,
                                   scale=1 / 16).then_inc(*act_made(f"exp_level{n}"))
                if d == 0:
                    act.wait_ge(*pe_made.by("out", j))
                    for par in range(2):
                        act.copy(y[:, par:par + 3:2, tokens(j)],
                                 ps_o[:, par, 0:2 * BLK].rearrange("p (i t) -> p i t", i=2)
                                 ).then_inc(*act_made(f"y{par}"))

        @block.gpsimd
        def _(pool):
            if d == 0:
                pool_made.begin(pool)
                with pool.Fori(0, NBLK) as j:
                    for n, r in enumerate(scored[1:], 1):
                        pool.wait_ge(*dve_made.by(f"part_{r}", j))
                        if n == 1:
                            pool.wait_ge(*pe_made.before(j))
                            pool.tensor_tensor(score[:, :, :], part[:, 0], part[:, 1],
                                               ALU.add).then_inc(*pool_made(f"sum_{r}"))
                        else:
                            pool.wait_ge(*pool_made.by(f"sum_{scored[n - 1]}", j))
                            pool.tensor_tensor(score[:, :, :], score[:, :, :], part[:, n % 2],
                                               ALU.add).then_inc(*pool_made(f"sum_{r}"))

        @block.tensor
        def _(pe):
            pe_made.begin(pe)
            pe.wait_ge(zeroed, 1)
            with pe.Fori(0, NBLK) as j:
                pe.wait_ge(*act_made.by("v", j))
                for i in range(4):
                    mm = pe.transpose(ps_v[:, i], v[:, i], cst(core, "ident"))
                mm.then_inc(*pe_made("v_tok"))
                pe.wait_ge(*dve_made.by("qk_s", j))
                for i in range(2):
                    mm = pe.transpose(ps_k[:, i], qk_s[:, 1, i], cst(core, "ident"))
                mm.then_inc(*pe_made("k_tok"))
                for n, r in enumerate(scored):
                    if r == "diag":
                        pe.wait_ge(*act_made.by("q", j))
                        src = qk
                    else:
                        pe.wait_ge(*dve_made.by(f"qk_{r}", j))
                        src = qk_l[:, (n - 1) % 2]
                    if n >= 2:
                        pe.wait_ge(*dve_made.by(f"part_{scored[n - 2]}", j))
                    for par in range(2):
                        rows = slice(64 * par, 64 * par + 64)
                        for i in range(2):
                            mm = pe.matmul(ps_score[:, n % 2, par, i * BLK:(i + 1) * BLK], src[rows, 1, i],
                                           src[rows, 0, i], start=True, stop=True)
                    mm.then_inc(*pe_made(f"score_{r}"))
                pe.wait_ge(*act_made.by("k_tok", j))
                pe.wait_ge(*dve_made.before(j))
                if d == 0:
                    pe.wait_ge(*act_made.before(j))
                    pe.wait_ge(*pool_made.by(f"sum_{scored[-1]}", j))
                for par in range(2):
                    rows = slice(64 * par, 64 * par + 64)
                    for i in range(2):
                        out = ps_o[:, par, i * BLK:(i + 1) * BLK]
                        if d == 0:
                            pe.matmul(out, v_tok[:, 2 * i + par], score[:, 2 * par + i], start=True, stop=False)
                        mm = pe.matmul(out, state[rows, i], qk_s[rows, 0, i], start=(d == 1), stop=True)
                mm.then_inc(*pe_made("out"))
                for par in range(2):
                    for i in range(2):
                        mm = pe.matmul(ps_k[64 * par:64 * par + 64, 2 + i], k_tok[:, i, 64 * par:64 * par + 64],
                                       v_tok[:, 2 * i + par], start=True, stop=True)
                mm.then_inc(*pe_made("gain"))

        @block.vector
        def _(dve):
            dve_made.begin(dve)
            dve.memset(state[:, :, :], 0.0).then_inc(zeroed, 1)
            dve.wait_ge(zeroed, 1)
            dve.wait_ge(loaded, 16)

            def halves(x, s):
                return x.rearrange("p i (n o r) -> p (i n) o r", o=2, r=s)

            def level_diff(j, n):
                s = LEVELS[n]
                fwd, bwd = halves(summed[:, 0], s), halves(summed[:, 1], s)
                q_out, k_out = halves(diff[:, n % 2, 0], s), halves(diff[:, n % 2, 1], s)
                pairs = 2 * BLK // (2 * s)
                end = fwd[:, :, 0, s - 1:s].to_broadcast([P, pairs, s])
                start = bwd[:, :, 1, 0:1].to_broadcast([P, pairs, s])
                if n >= 2:
                    dve.wait_ge(*act_made.by(f"exp_level{n - 2}", j))
                dve.tensor_tensor(q_out[:, :, 0, :], bwd[:, :, 0, :], start, ALU.subtract)
                dve.tensor_tensor(q_out[:, :, 1, :], fwd[:, :, 1, :], end, ALU.subtract)
                dve.tensor_tensor(k_out[:, :, 0, :], end, fwd[:, :, 0, :], ALU.subtract)
                dve.tensor_tensor(k_out[:, :, 1, :], start, bwd[:, :, 1, :],
                                  ALU.subtract).then_inc(*dve_made(f"diff_level{n}"))

            def masked(j, n):
                r = scored[n]
                dve.wait_ge(*pe_made.by(f"score_{r}", j))
                if n >= 2:
                    dve.wait_ge(*pool_made.by(f"sum_{scored[max(n - 2, 1)]}", j))
                out = part[:, n % 2].rearrange("p (a i) t -> p a (i t)", a=2)
                dve.tensor_tensor(out.rearrange("p a (i t) -> p a i t", i=2),
                                  ps_score[:, n % 2, :, 0:2 * BLK].rearrange("p a (i t) -> p a i t", i=2),
                                  mask[:, n, :].rearrange("p (a i t) -> p a i t", a=1, i=1).to_broadcast([P, 2, 2, BLK]),
                                  ALU.mult).then_inc(*dve_made(f"part_{r}"))

            with dve.Fori(0, NBLK) as j:
                dve.tensor_copy(summed[:, :, :, :], sums[:, :, :, tokens(j)]).then_inc(*dve_made("summed"))
                dve.wait_ge(*pe_made.before(j))
                dve.tensor_copy(qk[:, 1], z[:, 2:4, tokens(j)]).then_inc(*dve_made("k"))
                dve.wait_ge(*dve_made.by("summed", j))
                last = BLK - 1 if d == 0 else 0
                dve.tensor_copy(diff_s[:, 0], summed[:, d])
                dve.tensor_tensor(diff_s[:, 1], summed[:, d, :, last:last + 1].to_broadcast([P, 2, BLK]), summed[:, d],
                                  ALU.subtract).then_inc(*dve_made("diff_s"))
                dve.wait_ge(*act_made.by("exp_s", j))
                dve.wait_ge(*dve_made.by("k", j))
                dve.tensor_tensor(qk_s[:, :, :, :], qk[:, :, :, :], grown_s[:, :, :, :],
                                  ALU.mult).then_inc(*dve_made("qk_s"))
                if d == 0:
                    level_diff(j, 0)
                for n in levels:
                    if n < 6:
                        level_diff(j, n + 1)
                    dve.wait_ge(*act_made.by(f"exp_level{n}", j))
                    if n >= 2:
                        dve.wait_ge(*pe_made.by(f"score_level{n - 2}", j))
                    dve.tensor_tensor(qk_l[:, n % 2], qk[:, :, :, :], grown[:, n % 2],
                                      ALU.mult).then_inc(*dve_made(f"qk_level{n}"))
                    masked(j, n)
                if d == 0:
                    masked(j, 7)
                dve.wait_ge(*pe_made.by("gain", j))
                for i in range(2):
                    dve.scalar_tensor_tensor(state[:, i], state[:, i], grown_s[:, 0, i, last:last + 1], ps_k[:, 2 + i],
                                             ALU.mult, ALU.add).then_inc(*dve_made(f"state{i}"))
                if d == 1:
                    for par in range(2):
                        out = y[:, par:par + 3:2, tokens(j)]
                        dve.tensor_tensor(out, out, ps_o[:, par, 0:2 * BLK].rearrange("p (i t) -> p i t", i=2),
                                          ALU.add).then_inc(*dve_made(f"y{par}"))


def gla_finish(core, z, y):
    nc = core.nc
    with ExitStack() as ctx:
        sq = ctx.enter_context(nc.sbuf_tensor("gf_sq", [P, 2, T], F32))
        rs = ctx.enter_context(nc.sbuf_tensor("gf_rs", [P, 2, T], F32))
        sums = ctx.enter_context(nc.psum_tensor("gf_sums", [P, 2, T], F32))
        squared, summed, root, dve_did = (core.sem(f"gf_{x}") for x in ("squared", "summed", "root", "dve"))
        dve_made = Marks(dve_did, ["recip", "scaled", "gated"])
        block = ctx.enter_context(nc.Block())

        def make_root(act, m):
            act.wait_ge(summed, m + 1)
            if m >= 2:
                act.wait_ge(*dve_made.by("scaled", m - 2))
            act.activation(rs[:, m % 2], sums[:, m % 2], ACT.Sqrt, bias=eps(core, EPS_RMS),
                           scale=1.0 / P).then_inc(root, 1)

        @block.scalar
        def _(act):
            for m in range(4):
                if m >= 2:
                    act.wait_ge(summed, m - 1)
                act.activation(sq[:, m % 2], y[:, m], ACT.Square).then_inc(squared, 1)
                if m >= 1:
                    make_root(act, m - 1)
            make_root(act, 3)

        @block.tensor
        def _(pe):
            for m in range(4):
                pe.wait_ge(squared, m + 1)
                if m >= 2:
                    pe.wait_ge(root, m - 1)
                for h in range(2):
                    mm = pe.matmul(sums[:, m % 2, h * HALF:(h + 1) * HALF], cst(core, "ones"),
                                   sq[:, m % 2, h * HALF:(h + 1) * HALF], start=True, stop=True)
                mm.then_inc(summed, 1)

        @block.vector
        def _(dve):
            dve_made.begin(dve)
            for m in range(4):
                dve.wait_ge(root, m + 1)
                dve.reciprocal(rs[:, m % 2], rs[:, m % 2]).then_inc(*dve_made("recip"))
                dve.wait_ge(*dve_made.by("recip", m))
                dve.scalar_tensor_tensor(y[:, m], y[:, m], vec(core, "gla_norm"), rs[:, m % 2], ALU.mult,
                                         ALU.mult).then_inc(*dve_made("scaled"))
                dve.wait_ge(*dve_made.by("scaled", m))
                dve.tensor_tensor(y[:, m], y[:, m], z[:, 8 + m], ALU.mult).then_inc(*dve_made("gated"))


def rwkv_project(core, w, xn_hi, xn_lo, z):
    nc = core.nc
    with ExitStack() as ctx:
        edge = ctx.enter_context(nc.sbuf_tensor("rp_edge", [P, 2, T + 2], F32))
        around = ctx.enter_context(nc.sbuf_tensor("rp_around", [P, 2, T], F32))
        share = ctx.enter_context(nc.sbuf_tensor("rp_share", [P, 2, NZR], F32))
        edged, around_ready, kept, mixed = (core.sem(f"rp_{x}") for x in ("edged", "around_ready", "kept", "mixed"))

        def dve_first(dve):
            mu = core.vec[:, VEC["mu"]:VEC["mu"] + NZR]
            dve.tensor_scalar(share[:, 0], mu, -1.0, 1.0, ALU.mult, ALU.add).then_inc(edged, 1)
            dve.tensor_scalar(share[:, 1], mu, 0.5, None, ALU.mult).then_inc(edged, 1)
            dve.memset(edge[:, :, :], 0.0).then_inc(edged, 1)
            dve.wait_ge(edged, 3)

        def column(n, m):
            return share[:, n, m:m + 1] if isinstance(m, int) else share[:, n, ds(m, 1)]

        def act_epilogue(act, m, r, kind, psum, filled, drained):
            act.wait_ge(filled, m + 1)
            if not (isinstance(m, int) and m < 2):
                act.wait_ge(mixed, m - 1)
            act.copy(edge[:, r % 2, 1:T + 1], psum).then_inc(drained, 1)

        def pool_epilogue(pool, m, r, kind, drained):
            pool.wait_ge(drained, m + 1)
            x = edge[:, r % 2]
            pool.tensor_tensor(around[:, r % 2], x[:, 0:T], x[:, 2:T + 2], ALU.add).then_inc(around_ready, 1)

        def dve_epilogue(dve, m, r, kind, drained):
            dve.wait_ge(drained, m + 1)
            out = tile_of(z, m)
            dve.tensor_scalar(out, edge[:, r % 2, 1:T + 1], column(0, m), None, ALU.mult).then_inc(kept, 1)
            dve.wait_ge(kept, m + 1)
            dve.wait_ge(around_ready, m + 1)
            dve.scalar_tensor_tensor(out, around[:, r % 2], column(1, m), out, ALU.mult, ALU.add).then_inc(mixed, 1)

        dense(core, "rp", w, xn_hi, xn_lo, [(0, NZR, None)], act_epilogue, dve_epilogue, pool_epilogue,
              act_first=lambda act: act.wait_ge(edged, 3), dve_first=dve_first)


def rwkv_mix(core, dram_const, dram_lora, z):
    nc = core.nc
    n_masks = 16 + 4 + 12 + 2
    levels = range(1, 6)
    with ExitStack() as ctx:
        def sb(name, shape):
            return ctx.enter_context(nc.sbuf_tensor(f"rw_{name}", shape, F32))
        masks = sb("masks", [P, n_masks, P])
        keep = masks[:, 0:16].rearrange("p (d a) t -> p d (a t)", d=2)
        score_mask = masks[:, 16:20]
        level_t = masks[:, 20:32].rearrange("p (l d) t -> p l d t", d=2)
        level1_m = masks[:, 32:34]
        ident = cst(core, "ident")
        eye = ident.rearrange("p (a t) -> p a t", a=1).to_broadcast([P, 2, P])
        lora = sb("lora", [P, 3, 512])
        lora_i = sb("lora_i", [P, 3, P])
        ka_rest = sb("ka_rest", [P, 4])
        sig = sb("sig", [P, 2, T])
        cum = sb("cum", [P, 2, T])
        kk = sb("kk", [P, T])
        b = sb("b", [P, T])
        y2 = sb("y2", [P, 2, T])
        rate, tmp = y2[:, 0], y2[:, 1]
        ex = sb("ex", [P, 2, BLK])
        e_rho = sb("e_rho", [P, 2, BLK])
        e_alpha = sb("e_alpha", [P, 2, BLK])
        e_beta = sb("e_beta", [P, 2, BLK])
        v_b = sb("v_b", [P, 2, BLK])
        ar = sb("ar", [P, 2, 2, BLK])
        bk = sb("bk", [P, 2, 2, BLK])
        rho = sb("rho", [P, 2, BLK])
        decay = sb("decay", [P, 2, 2])
        beta_tok = sb("beta_tok", [P, 2, BLK])
        kv_tok = sb("kv_tok", [P, 4, BLK])
        an = sb("an", [P, 2, 2, BLK])
        mp = sb("mp", [P, 2, 2, 2, BLK])
        nq = sb("nq", [P, 2, 2, 2, BLK])
        m_level = sb("m_level", [P, 2, 5, 2, BLK])
        x = sb("x", [P, 2, 2, BLK])
        xt = sb("xt", [P, 2, 2, BLK])
        yy = sb("yy", [P, 2, 2, BLK])
        wu = sb("wu", [P, 2, 2, BLK])
        rho2 = sb("rho2", [P, 2, BLK])
        carry = sb("carry", [P, 2, 2, CH])
        gain = sb("gain", [P, 2, 2, CH])
        state = sb("state", [P, 2, 2, CH])
        ps = ctx.enter_context(nc.psum_tensor("rw_ps", [P, 8, 512], F32))
        loaded, setup, rest_ready = core.sem("rw_loaded"), core.sem("rw_setup"), core.sem("rw_rest_ready")

        def bank(h, n):
            return ps[:, 4 * h + n]

        def pairs(a):
            return a.rearrange("p (d t) -> p d t", d=2)

        heads = range(2)
        pe_steps = ["tokens_a", "tokens_b"] + [f"{s}{h}" for s in ("beta", "kappa", "m", "nv") for h in heads]
        for n in levels:
            pe_steps += [f"z{n}_{h}" for h in heads]
            pe_steps += [f"{s}{n}_{h}" for h in heads for s in (("x", "xt") if n < 5 else ("xt",))]
        pe_steps += [f"{s}{h}" for s in ("wu", "pw") for h in heads] + [f"chunk{c}_{h}" for h in heads for c in range(2)]
        pe_steps += ["state0_0", "state0_1"] + [f"{s}{h}" for h in heads for s in ("from_state", "state1_", "y")]
        act_steps = ["e_rho0", "e_rho1", "e_beta0", "e_beta1", "e_alpha", "v0", "v1", "rho", "alpha_tok", "beta_tok", "kv_tok",
                     "nv0", "nv1"] + [f"x{n}_{h}" for n in levels if n < 5 for h in heads] + \
            ["wu0", "wu1"] + [f"y{h}_{d}" for h in heads for d in range(2)]
        dve_steps = ["ex0", "ex1", "ar_bk", "decay", "mp0", "mp1", "nq0", "nq1", "x0m", "x1m", "x0", "x1"]
        for n in levels:
            dve_steps += [f"yy{n}_{h}" for h in heads] + [f"xt{n}_{h}" for h in heads]
        dve_steps += ["rho2_0", "rho2_1"] + [f"chunk{c}_{h}" for h in heads for c in range(2)] + \
            [f"state{m}_{h}" for m in range(2) for h in heads]
        pool_steps = ["xt0m", "xt1m", "xt0", "xt1"] + [f"level{n}_{h}" for n in levels for h in heads]
        pe_made, act_made, dve_made, pool_made = (
            Marks(core.sem(f"rw_{n}"), s) for n, s in
            (("pe", pe_steps), ("act", act_steps), ("dve", dve_steps), ("pool", pool_steps)))
        pe_pair = Marks(core.sem("rw_pe_pair"), ["loras", "kk_sum", "y_sum", "var_sum", "bonus_sum", "gate"])
        act_pair = Marks(core.sem("rw_act_pair"), ["lora_i", "sig0", "sig1", "rate", "kk_square", "kk_root",
                                                   "y_square", "y_root"])
        dve_pair = Marks(core.sem("rw_dve_pair"), ["cum0", "cum1", "kk_raw", "kk_floor", "kk_recip", "kk", "k_scale", "k",
                                                   "b", "zero", "y", "centred", "y_recip", "y_scaled", "rk", "bonus",
                                                   "y_sum", "out"])
        block = ctx.enter_context(nc.Block())

        def tokens(d, j):
            return ds(j * BLK if d == 0 else (NBLK - 1) * BLK - j * BLK, BLK)

        @block.sync
        def _(sp):
            c = CONST["chunk_keep"] * P
            sp.dma_start(masks[:, :, :].rearrange("p a t -> p (a t)"),
                         dram_const[:, c:c + n_masks * P]).then_inc(loaded, 16)
            sp.dma_start(lora[:, :, :], dram_lora).then_inc(loaded, 16)

        @block.scalar
        def _(act):
            act_made.begin(act)
            act_pair.begin(act)
            act.wait_ge(loaded, 32)
            act.activation(z[:, 12], z[:, 12], ACT.Tanh).then_inc(setup, 1)
            act.activation(z[:, 14], z[:, 14], ACT.Sigmoid).then_inc(setup, 1)
            with act.Fori(0, HEAD_PAIRS) as i:
                act.wait_ge(*pe_pair.before(i))
                act.copy(lora_i[:, :, :], lora[:, :, ds(i * P, P)]).then_inc(*act_pair("lora_i"))
                act.wait_ge(*pe_pair.by("loras", i))
                act.wait_ge(*dve_pair.before(i))
                for d in range(2):
                    act.activation(sig[:, d], ps[:, 2 * d:2 * d + 2].rearrange("p a t -> p (a t)"), ACT.Sigmoid,
                                   bias=vec(core, "w0", i + 4 * d)).then_inc(*act_pair(f"sig{d}"))
                act.activation(rate, ps[:, 4:6].rearrange("p a t -> p (a t)"), ACT.Sigmoid,
                               bias=vec(core, "a0", i)).then_inc(*act_pair("rate"))
                act.wait_ge(*dve_pair.by("kk_raw", i))
                act.activation(tmp, kk[:, :], ACT.Square).then_inc(*act_pair("kk_square"))
                act.wait_ge(*dve_pair.by("kk_floor", i))
                act.activation(tmp, tmp, ACT.Sqrt).then_inc(*act_pair("kk_root"))
                act.wait_ge(*dve_pair.by("zero", i))
                with act.Fori(0, NBLK) as j:
                    t = i * NBLK + j
                    act.wait_ge(*dve_made.before(t))
                    act.wait_ge(*pe_made.before(t))
                    for d in range(2):
                        act.activation(e_rho[:, d], cum[:, d, tokens(d, j)], ACT.Exp,
                                       scale=-DECAY).then_inc(*act_made(f"e_rho{d}"))
                    for d in range(2):
                        act.activation(e_beta[:, d], cum[:, d, tokens(d, j)], ACT.Exp,
                                       scale=DECAY).then_inc(*act_made(f"e_beta{d}"))
                    act.wait_ge(*dve_made.by("ex1", t))
                    act.activation(e_alpha[:, :, :], ex[:, :, :], ACT.Exp, scale=-DECAY).then_inc(*act_made("e_alpha"))
                    for d in range(2):
                        act.copy(v_b[:, d], tile_of(z, i + 8)[:, tokens(d, j)]).then_inc(*act_made(f"v{d}"))
                    act.wait_ge(*dve_made.by("ar_bk", t))
                    act.copy(rho[:, :, :], ar[:, :, 1]).then_inc(*act_made("rho"))
                    act.wait_ge(*pe_made.by("tokens_a", t))
                    act.copy(an[:, :, :, 0:CH].rearrange("p h d c -> p d h c"),
                             bank(0, 0)[:, 0:2 * P].rearrange("p (d h c) -> p d h c", d=2, h=2)
                             ).then_inc(*act_made("alpha_tok"))
                    act.copy(beta_tok[:, :, :], pairs(bank(0, 0)[:, 2 * P:])).then_inc(*act_made("beta_tok"))
                    act.wait_ge(*pe_made.by("tokens_b", t))
                    act.copy(kv_tok[:, :, :].rearrange("p a t -> p (a t)"), bank(1, 0)).then_inc(*act_made("kv_tok"))
                    for h in heads:
                        act.wait_ge(*pe_made.by(f"nv{h}", t))
                        act.copy(an[:, h, :, CH:], pairs(bank(h, 0)[:, 0:2 * CH])).then_inc(*act_made(f"nv{h}"))
                    for n in levels:
                        for h in heads:
                            if n < 5:
                                act.wait_ge(*pe_made.by(f"x{n}_{h}", t))
                                act.copy(x[:, h], pairs(bank(h, 2)[:, 0:2 * P])).then_inc(*act_made(f"x{n}_{h}"))
                    for h in heads:
                        act.wait_ge(*pe_made.by(f"wu{h}", t))
                        act.copy(wu[:, h], pairs(bank(h, 0)[:, 0:2 * P])).then_inc(*act_made(f"wu{h}"))
                    for h in heads:
                        rows = slice(64 * h, 64 * h + 64)
                        act.wait_ge(*pe_made.by(f"y{h}", t))
                        for d in range(2):
                            act.copy(y2[rows, d, tokens(d, j)],
                                     bank(h, 0)[rows, d * P:(d + 1) * P]).then_inc(*act_made(f"y{h}_{d}"))
                act.wait_ge(*dve_pair.by("centred", i))
                act.activation(kk[:, :], y2[:, 0], ACT.Square).then_inc(*act_pair("y_square"))
                act.wait_ge(*pe_pair.by("var_sum", i))
                act.activation(b[:, :], ps[:, 2:4].rearrange("p a t -> p (a t)"), ACT.Sqrt, bias=eps(core, EPS_GN),
                               scale=1.0 / CH).then_inc(*act_pair("y_root"))

        @block.gpsimd
        def _(pool):
            pool_made.begin(pool)
            pool.wait_ge(loaded, 32)
            with pool.Fori(0, HEAD_PAIRS) as i:
                with pool.Fori(0, NBLK) as j:
                    t = i * NBLK + j
                    for h in heads:
                        pool.wait_ge(*dve_made.by(f"mp{h}", t))
                        pool.tensor_tensor(xt[:, h], mp[:, h, :, 0], level_t[:, 0], ALU.mult).then_inc(*pool_made(f"xt{h}m"))
                    for h in heads:
                        pool.wait_ge(*pool_made.by(f"xt{h}m", t))
                        pool.tensor_tensor(xt[:, h], xt[:, h], eye, ALU.add).then_inc(*pool_made(f"xt{h}"))
                    for n in levels:
                        for h in heads:
                            pool.tensor_tensor(m_level[:, h, n - 1], mp[:, h, :, 0], level_t[:, n],
                                               ALU.mult).then_inc(*pool_made(f"level{n}_{h}"))

        @block.tensor
        def _(pe):
            def head_sums(src, first_bank, mark):
                for hf in range(2):
                    mm = pe.matmul(ps[:, first_bank + hf], cst(core, "head_ones"), src[:, hf * HALF:(hf + 1) * HALF],
                                   start=True, stop=True)
                mm.then_inc(*pe_pair(mark))

            pe_made.begin(pe)
            pe_pair.begin(pe)
            with pe.Fori(0, HEAD_PAIRS) as i:
                pe.wait_ge(setup, 2)
                pe.wait_ge(*act_pair.by("lora_i", i))
                pe.wait_ge(*dve_pair.before(i))
                for n, (rows, w_n, z_n) in enumerate(((slice(0, 64), 0, 12), (slice(64, 128), 0, 12),
                                                      (slice(0, 64), 1, 13))):
                    for hf in range(2):
                        mm = pe.matmul(ps[:, 2 * n + hf], lora_i[rows, w_n], z[rows, z_n, hf * HALF:(hf + 1) * HALF],
                                       start=True, stop=True)
                mm.then_inc(*pe_pair("loras"))
                pe.wait_ge(*act_pair.by("kk_square", i))
                head_sums(tmp, 6, "kk_sum")
                with pe.Fori(0, NBLK) as j:
                    t = i * NBLK + j
                    pe.wait_ge(*dve_made.by("ar_bk", t))
                    pe.wait_ge(*act_made.before(t))
                    for d in range(2):
                        pe.transpose(bank(0, 0)[:, d * P:(d + 1) * P], ar[:, d, 0], ident)
                    for d in range(2):
                        mm = pe.transpose(bank(0, 0)[:, (2 + d) * P:(3 + d) * P], bk[:, 0, d], ident)
                    mm.then_inc(*pe_made("tokens_a"))
                    for d in range(2):
                        pe.transpose(bank(1, 0)[:, d * P:(d + 1) * P], bk[:, 1, d], ident)
                    pe.wait_ge(*act_made.by("v1", t))
                    for d in range(2):
                        mm = pe.transpose(bank(1, 0)[:, (2 + d) * P:(3 + d) * P], v_b[:, d], ident)
                    mm.then_inc(*pe_made("tokens_b"))
                    for n, s in enumerate(("beta", "kappa")):
                        for h in heads:
                            rows = slice(64 * h, 64 * h + 64)
                            for d in range(2):
                                mm = pe.matmul(bank(h, 1 + n)[:, d * 2 * P:(d + 1) * 2 * P], bk[rows, n, d],
                                               ar[rows, d].rearrange("p a t -> p (a t)"), start=True, stop=True)
                            mm.then_inc(*pe_made(f"{s}{h}"))
                    for h in heads:
                        rows = slice(64 * h, 64 * h + 64)
                        for d in range(2):
                            mm = pe.matmul(bank(h, 3)[:, d * P:(d + 1) * P], ar[rows, d, 0], bk[rows, 0, d],
                                           start=True, stop=True)
                        mm.then_inc(*pe_made(f"m{h}"))
                    pe.wait_ge(*act_made.by("kv_tok", t))
                    for h in heads:
                        pe.wait_ge(*dve_made.by(f"nq{h}", t))
                        for d in range(2):
                            mm = pe.matmul(bank(h, 0)[:, d * CH:(d + 1) * CH], nq[:, h, d, 0],
                                           kv_tok[:, 2 + d, h * CH:(h + 1) * CH], start=True, stop=True)
                        mm.then_inc(*pe_made(f"nv{h}"))
                    for n in levels:
                        for h in heads:
                            pe.wait_ge(*pool_made.by(f"level{n}_{h}", t))
                            if n == 1:
                                pe.wait_ge(*dve_made.by(f"x{h}", t))
                            else:
                                pe.wait_ge(*act_made.by(f"x{n - 1}_{h}", t))
                            for d in range(2):
                                mm = pe.matmul(bank(h, 1)[:, d * P:(d + 1) * P], m_level[:, h, n - 1, d], x[:, h, d],
                                               start=True, stop=True)
                            mm.then_inc(*pe_made(f"z{n}_{h}"))
                        for h in heads:
                            pe.wait_ge(*dve_made.by(f"yy{n}_{h}", t))
                            if n > 1:
                                pe.wait_ge(*dve_made.by(f"xt{n - 1}_{h}", t))
                            if n < 5:
                                for d in range(2):
                                    mm = pe.matmul(bank(h, 2)[:, d * P:(d + 1) * P], xt[:, h, d], yy[:, h, d],
                                                   start=True, stop=True)
                                mm.then_inc(*pe_made(f"x{n}_{h}"))
                            for d in range(2):
                                mm = pe.matmul(bank(h, 3)[:, d * P:(d + 1) * P], yy[:, h, d], xt[:, h, d],
                                               start=True, stop=True)
                            mm.then_inc(*pe_made(f"xt{n}_{h}"))
                    for h in heads:
                        pe.wait_ge(*dve_made.by(f"xt5_{h}", t))
                        pe.wait_ge(*act_made.by(f"nv{h}", t))
                        for d in range(2):
                            mm = pe.matmul(bank(h, 0)[:, d * P:(d + 1) * P], xt[:, h, d], an[:, h, d],
                                           start=True, stop=True)
                        mm.then_inc(*pe_made(f"wu{h}"))
                    for h in heads:
                        rows = slice(64 * h, 64 * h + 64)
                        pe.wait_ge(*act_made.by(f"wu{h}", t))
                        for d in range(2):
                            mm = pe.matmul(bank(h, 1)[rows, d * P:(d + 1) * P], wu[:, h, d, 0:CH], mp[:, h, d, 1],
                                           start=True, stop=True)
                        mm.then_inc(*pe_made(f"pw{h}"))
                    for h in heads:
                        rows, cols = slice(64 * h, 64 * h + 64), slice(h * CH, (h + 1) * CH)
                        for c in range(2):
                            at = slice(64 * c, 64 * c + 64)
                            out = bank(h, 2 + c)
                            for d in range(2):
                                pe.matmul(out[rows, d * CH:(d + 1) * CH], wu[at, h, d, 0:CH], beta_tok[at, d, cols],
                                          start=True, stop=True)
                            for d in range(2):
                                here = out[rows, (2 + d) * CH:(3 + d) * CH]
                                pe.matmul(here, beta_tok[at, d, cols], wu[at, h, d, CH:], start=True, stop=False)
                                mm = pe.matmul(here, kv_tok[at, d, cols], kv_tok[at, 2 + d, cols],
                                               start=False, stop=True)
                            mm.then_inc(*pe_made(f"chunk{c}_{h}"))
                    def from_block(h, d):
                        rows, cols = slice(64 * h, 64 * h + 64), slice(h * CH, (h + 1) * CH)
                        out = bank(h, 0)[rows, d * P:(d + 1) * P]
                        pe.matmul(out, wu[:, h, d, CH:], mp[:, h, d, 1], start=(d == 0), stop=False)
                        pe.matmul(out, kv_tok[:, 2 + d, cols], nq[:, h, d, 1], start=False, stop=False)

                    def next_state(h, m):
                        rows = slice(64 * h, 64 * h + 64)
                        for d in range(2):
                            mm = pe.matmul(bank(h, 1)[rows, (2 * m + d) * CH:(2 * m + d + 1) * CH],
                                           carry[rows, m if d == 0 else 1 - m, d], state[rows, m, d],
                                           start=True, stop=True)
                        mm.then_inc(*pe_made(f"state{m}_{h}"))

                    def from_state(h, m, mark):
                        rows = slice(64 * h, 64 * h + 64)
                        for d in range(2):
                            c = m if d == 0 else 1 - m
                            mm = pe.matmul(bank(h, 0)[rows, d * P + c * CH:d * P + (c + 1) * CH],
                                           state[rows, m, d], rho2[rows, d, c * CH:(c + 1) * CH],
                                           start=False, stop=(m == 1 and d == 1))
                        mm.then_inc(*pe_made(mark))

                    for h in heads:
                        pe.wait_ge(*dve_made.by(f"chunk1_{h}", t))
                        from_block(h, 0)
                        next_state(h, 0)
                    for h in heads:
                        pe.wait_ge(*dve_made.by(f"state0_{h}", t))
                        from_block(h, 1)
                        from_state(h, 0, f"from_state{h}")
                        next_state(h, 1)
                        from_state(h, 1, f"y{h}")
                pe.wait_ge(*dve_pair.by("y", i))
                head_sums(y2[:, 0], 0, "y_sum")
                pe.wait_ge(*act_pair.by("y_square", i))
                head_sums(kk, 2, "var_sum")
                pe.wait_ge(*dve_pair.by("rk", i))
                head_sums(y2[:, 1], 4, "bonus_sum")
                for hf in range(2):
                    mm = pe.matmul(ps[:, 6 + hf], lora_i[:, 2], z[:, 14, hf * HALF:(hf + 1) * HALF],
                                   start=True, stop=True)
                mm.then_inc(*pe_pair("gate"))

        @block.vector
        def _(dve):
            dve_made.begin(dve)
            dve_pair.begin(dve)
            dve.tensor_scalar(ka_rest[:, :], core.vec[:, VEC["k_a"]:VEC["k_a"] + 4], -1.0, 1.0, ALU.mult,
                              ALU.add).then_inc(rest_ready, 1)
            dve.wait_ge(rest_ready, 1)
            dve.wait_ge(loaded, 32)

            def wide(first_bank):
                return ps[:, first_bank:first_bank + 2].rearrange("p a t -> p (a t)")

            with dve.Fori(0, HEAD_PAIRS) as i:
                r_i, k_i, v_i = tile_of(z, i + 0), tile_of(z, i + 4), tile_of(z, i + 8)
                dve.wait_ge(*act_pair.by("sig0", i))
                dve.tensor_tensor_scan(cum[:, 0], keep[:, 0], sig[:, 0], 0.0, ALU.mult, ALU.add
                                       ).then_inc(*dve_pair("cum0"))
                dve.wait_ge(*act_pair.by("sig1", i))
                dve.tensor_tensor_scan(cum[:, 1, ::-1], keep[:, 1, ::-1], sig[:, 1, ::-1], 0.0, ALU.mult, ALU.add
                                       ).then_inc(*dve_pair("cum1"))
                dve.tensor_scalar(kk[:, :], k_i, vec(core, "k_k", i), None, ALU.mult).then_inc(*dve_pair("kk_raw"))
                dve.wait_ge(*pe_pair.by("kk_sum", i))
                dve.tensor_scalar(tmp, wide(6), 1e-24, None, ALU.max).then_inc(*dve_pair("kk_floor"))
                dve.wait_ge(*act_pair.by("kk_root", i))
                dve.reciprocal(tmp, tmp).then_inc(*dve_pair("kk_recip"))
                dve.wait_ge(*dve_pair.by("kk_recip", i))
                dve.tensor_tensor(kk[:, :], kk[:, :], tmp, ALU.mult).then_inc(*dve_pair("kk"))
                ka = core.vec[:, ds(VEC["k_a"] + i, 1)]
                dve.wait_ge(*dve_pair.by("kk", i))
                dve.tensor_scalar(tmp, rate, ka, ka_rest[:, ds(i, 1)], ALU.mult, ALU.add).then_inc(*dve_pair("k_scale"))
                dve.wait_ge(*dve_pair.by("k_scale", i))
                dve.tensor_tensor(k_i, k_i, tmp, ALU.mult).then_inc(*dve_pair("k"))
                dve.tensor_tensor(b[:, :], kk[:, :], rate, ALU.mult).then_inc(*dve_pair("b"))
                dve.memset(state[:, 0], 0.0).then_inc(*dve_pair("zero"))
                with dve.Fori(0, NBLK) as j:
                    t = i * NBLK + j
                    dve.wait_ge(*dve_pair.by("zero", i))
                    dve.wait_ge(*act_made.before(t))
                    for d in range(2):
                        at = tokens(d, j)
                        dve.tensor_tensor(ex[:, d], cum[:, d, at], sig[:, d, at], ALU.subtract
                                          ).then_inc(*dve_made(f"ex{d}"))
                    dve.wait_ge(*act_made.by("e_beta1", t))
                    for d in range(2):
                        at = tokens(d, j)
                        dve.tensor_tensor(ar[:, d, 1], r_i[:, at], e_rho[:, d], ALU.mult)
                        dve.tensor_tensor(bk[:, 0, d], b[:, at], e_beta[:, d], ALU.mult)
                        dve.tensor_tensor(bk[:, 1, d], k_i[:, at], e_beta[:, d], ALU.mult)
                    dve.wait_ge(*act_made.by("e_alpha", t))
                    for d in range(2):
                        ins = dve.scalar_tensor_tensor(ar[:, d, 0], kk[:, tokens(d, j)], -1.0, e_alpha[:, d],
                                                       ALU.mult, ALU.mult)
                    ins.then_inc(*dve_made("ar_bk"))
                    dve.tensor_copy(decay[:, 0], e_rho[:, 0, CH - 1::CH])
                    dve.tensor_copy(decay[:, 1], e_rho[:, 1, 0::CH]).then_inc(*dve_made("decay"))
                    for n, (s, dst) in enumerate((("mp", mp), ("nq", nq))):
                        for h in heads:
                            dve.wait_ge(*pe_made.by(("beta", "kappa")[n] + str(h), t))
                            dve.tensor_tensor(dst[:, h].rearrange("p d a t -> p (d a t)"), bank(h, 1 + n),
                                              score_mask.rearrange("p a t -> p (a t)"), ALU.mult
                                              ).then_inc(*dve_made(f"{s}{h}"))
                    for h in heads:
                        dve.wait_ge(*pe_made.by(f"m{h}", t))
                        dve.tensor_tensor(x[:, h], pairs(bank(h, 3)[:, 0:2 * P]), level1_m, ALU.mult
                                          ).then_inc(*dve_made(f"x{h}m"))
                    for h in heads:
                        dve.wait_ge(*dve_made.by(f"x{h}m", t))
                        dve.tensor_tensor(x[:, h], x[:, h], eye, ALU.add).then_inc(*dve_made(f"x{h}"))
                    for n in levels:
                        for h in heads:
                            dve.wait_ge(*pe_made.by(f"z{n}_{h}", t))
                            dve.tensor_tensor(yy[:, h], pairs(bank(h, 1)[:, 0:2 * P]), eye, ALU.add
                                              ).then_inc(*dve_made(f"yy{n}_{h}"))
                        for h in heads:
                            dve.wait_ge(*pe_made.by(f"xt{n}_{h}", t))
                            dve.tensor_copy(xt[:, h], pairs(bank(h, 3)[:, 0:2 * P])).then_inc(*dve_made(f"xt{n}_{h}"))
                    for h in heads:
                        rows = slice(64 * h, 64 * h + 64)
                        dve.wait_ge(*pe_made.by(f"pw{h}", t))
                        dve.wait_ge(*act_made.by("rho", t))
                        dve.tensor_tensor(rho2[rows], pairs(bank(h, 1)[rows, 0:2 * P]), rho[rows], ALU.add
                                          ).then_inc(*dve_made(f"rho2_{h}"))
                    dve.wait_ge(*dve_made.by("decay", t))
                    for h in heads:
                        rows = slice(64 * h, 64 * h + 64)
                        eye64 = cst(core, "eye64")[rows, 0:CH].rearrange("p (a c) -> p a c", a=1).to_broadcast([64, 2, CH])
                        for c in range(2):
                            dve.wait_ge(*pe_made.by(f"chunk{c}_{h}", t))
                            dve.tensor_tensor(carry[rows, c], pairs(bank(h, 2 + c)[rows, 0:2 * CH]), eye64, ALU.add)
                            for d in range(2):
                                ins = dve.tensor_scalar(gain[rows, c, d], bank(h, 2 + c)[rows, (2 + d) * CH:(3 + d) * CH],
                                                        decay[rows, d, c:c + 1], None, ALU.mult)
                            ins.then_inc(*dve_made(f"chunk{c}_{h}"))
                    for m in range(2):
                        for h in heads:
                            rows = slice(64 * h, 64 * h + 64)
                            dve.wait_ge(*pe_made.by(f"state{m}_{h}", t))
                            if m == 0:
                                dve.wait_ge(*dve_made.by(f"chunk1_{h}", t))
                            else:
                                dve.wait_ge(*pe_made.by(f"from_state{h}", t))
                            for d in range(2):
                                c = m if d == 0 else 1 - m
                                ins = dve.scalar_tensor_tensor(
                                    state[rows, 1 - m, d], bank(h, 1)[rows, (2 * m + d) * CH:(2 * m + d + 1) * CH],
                                    decay[rows, d, c:c + 1], gain[rows, c, d], ALU.mult, ALU.add)
                            ins.then_inc(*dve_made(f"state{m}_{h}"))
                dve.wait_ge(*act_made.before((i + 1) * NBLK))
                dve.tensor_tensor(y2[:, 0], y2[:, 0], y2[:, 1], ALU.add).then_inc(*dve_pair("y"))
                dve.wait_ge(*pe_pair.by("y_sum", i))
                dve.wait_ge(*dve_pair.by("y", i))
                dve.scalar_tensor_tensor(y2[:, 0], wide(0), -1.0 / CH, y2[:, 0], ALU.mult, ALU.add
                                         ).then_inc(*dve_pair("centred"))
                dve.wait_ge(*act_pair.by("y_root", i))
                dve.reciprocal(b[:, :], b[:, :]).then_inc(*dve_pair("y_recip"))
                dve.wait_ge(*dve_pair.by("y_recip", i))
                dve.scalar_tensor_tensor(y2[:, 0], y2[:, 0], vec(core, "ln_w", i), b[:, :], ALU.mult, ALU.mult
                                         ).then_inc(*dve_pair("y_scaled"))
                dve.scalar_tensor_tensor(y2[:, 1], r_i, vec(core, "r_k", i), k_i, ALU.mult, ALU.mult
                                         ).then_inc(*dve_pair("rk"))
                dve.wait_ge(*pe_pair.by("bonus_sum", i))
                dve.tensor_tensor(cum[:, 0], wide(4), v_i, ALU.mult).then_inc(*dve_pair("bonus"))
                dve.wait_ge(*dve_pair.by("bonus", i))
                dve.scalar_tensor_tensor(y2[:, 0], y2[:, 0], vec(core, "ln_b", i), cum[:, 0], ALU.add, ALU.add
                                         ).then_inc(*dve_pair("y_sum"))
                dve.wait_ge(*dve_pair.by("y_sum", i))
                dve.wait_ge(*pe_pair.by("gate", i))
                dve.tensor_tensor(r_i, y2[:, 0], wide(6), ALU.mult).then_inc(*dve_pair("out"))


def split_tiles(core, name, sources, hi, lo):
    hi_done, lo_done = core.sem(f"{name}_hi"), core.sem(f"{name}_lo")
    with core.nc.Block() as block:
        @block.scalar
        def _(act):
            for n, src in enumerate(sources):
                act.copy(hi[:, n], src).then_inc(hi_done, 1)

        @block.vector
        def _(dve):
            for n, src in enumerate(sources):
                dve.wait_ge(hi_done, n + 1)
                dve.tensor_tensor(lo[:, n], src, hi[:, n].bitcast(F32), ALU.subtract).then_inc(lo_done, 1)


def swiglu(core, name, w_gate, w_up, w_down, x_hi, x_lo, f, spare):
    nc = core.nc
    with ExitStack() as ctx:
        def sbr(n, shape):
            return ctx.enter_context(nc.sbuf_tensor(f"{name}_{n}", shape, F32R))
        raw = {s: spare[:, n] for n, s in enumerate(("gate", "up", "down"))}
        silu = spare[:, 3]
        w_hi = {s: sbr(f"{s}_hi", [P, KD, P]) for s in raw}
        w_lo = {s: sbr(f"{s}_lo", [P, KD, P]) for s in raw}
        a_hi, a_lo = sbr("a_hi", [P, 2, T]), sbr("a_lo", [P, 2, T])
        a = ctx.enter_context(nc.sbuf_tensor(f"{name}_a", [P, T], F32))
        acc = {s: ctx.enter_context(nc.psum_tensor(f"{name}_ps_{s}", [P, T], F32)) for s in ("gate", "up")}
        acc_down = ctx.enter_context(nc.psum_tensor(f"{name}_ps_down", [P, 2, T], F32))
        dram = {"gate": w_gate, "up": w_up, "down": w_down}
        loaded = {s: core.sem(f"{name}_{s}_loaded") for s in raw}
        hi_ready = {s: core.sem(f"{name}_{s}_hi_ready") for s in raw}
        lo_ready = {s: core.sem(f"{name}_{s}_lo_ready") for s in raw}
        filled = {s: core.sem(f"{name}_{s}_filled") for s in raw}
        zeroed, silu_ready, a_ready, a_hi_ready, a_lo_ready, added = (
            core.sem(f"{name}_{n}") for n in ("zeroed", "silu_ready", "a_ready", "a_hi_ready", "a_lo_ready", "added"))
        block = ctx.enter_context(nc.Block())

        def cycles(e, body):
            body(0, 0)
            body(1, 1)
            with e.Fori(0, (NF - 4) // 2) as i:
                body(i * 2 + 2, 0)
                body(i * 2 + 3, 1)
            body(NF - 2, 0)
            body(NF - 1, 1)

        def more(j):
            return not (isinstance(j, int) and j == NF - 1)

        @block.sync
        def _(sp):
            def body(j, par):
                for s in raw:
                    sp.wait_ge(lo_ready[s], j)
                    src = dram[s][j] if isinstance(j, int) else dram[s][ds(j, 1)].rearrange("a p k -> (a p) k")
                    sp.dma_start(raw[s], src).then_inc(loaded[s], 16)
            cycles(sp, body)

        def split_hi(act, s, j):
            act.wait_ge(loaded[s], j * 16 + 16)
            act.wait_ge(filled[s], j * (KD if s == "down" else 1))
            act.copy(w_hi[s][:, :, :].rearrange("p k c -> p (k c)"), raw[s]).then_inc(hi_ready[s], 1)

        def split_lo(dve, s, j):
            dve.wait_ge(hi_ready[s], j + 1)
            dve.tensor_tensor(w_lo[s][:, :, :].rearrange("p k c -> p (k c)"), raw[s],
                              w_hi[s][:, :, :].rearrange("p k c -> p (k c)").bitcast(F32),
                              ALU.subtract).then_inc(lo_ready[s], 1)

        @block.scalar
        def _(act):
            split_hi(act, "gate", 0)
            split_hi(act, "up", 0)

            def body(j, par):
                act.wait_ge(filled["gate"], j + 1)
                act.wait_ge(a_ready, j)
                act.activation(silu, acc["gate"][:, :], ACT.Silu).then_inc(silu_ready, 1)
                if more(j):
                    split_hi(act, "gate", j + 1)
                    split_hi(act, "up", j + 1)
                act.wait_ge(a_ready, j + 1)
                act.copy(a_hi[:, par], a[:, :]).then_inc(a_hi_ready, 1)
                split_hi(act, "down", j)
            cycles(act, body)

        @block.vector
        def _(dve):
            split_lo(dve, "gate", 0)
            split_lo(dve, "up", 0)
            dve.wait_ge(zeroed, 1)

            def add_down(j):
                for n in range(KD):
                    dve.wait_ge(filled["down"], j * KD + n + 1)
                    dve.tensor_tensor(f[:, n], f[:, n], acc_down[:, n % 2], ALU.add).then_inc(added, 1)

            def body(j, par):
                if more(j):
                    split_lo(dve, "gate", j + 1)
                dve.wait_ge(silu_ready, j + 1)
                dve.wait_ge(filled["up"], j + 1)
                dve.wait_ge(a_lo_ready, j)
                dve.tensor_tensor(a[:, :], silu, acc["up"][:, :], ALU.mult).then_inc(a_ready, 1)
                if more(j):
                    split_lo(dve, "up", j + 1)
                dve.wait_ge(a_hi_ready, j + 1)
                dve.tensor_tensor(a_lo[:, par], a[:, :], a_hi[:, par].bitcast(F32), ALU.subtract).then_inc(a_lo_ready, 1)
                if not (isinstance(j, int) and j == 0):
                    add_down(j - 1)
                split_lo(dve, "down", j)
            cycles(dve, body)
            add_down(NF - 1)

        @block.gpsimd
        def _(pool):
            pool.memset(f, 0.0).then_inc(zeroed, 1)

        @block.tensor
        def _(pe):
            def down(j, par):
                pe.wait_ge(a_lo_ready, j + 1)
                pe.wait_ge(lo_ready["down"], j + 1)
                for n in range(KD):
                    if not (isinstance(j, int) and j == 0 and n < 2):
                        pe.wait_ge(added, j * KD + (n - 1))
                    for w, x in ((w_hi, a_hi), (w_hi, a_lo), (w_lo, a_hi)):
                        for h in range(2):
                            mm = pe.matmul(acc_down[:, n % 2, h * HALF:(h + 1) * HALF], w["down"][:, n],
                                           x[:, par, h * HALF:(h + 1) * HALF],
                                           start=(w is w_hi and x is a_hi), stop=(w is w_lo))
                    mm.then_inc(filled["down"], 1)

            def body(j, par):
                for s in ("gate", "up"):
                    pe.wait_ge(lo_ready[s], j + 1)
                    pe.wait_ge(silu_ready if s == "gate" else a_ready, j)
                    for k in range(KD):
                        for w, x in ((w_hi, x_hi), (w_hi, x_lo), (w_lo, x_hi)):
                            for h in range(2):
                                mm = pe.matmul(acc[s][:, h * HALF:(h + 1) * HALF], w[s][:, k],
                                               x[:, k, h * HALF:(h + 1) * HALF],
                                               start=(k == 0 and w is w_hi and x is x_hi),
                                               stop=(k == KD - 1 and w is w_lo))
                    mm.then_inc(filled[s], 1)
                if not (isinstance(j, int) and j == 0):
                    down(j - 1, 1 - par)
            cycles(pe, body)
            down(NF - 1, 1)


def modulation(core, w, gains):
    nc = core.nc
    n_tiles, ring = 6 * KD, 4
    with ExitStack() as ctx:
        raw = ctx.enter_context(nc.sbuf_tensor("ad_raw", [P, ring, KD, P], F32))
        c = ctx.enter_context(nc.sbuf_tensor("ad_c", [P, KD], F32))
        mod = ctx.enter_context(nc.sbuf_tensor("ad_mod", [P, 6, KD], F32))
        acc = ctx.enter_context(nc.psum_tensor("ad_acc", [P, n_tiles], F32))
        loaded = [core.sem(f"ad_loaded{s}") for s in range(ring)]
        c_ready, used, step = core.sem("ad_c_ready"), core.sem("ad_used"), core.sem("ad_step")
        block = ctx.enter_context(nc.Block())

        @block.sync
        def _(sp):
            for s in range(ring):
                sp.dma_start(raw[:, s].rearrange("p k c -> p (k c)"), w[s]).then_inc(loaded[s], 16)
            with sp.Fori(0, n_tiles // ring - 1) as i:
                for s in range(ring):
                    sp.wait_ge(used, i * ring + s + 1)
                    sp.dma_start(raw[:, s].rearrange("p k c -> p (k c)"),
                                 w[ds(i * ring + ring + s, 1)].rearrange("a p k -> (a p) k")).then_inc(loaded[s], 16)

        @block.scalar
        def _(act):
            act.activation(c[:, :], core.vec[:, VEC["c"]:VEC["c"] + KD], ACT.Silu).then_inc(c_ready, 1)

        @block.tensor
        def _(pe):
            pe.wait_ge(c_ready, 1)
            with pe.Fori(0, n_tiles // ring) as i:
                for s in range(ring):
                    pe.wait_ge(loaded[s], i * 16 + 16)
                    for k in range(KD):
                        mm = pe.matmul(acc[:, ds(i * ring + s, 1)], raw[:, s, k], c[:, k:k + 1],
                                       start=(k == 0), stop=(k == KD - 1))
                    mm.then_inc(used, 1)

        @block.vector
        def _(dve):
            dve.wait_ge(used, n_tiles)
            dve.tensor_tensor(mod[:, :, :].rearrange("p a k -> p (a k)"), acc[:, :],
                              core.vec[:, VEC["ada_b"]:VEC["ada_b"] + n_tiles], ALU.add).then_inc(step, 1)
            dve.wait_ge(step, 1)
            own = core.vec[:, VEC["gains2"]:VEC["gains2"] + 4 * KD].rearrange("p (a k) -> p a k", k=KD)
            for half in range(2):
                shift, scale, gate = (mod[:, 3 * half + n] for n in range(3))
                dve.scalar_tensor_tensor(gains[:, 3 * half], scale, 1.0, own[:, 2 * half], ALU.add, ALU.mult)
                dve.tensor_copy(gains[:, 3 * half + 1], shift)
                dve.tensor_tensor(gains[:, 3 * half + 2], gate, own[:, 2 * half + 1], ALU.mult).then_inc(step, 1)


def project(core, name, w, x_hi, x_lo, out):
    def act_epilogue(act, m, r, kind, psum, filled, drained):
        act.wait_ge(filled, m + 1)
        act.copy(tile_of(out, m), psum).then_inc(drained, 1)
    dense(core, name, w, x_hi, x_lo, [(0, KD, None)], act_epilogue)


def embedding_gate(core, w, h_hi, h_lo, e):
    nc = core.nc
    with ExitStack() as ctx:
        gate = ctx.enter_context(nc.sbuf_tensor("eg_gate", [P, 2, T], F32))
        gated = core.sem("eg_gated")

        def act_epilogue(act, m, r, kind, psum, filled, drained):
            act.wait_ge(filled, m + 1)
            if not (isinstance(m, int) and m < 2):
                act.wait_ge(gated, m - 1)
            act.activation(gate[:, r % 2], psum, ACT.Sigmoid, bias=vec(core, "ple_b", m)).then_inc(drained, 1)

        def dve_epilogue(dve, m, r, kind, drained):
            dve.wait_ge(drained, m + 1)
            dve.tensor_tensor(tile_of(e, m), tile_of(e, m), gate[:, r % 2], ALU.mult).then_inc(gated, 1)

        dense(core, "eg", w, h_hi, h_lo, [(0, KD, None)], act_epilogue, dve_epilogue)


def short_conv(core, w, x_hi, x_lo, y):
    nc = core.nc
    with ExitStack() as ctx:
        cvb = ctx.enter_context(nc.sbuf_tensor("sc_cvb", [P, 3, T], F32))
        u = ctx.enter_context(nc.sbuf_tensor("sc_u", [P, T + 2], F32))
        conv = ctx.enter_context(nc.sbuf_tensor("sc_conv", [P, T], F32))
        padded = core.sem("sc_padded")
        dve_made = Marks(core.sem("sc_dve"), ["u", "tap0", "tap1", "conv", "y"])

        def act_epilogue(act, m, r, jt, psum, filled, drained):
            act.wait_ge(filled, m + 1)
            if not (isinstance(m, int) and m < 3):
                act.wait_ge(*dve_made.by("u" if r % 3 < 2 else "y", jt - 1))
            act.copy(cvb[:, r % 3], psum).then_inc(drained, 1)

        def dve_epilogue(dve, m, r, jt, drained):
            if r % 3 == 1:
                dve.wait_ge(drained, m + 1)
                dve.tensor_tensor(u[:, 2:T + 2], cvb[:, 0], cvb[:, 1], ALU.mult).then_inc(*dve_made("u"))
                dve.wait_ge(*dve_made.by("u", jt))
                dve.tensor_scalar(conv[:, :], u[:, 0:T], vec(core, "conv2", jt), None, ALU.mult
                                  ).then_inc(*dve_made("tap0"))
                dve.wait_ge(*dve_made.by("tap0", jt))
                dve.scalar_tensor_tensor(conv[:, :], u[:, 1:T + 1], vec(core, "conv2", KD + jt), conv[:, :],
                                         ALU.mult, ALU.add).then_inc(*dve_made("tap1"))
                dve.wait_ge(*dve_made.by("tap1", jt))
                dve.scalar_tensor_tensor(conv[:, :], u[:, 2:T + 2], vec(core, "conv2", 2 * KD + jt), conv[:, :],
                                         ALU.mult, ALU.add).then_inc(*dve_made("conv"))
            if r % 3 == 2:
                dve.wait_ge(drained, m + 1)
                dve.wait_ge(*dve_made.by("conv", jt))
                dve.tensor_tensor(tile_of(y, jt), cvb[:, 2], conv[:, :], ALU.mult).then_inc(*dve_made("y"))

        def dve_first(dve):
            dve_made.begin(dve)
            dve.memset(u[:, :], 0.0).then_inc(padded, 1)
            dve.wait_ge(padded, 1)

        dense(core, "sc", w, x_hi, x_lo, [(0, 3 * KD, "third")], act_epilogue, dve_epilogue, unroll=6,
              dve_first=dve_first)


def load_inputs(core, d_vec, d_const, d_x, h):
    nc = core.nc
    loaded = core.sem("in_loaded")
    with nc.Block() as block:
        @block.sync
        def _(sp):
            sp.dma_start(core.vec[:, :], d_vec).then_inc(loaded, 16)
            sp.dma_start(core.const[:, :], d_const[:, 0:N_STAY * P]).then_inc(loaded, 16)
            sp.dma_start(h, d_x).then_inc(loaded, 16)
            sp.wait_ge(loaded, 48)


def load_tiles(core, name, dst, src):
    loaded = core.sem(f"{name}_loaded")
    with core.nc.Block() as block:
        @block.sync
        def _(sp):
            sp.dma_start(dst, src).then_inc(loaded, 16)
            sp.wait_ge(loaded, 16)


def build(nc, a, out, tap=None, stop=None):
    with ExitStack() as ctx:
        core = Core(nc, ctx)
        core.vec = ctx.enter_context(nc.sbuf_tensor("vec", [P, NVEC], F32))
        core.const = ctx.enter_context(nc.sbuf_tensor("const", [P, N_STAY * P], F32))
        big = ctx.enter_context(nc.sbuf_tensor("big", [P, 20, T], F32))
        z, y_gla = big[:, 0:16], big[:, 16:20]

        def dump(view):
            done = core.sem("dumped")
            with nc.Block() as block:
                @block.sync
                def _(sp):
                    sp.dma_start(tap, view).then_inc(done, 16)
                    sp.wait_ge(done, 16)

        h = z[:, 0:8]
        load_inputs(core, a["vec"], a["const"], a["x"], h)
        with ExitStack() as scope:
            xn_hi = scope.enter_context(nc.sbuf_tensor("xn_hi", [P, KD, T], F32R))
            xn_lo = scope.enter_context(nc.sbuf_tensor("xn_lo", [P, KD, T], F32R))
            joint(core, "pre", None, None, h, core.vec[:, VEC["norm_mix_pre"]:VEC["norm_mix_pre"] + 8], None,
                  xn_hi, xn_lo)
            gla_project(core, a["w_gla"], xn_hi, xn_lo, z, z[:, 12])
            with ExitStack() as inner:
                sums = inner.enter_context(nc.sbuf_tensor("gla_sums", [P, 2, 2, T], F32))
                gla_decay(core, a["const"], a["gla_a_up"], z[:, 12], sums)
                gla_direction(core, a["const"], z, sums, y_gla, 0)
                gla_direction(core, a["const"], z, sums, y_gla, 1)
            gla_finish(core, z, y_gla)
            if stop == "gla":
                return dump(y_gla)
            rwkv_project(core, a["w_rwkv"], xn_hi, xn_lo, z)
            if stop == "zr":
                return dump(z[:, 0:15])
        rwkv_mix(core, a["const"], a["lora"], z)
        if stop == "rwkv":
            return dump(z[:, 0:4])
        core.clear_sems()
        gains = ctx.enter_context(nc.sbuf_tensor("gains", [P, 6, KD], F32))
        modulation(core, a["ada"], gains)

        def own(name):
            return core.vec[:, VEC[name]:VEC[name] + KD]

        x_hi = ctx.enter_context(nc.sbuf_tensor("x_hi", [P, KD, T], F32R))
        x_lo = ctx.enter_context(nc.sbuf_tensor("x_lo", [P, KD, T], F32R))
        y, spare = z[:, 8:16], big[:, 16:20]
        split_tiles(core, "ys", [z[:, n] for n in range(4)] + [y_gla[:, n] for n in range(4)], x_hi, x_lo)
        load_tiles(core, "h", h, a["x"])
        project(core, "wo", a["w_out"], x_hi, x_lo, y)
        joint(core, "mix", y, own("norm_mix_post"), h, own("norm_ffn_pre"), None, x_hi, x_lo)
        if stop == "h1":
            return dump(h)
        swiglu(core, "f1", a["ffn_gate"], a["ffn_up"], a["ffn_down"], x_hi, x_lo, y, spare)
        joint(core, "ffn", y, own("norm_ffn_post"), h, None, None, x_hi, x_lo)
        if stop == "h2":
            return dump(h)
        with ExitStack() as scope:
            p_hi = scope.enter_context(nc.sbuf_tensor("p_hi", [P, 2, T], F32R))
            p_lo = scope.enter_context(nc.sbuf_tensor("p_lo", [P, 2, T], F32R))
            load_tiles(core, "p", spare[:, 0:2], a["p"])
            split_tiles(core, "ps", [spare[:, 0], spare[:, 1]], p_hi, p_lo)
            project(core, "pe", a["ple_proj"], p_hi, p_lo, y)
        embedding_gate(core, a["ple_gate"], x_hi, x_lo, y)
        joint(core, "ple", y, own("norm_ple"), h, gains[:, 0], gains[:, 1], x_hi, x_lo)
        if stop == "h3":
            return dump(h)
        short_conv(core, a["conv_in"], x_hi, x_lo, y)
        split_tiles(core, "cs", [y[:, n] for n in range(KD)], x_hi, x_lo)
        project(core, "co", a["conv_out"], x_hi, x_lo, y)
        joint(core, "conv", y, gains[:, 2], h, gains[:, 3], gains[:, 4], x_hi, x_lo)
        swiglu(core, "f2", a["ffn2_gate"], a["ffn2_up"], a["ffn2_down"], x_hi, x_lo, y, spare)
        joint(core, "out", y, gains[:, 5], h, None, None, None, None, store=out)


def tiled(w):
    k, n = w.shape
    nt = -(-n // P)
    full = np.zeros((k, nt * P), w.dtype)
    full[:, :n] = w
    return np.ascontiguousarray(full.reshape(k // P, P, nt, P).transpose(2, 1, 0, 3).reshape(nt, P, k))


def by_tile(v):
    return np.ascontiguousarray(np.asarray(v).reshape(-1, P).T)


def channels_first(x):
    t, c = x.shape
    return np.ascontiguousarray(x.T.reshape(c // P, P, t).transpose(1, 0, 2))


def laid_out(i):
    w_in, mu = i["w_in"][0], i["rwkv_mu"][0]
    zero = lambda n: np.zeros((w_in.shape[0], n), w_in.dtype)
    w_rwkv = np.concatenate([w_in[:, :1728], zero(64), w_in[:, 1728:1856]], axis=1)
    g = w_in[:, 1856:]
    w_gla = np.concatenate([g[:, :1536], g[:, 1536:1552], zero(16), g[:, 1552:1568], zero(80)], axis=1)
    a = {"x": channels_first(i["x"][0]), "p": channels_first(i["p"][0, 0]), "const": constants()}
    a["w_rwkv"], a["w_gla"] = tiled(w_rwkv), tiled(w_gla)
    up = np.zeros((P, 256), w_in.dtype)
    up[0:16], up[32:48] = i["gla_a_up"][0, 0], i["gla_a_up"][0, 1]
    a["gla_a_up"] = up
    lora = np.zeros((P, 3, 512), w_in.dtype)
    lora[:, 0] = i["rwkv_w_up"][0].reshape(P, 512)
    lora[0:64, 1] = i["rwkv_a_up"][0]
    lora[:, 2] = i["rwkv_g_up"][0]
    a["lora"] = lora
    a["w_out"] = tiled(i["w_out"][0])
    for n in ("gate", "up"):
        a[f"ffn_{n}"] = tiled(i[f"ffn_{n}"][0])
    a["ffn_down"] = np.ascontiguousarray(i["ffn_down"][0].reshape(NF, P, D))
    a["ple_proj"], a["ple_gate"] = tiled(i["ple_proj"][0]), tiled(i["ple_gate"][0])
    a["ada"] = tiled(i["ada_w_2"][0])
    c_in = i["conv_w_in_2"][0].reshape(D, 3, KD, P)
    a["conv_in"] = tiled(c_in[:, [1, 2, 0]].transpose(0, 2, 1, 3).reshape(D, 3 * D))
    a["conv_out"] = tiled(i["conv_w_out_2"][0])
    gu = i["ffn_w_gate_up_2"][0]
    a["ffn2_gate"], a["ffn2_up"] = tiled(gu[:, :FF]), tiled(gu[:, FF:])
    a["ffn2_down"] = np.ascontiguousarray(i["ffn_w_down_2"][0].reshape(NF, P, D))
    mu_l = np.concatenate([mu[:1728], np.zeros(64, mu.dtype), mu[1728:]])
    fields = {
        "norm_mix_pre": i["norm_mix_pre"], "norm_mix_post": i["norm_mix_post"], "norm_ffn_pre": i["norm_ffn_pre"],
        "norm_ffn_post": i["norm_ffn_post"], "norm_ple": i["norm_ple"], "mu": mu_l, "w0": i["rwkv_w0"],
        "a0": i["rwkv_a0"], "k_k": i["rwkv_k_k"], "k_a": i["rwkv_k_a"], "r_k": i["rwkv_r_k"],
        "ln_w": i["rwkv_ln_w"], "ln_b": i["rwkv_ln_b"], "conv": i["gla_conv"], "a_b": i["gla_a_b"],
        "gla_norm": i["gla_norm"], "ple_b": i["ple_gate_b"], "c": i["c_2"], "ada_b": i["ada_b_2"],
        "gains2": i["norm_gains_2"], "conv2": i["conv_w_2"],
    }
    a["vec"] = np.concatenate([by_tile(fields[n]) for n, _ in VEC_FIELDS], axis=1)
    return a


def kernel(**inputs):
    import concourse.bacc as bacc
    from concourse.bass_utils import run_bass_kernel_spmd

    nc = bacc.Bacc("TRN2", target_bir_lowering=False, num_devices=1)
    arrays = {f"in_{n}": v for n, v in laid_out({n: np.asarray(v) for n, v in inputs.items()}).items()}
    aps = {n[3:]: nc.dram_tensor(n, v.shape, mybir.dt.from_np(v.dtype), kind="ExternalInput").ap()
           for n, v in arrays.items()}
    out = nc.dram_tensor("out", (P, KD, T), F32, kind="ExternalOutput").ap()
    build(nc, aps, out)
    r = run_bass_kernel_spmd(nc, [arrays], core_ids=[0])
    got = r.results[0]["out"]
    return np.ascontiguousarray(got.transpose(2, 1, 0)).reshape(1, T, D)
```

```python
from contextlib import ExitStack

import numpy as np

import concourse.bass as bass
from concourse import mybir

P = 128
T = 1024
D = 1024
KD = D // P
HALF = 512
FF = 2816
NF = FF // P
HEAD_PAIRS = 4
BLK = 128
NBLK = T // BLK
CH = 64
NZR = 15
NZG = 13
DECAY = float(np.exp(-0.5))
LEVELS = [1, 2, 4, 8, 16, 32, 64]

F32 = mybir.dt.float32
F32R = mybir.dt.float32r
ALU = mybir.AluOpType
ACT = mybir.ActivationFunctionType
ds = bass.ds

VEC_FIELDS = [
    ("norm_mix_pre", 8), ("norm_mix_post", 8), ("norm_ffn_pre", 8), ("norm_ffn_post", 8), ("norm_ple", 8),
    ("mu", NZR), ("w0", 8), ("a0", 4), ("k_k", 4), ("k_a", 4), ("r_k", 4), ("ln_w", 4), ("ln_b", 4),
    ("conv", 24), ("a_b", 4), ("gla_norm", 1), ("ple_b", 8), ("c", 8), ("ada_b", 48), ("gains2", 32),
    ("conv2", 24),
]
VEC = {}
_at = 0
for _name, _n in VEC_FIELDS:
    VEC[_name] = _at
    _at += _n
NVEC = _at

CONST_FIELDS = [("ident", 1), ("ones", 1), ("head_ones", 1), ("eye64", 1), ("eps", 1), ("head_rows", 1), ("spread", 4),
                ("chunk_keep", 16), ("score_mask", 4), ("level1_t", 2), ("level1_m", 2), ("level_m", 5),
                ("block_keep", 16), ("gla_diag", 1), ("gla_level", 7)]
CONST = {}
_at = 0
for _name, _n in CONST_FIELDS:
    CONST[_name] = _at
    _at += _n
NCONST = _at
N_STAY = CONST["chunk_keep"]
EPS_RMS, EPS_GN, EPS_ZERO = 0, 1, 2


def constants():
    out = np.zeros((P, NCONST, P), np.float32)
    p, j = np.arange(P)[:, None], np.arange(P)[None, :]
    out[:, CONST["ident"]] = p == j
    out[:, CONST["ones"]] = 1
    out[:, CONST["head_ones"]] = p // 64 == j // 64
    out[:, CONST["eye64"]] = p % 64 == j % 64
    out[:, CONST["eps"], EPS_RMS] = 1e-6
    out[:, CONST["eps"], EPS_GN] = 64e-5
    for n in range(HEAD_PAIRS):
        out[:, CONST["head_rows"], 32 * n:32 * n + 32] = np.arange(32)[None] == 2 * n + p // 64
        out[:, CONST["spread"] + n] = -1.0 * (p == 2 * n + j // 64)
    t = np.arange(T)
    out[:, CONST["chunk_keep"]:CONST["chunk_keep"] + 8] = (t % CH != 0).reshape(8, P)[None]
    out[:, CONST["chunk_keep"] + 8:CONST["chunk_keep"] + 16] = (t % CH != CH - 1).reshape(8, P)[None]
    out[:, CONST["block_keep"]:CONST["block_keep"] + 8] = (t % BLK != 0).reshape(8, P)[None]
    out[:, CONST["block_keep"] + 8:CONST["block_keep"] + 16] = (t % BLK != BLK - 1).reshape(8, P)[None]
    same = p // CH == j // CH
    for d in range(2):
        before = (p < j) if d == 0 else (p > j)
        out[:, CONST["score_mask"] + 2 * d] = same & before
        out[:, CONST["score_mask"] + 2 * d + 1] = same & (before | (p == j))
        out[:, CONST["level1_t"] + d] = (p // 2 == j // 2) & before
        for n, s in enumerate(LEVELS[1:6]):
            col = np.arange(P).reshape(P // (2 * s), 2, s)[:, d].reshape(-1)
            out[:, CONST["level_m"] + n, d * CH:(d + 1) * CH] = (p // (2 * s) == col // (2 * s)) & (p // s != col // s)
        out[:, CONST["level1_m"] + d] = (p // 2 == j // 2) & ((p > j) if d == 0 else (p < j))
    for n, s in enumerate(LEVELS):
        out[:, CONST["gla_level"] + n] = (p // (2 * s) == j // (2 * s)) & (p // s != j // s)
    out[:, CONST["gla_diag"]] = 2.0 * (p == j)
    return out.reshape(P, NCONST * P)


class Core:

    def __init__(self, nc, ctx):
        self.nc, self.ctx, self.sems = nc, ctx, []

    def sem(self, name):
        self.sems.append(self.nc.alloc_semaphore(name=name))
        return self.sems[-1]

    def clear_sems(self):
        self.nc.clear_and_free_semaphores(self.sems)
        self.nc.all_engine_barrier()
        self.sems = []


def cst(core, name, n=0):
    a = CONST[name]
    return core.const[:, (a + n) * P:(a + n + 1) * P] if isinstance(n, int) else core.const[:, ds((n + a) * P, P)]


def head_rows(core, n):
    return cst(core, "head_rows")[:, 32 * n:32 * n + 32]


def head_spread(core, n):
    return cst(core, "spread", n)[0:32]


class Marks:

    def __init__(self, sem, names):
        self.sem, self.names, self.next = sem, names, 0

    def begin(self, engine):
        engine.sem_inc(self.sem, 1)

    def before(self, turn):
        return self.sem, turn * len(self.names) + 1

    def __call__(self, name):
        assert self.names[self.next % len(self.names)] == name, (name, self.names[self.next % len(self.names)])
        self.next += 1
        return self.sem, 1

    def by(self, name, turn=0):
        return self.sem, turn * len(self.names) + (self.names.index(name) + 2)


def eps(core, which):
    a = CONST["eps"] * P + which
    return core.const[:, a:a + 1]


def vec(core, name, n=0):
    return core.vec[:, ds(VEC[name] + n, 1)] if not isinstance(n, int) else core.vec[:, VEC[name] + n:VEC[name] + n + 1]


def tile_of(buf, n):
    if isinstance(n, int):
        return buf[:, n, :]
    return buf[:, ds(n, 1), :].rearrange("p a t -> p (a t)")


def walk(e, segments, unroll, body):
    total = segments[-1][1]
    for a, b, kind in segments:
        m = a
        while m < min(b, unroll if a == 0 else a):
            body(m, m % 6, m // 3 if kind == "third" else kind)
            m += 1
        last = b - 1 if b == total else b
        turns = max(0, (last - m) // unroll)
        if turns > 1:
            with e.Fori(0, turns) as i:
                for u in range(unroll):
                    body(i * unroll + (m + u), (m + u) % 6 if unroll == 6 else (m + u) % 2,
                         i * 2 + (m + u) // 3 if kind == "third" else kind)
            m += turns * unroll
        while m < b:
            body(m, m % 6, m // 3 if kind == "third" else kind)
            m += 1


def dense(core, name, weights, act_hi, act_lo, segments, act_epilogue, dve_epilogue=None, pool_epilogue=None,
          unroll=2, act_first=None, dve_first=None, pool_first=None, load=None):
    nc = core.nc
    total = segments[-1][1]
    kt = weights.shape[2] // P
    with ExitStack() as ctx:
        raw = ctx.enter_context(nc.sbuf_tensor(f"{name}_raw", [P, 2, kt, P], F32))
        w_hi = ctx.enter_context(nc.sbuf_tensor(f"{name}_whi", [P, 2, kt, P], F32R))
        w_lo = ctx.enter_context(nc.sbuf_tensor(f"{name}_wlo", [P, 2, kt, P], F32R))
        acc = ctx.enter_context(nc.psum_tensor(f"{name}_acc", [P, 2, T], F32))
        loaded = [core.sem(f"{name}_loaded{s}") for s in range(2)]
        other_loaded = core.sem(f"{name}_other_loaded")
        hi_ready, lo_ready, filled, drained = (core.sem(f"{name}_{x}") for x in
                                               ("hi_ready", "lo_ready", "filled", "drained"))
        block = ctx.enter_context(nc.Block())

        @block.sync
        def _(sp):
            def load_weights(m, r, kind):
                if not (isinstance(m, int) and m < 2):
                    sp.wait_ge(lo_ready, m - 1)
                src = weights[m] if isinstance(m, int) else weights[ds(m, 1)].rearrange("a p k -> (a p) k")
                sp.dma_start(raw[:, r % 2].rearrange("p k c -> p (k c)"), src).then_inc(loaded[r % 2], 16)
            if load is not None:
                for r in range(2):
                    load_weights(r, r, None)
                sp.dma_start(*load).then_inc(other_loaded, 16)
                walk(sp, [(2, total, None)], 2, load_weights)
                sp.wait_ge(other_loaded, 16)
            else:
                walk(sp, [(0, total, None)], 2, load_weights)

        @block.scalar
        def _(act):
            if act_first:
                act_first(act)

            def split_hi(m, slot, first):
                act.wait_ge(loaded[slot], (m - slot) * 8 + 16)
                if not first:
                    act.wait_ge(filled, m - 1)
                act.copy(w_hi[:, slot], raw[:, slot]).then_inc(hi_ready, 1)

            def body(m, r, kind):
                if not (isinstance(m, int) and m + 1 >= total):
                    split_hi(m + 1, (r + 1) % 2, isinstance(m, int) and m == 0)
                act_epilogue(act, m, r, kind, acc[:, r % 2], filled, drained)
            split_hi(0, 0, True)
            walk(act, segments, unroll, body)

        @block.vector
        def _(dve):
            if dve_first:
                dve_first(dve)

            def split_lo(m, slot):
                dve.wait_ge(hi_ready, m + 1)
                dve.tensor_tensor(w_lo[:, slot], raw[:, slot], w_hi[:, slot].bitcast(F32),
                                  ALU.subtract).then_inc(lo_ready, 1)

            def body(m, r, kind):
                if not (isinstance(m, int) and m + 1 >= total):
                    split_lo(m + 1, (r + 1) % 2)
                if dve_epilogue:
                    dve_epilogue(dve, m, r, kind, drained)
            split_lo(0, 0)
            walk(dve, segments, unroll, body)

        @block.gpsimd
        def _(pool):
            if pool_first:
                pool_first(pool)
            if pool_epilogue:
                walk(pool, segments, unroll, lambda m, r, kind: pool_epilogue(pool, m, r, kind, drained))

        @block.tensor
        def _(pe):
            def body(m, r, kind):
                slot = r % 2
                pe.wait_ge(lo_ready, m + 1)
                if not (isinstance(m, int) and m < 2):
                    pe.wait_ge(drained, m - 1)
                for k in range(kt):
                    for w, x in ((w_hi, act_hi), (w_hi, act_lo), (w_lo, act_hi)):
                        for h in range(2):
                            mm = pe.matmul(acc[:, slot, h * HALF:(h + 1) * HALF], w[:, slot, k],
                                           x[:, k, h * HALF:(h + 1) * HALF],
                                           start=(k == 0 and w is w_hi and x is act_hi),
                                           stop=(k == kt - 1 and w is w_lo))
                mm.then_inc(filled, 1)
            walk(pe, segments, unroll, body)


def joint(core, name, y, y_gain, h, gain, shift, hi, lo, store=None, load=None):
    nc = core.nc
    groups = [("y", hf) for hf in range(2)] if y is not None else []
    groups += [("h", hf) for hf in range(2)] if hi is not None and gain is not None else []
    n_blocks, slots = HALF // P, 4
    with ExitStack() as ctx:
        sq = ctx.enter_context(nc.sbuf_tensor(f"{name}_sq", [P, slots, HALF], F32))
        tmp = ctx.enter_context(nc.sbuf_tensor(f"{name}_tmp", [P, slots, HALF], F32))
        root = ctx.enter_context(nc.sbuf_tensor(f"{name}_root", [P, len(groups), n_blocks], F32))
        sums = ctx.enter_context(nc.psum_tensor(f"{name}_sums", [P, len(groups), HALF], F32))
        rs = ctx.enter_context(nc.psum_tensor(f"{name}_rs", [P, len(groups), HALF], F32))
        sq_ready, sq_used, root_ready, recip, spread, scaled, normed, hi_done, stored = (
            core.sem(f"{name}_{x}") for x in ("sq_ready", "sq_used", "root_ready", "recip", "spread", "scaled",
                                              "normed", "hi_done", "stored"))
        loaded = core.sem(f"{name}_loaded")
        h_ready = [core.sem(f"{name}_h_even"), core.sem(f"{name}_h_odd")]
        lo_done = [core.sem(f"{name}_lo_even"), core.sem(f"{name}_lo_odd")]
        block = ctx.enter_context(nc.Block())
        pool_lo = shift is None

        def cols(hf):
            return slice(hf * HALF, (hf + 1) * HALF)

        def wait_h(e, hf, m):
            if y is not None:
                e.wait_ge(h_ready[m % 2], hf * (KD // 2) + m // 2 + 1)

        def normed_tile(hf, m):
            return tmp[:, m % slots] if gain is not None else h[:, m, cols(hf)]

        def low_part(e, hf, m):
            e.wait_ge(hi_done, hf * KD + m + 1)
            hi_m = hi[:, m, cols(hf)].bitcast(F32)
            if shift is None:
                ins = e.tensor_tensor(lo[:, m, cols(hf)], normed_tile(hf, m), hi_m, ALU.subtract)
            else:
                ins = e.scalar_tensor_tensor(lo[:, m, cols(hf)], normed_tile(hf, m), shift[:, m:m + 1], hi_m,
                                             ALU.add, ALU.subtract)
            ins.then_inc(lo_done[m % 2 if pool_lo else 0], 1)

        @block.scalar
        def _(act):
            count = 0
            for n, (stage, hf) in enumerate(groups):
                for m in range(KD):
                    if count >= slots:
                        act.wait_ge(sq_used, count - slots + 1)
                    if stage == "h":
                        wait_h(act, hf, m)
                    src = y if stage == "y" else h
                    act.activation(sq[:, count % slots], src[:, m, cols(hf)], ACT.Square).then_inc(sq_ready, 1)
                    count += 1
                act.wait_ge(sq_used, count)
                act.activation(root[:, n], sums[:, n, ::P], ACT.Sqrt, bias=eps(core, EPS_RMS), scale=1.0 / D
                               ).then_inc(root_ready, 1)
            if hi is not None:
                for hf in range(2):
                    for m in range(KD):
                        if gain is not None:
                            act.wait_ge(normed, hf * KD + m + 1)
                        else:
                            wait_h(act, hf, m)
                        act.activation(hi[:, m, cols(hf)], normed_tile(hf, m), ACT.Identity,
                                       bias=shift[:, m:m + 1] if shift is not None else 0.0).then_inc(hi_done, 1)

        @block.tensor
        def _(pe):
            count = 0
            for n in range(len(groups)):
                for m in range(KD):
                    pe.wait_ge(sq_ready, count + 1)
                    for b in range(n_blocks):
                        mm = pe.matmul(sums[:, n, b * P:(b + 1) * P], sq[:, count % slots, b * P:(b + 1) * P],
                                       cst(core, "ones"), start=(m == 0 and b == 0),
                                       stop=(m == KD - 1 and b == n_blocks - 1))
                    mm.then_inc(sq_used, 1)
                    count += 1
                pe.wait_ge(recip, n + 1)
                for b in range(n_blocks):
                    mm = pe.matmul(rs[:, n, b * P:(b + 1) * P], root[:, n, b:b + 1].to_broadcast([P, P]),
                                   cst(core, "ident"), start=True, stop=True)
                mm.then_inc(spread, 1)

        @block.vector
        def _(dve):
            def reciprocal(n):
                if n < len(groups):
                    dve.wait_ge(root_ready, n + 1)
                    dve.reciprocal(root[:, n], root[:, n]).then_inc(recip, 1)

            reciprocal(0)
            for n, (stage, hf) in enumerate(groups):
                dve.wait_ge(spread, n + 1)
                for m in range(KD):
                    if m == KD // 2:
                        reciprocal(n + 1)
                    if stage == "y":
                        dve.scalar_tensor_tensor(y[:, m, cols(hf)], y[:, m, cols(hf)], y_gain[:, m:m + 1], rs[:, n],
                                                 ALU.mult, ALU.mult).then_inc(scaled, 1)
                        if m % 2 == 0:
                            dve.wait_ge(scaled, hf * KD + m + 1)
                            dve.tensor_tensor(h[:, m, cols(hf)], h[:, m, cols(hf)], y[:, m, cols(hf)],
                                              ALU.add).then_inc(h_ready[0], 1)
                        continue
                    tile = hf * KD + m
                    if tile >= slots:
                        if pool_lo:
                            dve.wait_ge(lo_done[m % 2], (tile - slots) // 2 + 1)
                        else:
                            dve.wait_ge(lo_done[0], tile - slots + 1)
                    wait_h(dve, hf, m)
                    dve.scalar_tensor_tensor(tmp[:, m % slots], h[:, m, cols(hf)], gain[:, m:m + 1], rs[:, n],
                                             ALU.mult, ALU.mult).then_inc(normed, 1)
                    if m >= 1 and (m % 2 == 1 or not pool_lo):
                        low_part(dve, hf, m - 1)
                if stage == "h" and not pool_lo:
                    low_part(dve, hf, KD - 1)
            if hi is not None and gain is None:
                for hf in range(2):
                    for m in range(0, KD, 2):
                        low_part(dve, hf, m)

        @block.gpsimd
        def _(pool):
            if y is not None:
                for hf in range(2):
                    for m in range(1, KD, 2):
                        pool.wait_ge(scaled, hf * KD + m + 1)
                        pool.tensor_tensor(h[:, m, cols(hf)], h[:, m, cols(hf)], y[:, m, cols(hf)],
                                           ALU.add).then_inc(h_ready[1], 1)
            if hi is not None and pool_lo:
                for hf in range(2):
                    for m in range(1, KD, 2):
                        low_part(pool, hf, m)

        @block.sync
        def _(sp):
            if load is not None:
                sp.dma_start(*load).then_inc(loaded, 16)
                sp.wait_ge(loaded, 16)
            if store is not None:
                for hf in range(2):
                    for half_tiles in h_ready:
                        sp.wait_ge(half_tiles, (hf + 1) * KD // 2)
                    sp.dma_start(store[:, :, cols(hf)], h[:, :, cols(hf)]).then_inc(stored, 16)
                sp.wait_ge(stored, 32)


def gla_project(core, w, xn_hi, xn_lo, z, lora):
    nc = core.nc
    with ExitStack() as ctx:
        edge = ctx.enter_context(nc.sbuf_tensor("gp_edge", [P, 2, T + 2], F32))
        mix = ctx.enter_context(nc.sbuf_tensor("gp_mix", [P, T], F32))
        edged, raw_z, part, mixed, used = (core.sem(f"gp_{x}") for x in ("edged", "raw_z", "part", "mixed", "used"))
        segments = [(0, 8, "conv"), (8, 12, "gate"), (12, 13, "lora")]

        def dve_first(dve):
            dve.memset(edge[:, :, :], 0.0).then_inc(edged, 1)

        def act_first(act):
            act.wait_ge(edged, 1)

        def act_epilogue(act, m, r, kind, psum, filled, drained):
            act.wait_ge(filled, m + 1)
            if kind == "conv":
                act.copy(edge[:, r % 2, 1:T + 1], psum).then_inc(drained, 1)
                act.wait_ge(drained, m + 1)
                act.wait_ge(mixed, m + 1)
                act.activation(tile_of(z, m), mix[:, :], ACT.Silu).then_inc(used, 1)
            elif kind == "gate":
                act.activation(tile_of(z, m), psum, ACT.Silu).then_inc(drained, 1)
            else:
                act.copy(lora, psum).then_inc(drained, 1)

        def dve_epilogue(dve, m, r, kind, drained):
            if kind != "conv":
                return
            x = edge[:, r % 2]
            dve.wait_ge(drained, m + 1)
            if not (isinstance(m, int) and m == 0):
                dve.wait_ge(used, m)
            taps = [vec(core, "conv", t * 8 + m) for t in range(3)]
            dve.tensor_scalar(mix[:, :], x[:, 0:T], taps[0], None, ALU.mult).then_inc(part, 1)
            dve.wait_ge(part, m * 2 + 1)
            dve.scalar_tensor_tensor(mix[:, :], x[:, 1:T + 1], taps[1], mix[:, :], ALU.mult,
                                     ALU.add).then_inc(part, 1)
            dve.wait_ge(part, m * 2 + 2)
            dve.scalar_tensor_tensor(mix[:, :], x[:, 2:T + 2], taps[2], mix[:, :], ALU.mult,
                                     ALU.add).then_inc(mixed, 1)

        dense(core, "gp", w, xn_hi, xn_lo, segments, act_epilogue, dve_epilogue, act_first=act_first,
              dve_first=dve_first)


def gla_decay(core, dram_const, dram_a_up, lora, sums):
    nc = core.nc
    with ExitStack() as ctx:
        a_up = ctx.enter_context(nc.sbuf_tensor("gd_aup", [P, 2 * P], F32))
        keep = ctx.enter_context(nc.sbuf_tensor("gd_keep", [P, 2, T], F32))
        away = ctx.enter_context(nc.sbuf_tensor("gd_away", [P, T], F32))
        low = ctx.enter_context(nc.sbuf_tensor("gd_low", [P, 2, T], F32))
        gate = ctx.enter_context(nc.psum_tensor("gd_gate", [P, 4, T], F32))
        loaded, products, act_did, dve_did = (core.sem(f"gd_{x}") for x in ("loaded", "products", "act", "dve"))
        cases = [(d, i) for d in range(2) for i in range(2)]
        act_made = Marks(act_did, ["abs", "exp", "ln"])
        dve_made = Marks(dve_did, ["min", "log_sigmoid", "scan"])
        block = ctx.enter_context(nc.Block())

        @block.sync
        def _(sp):
            sp.dma_start(a_up[:, :], dram_a_up).then_inc(loaded, 16)
            c = CONST["block_keep"] * P
            sp.dma_start(keep[:, :, :].rearrange("p d t -> p (d t)"), dram_const[:, c:c + 2 * T]).then_inc(loaded, 16)

        @block.tensor
        def _(pe):
            pe.wait_ge(loaded, 32)
            for n, (d, i) in enumerate(cases):
                rows = slice(32 * d, 32 * d + 16)
                for h in range(2):
                    mm = pe.matmul(gate[:, n, h * HALF:(h + 1) * HALF], a_up[rows, i * P:(i + 1) * P],
                                   lora[rows, h * HALF:(h + 1) * HALF], start=True, stop=True)
                mm.then_inc(products, 1)

        @block.scalar
        def _(act):
            act_made.begin(act)
            for n, (d, i) in enumerate(cases):
                act.wait_ge(products, n + 1)
                if n:
                    act.wait_ge(*dve_made.by("log_sigmoid", n - 1))
                act.activation(away[:, :], gate[:, n], ACT.Abs, bias=vec(core, "a_b", n)).then_inc(*act_made("abs"))
                act.wait_ge(*act_made.by("abs", n))
                act.activation(away[:, :], away[:, :], ACT.Exp, scale=-1.0).then_inc(*act_made("exp"))
                act.wait_ge(*act_made.by("exp", n))
                act.activation(away[:, :], away[:, :], ACT.Ln, bias=1.0).then_inc(*act_made("ln"))

        @block.vector
        def _(dve):
            dve_made.begin(dve)
            dve.wait_ge(loaded, 32)
            for n, (d, i) in enumerate(cases):
                ls = low[:, n % 2]
                dve.wait_ge(*act_made.by("abs", n))
                dve.tensor_scalar(ls, gate[:, n], vec(core, "a_b", n), 0.0, ALU.add,
                                  ALU.min).then_inc(*dve_made("min"))
                dve.wait_ge(*dve_made.by("min", n))
                dve.wait_ge(*act_made.by("ln", n))
                dve.tensor_tensor(ls, ls, away[:, :], ALU.subtract).then_inc(*dve_made("log_sigmoid"))
                dve.wait_ge(*dve_made.by("log_sigmoid", n))
                out = sums[:, d, i]
                if d == 0:
                    dve.tensor_tensor_scan(out, keep[:, 0], ls, 0.0, ALU.mult, ALU.add).then_inc(*dve_made("scan"))
                else:
                    dve.tensor_tensor_scan(out[:, ::-1], keep[:, 1, ::-1], ls[:, ::-1], 0.0, ALU.mult,
                                           ALU.add).then_inc(*dve_made("scan"))


def gla_direction(core, dram_const, z, sums, y, d):
    nc = core.nc
    levels = range(7) if d == 0 else []
    scored = (["diag"] + [f"level{n}" for n in levels]) if d == 0 else []
    with ExitStack() as ctx:
        def sb(name, shape):
            return ctx.enter_context(nc.sbuf_tensor(f"g{d}_{name}", shape, F32))

        def psum(name, shape):
            return ctx.enter_context(nc.psum_tensor(f"g{d}_ps_{name}", shape, F32))
        mask = sb("mask", [P, 8, BLK])
        summed = sb("summed", [P, 2, 2, BLK])
        qk = sb("qk", [P, 2, 2, BLK])
        v = sb("v", [P, 4, BLK])
        diff_s = sb("diff_s", [P, 2, 2, BLK])
        grown_s = sb("grown_s", [P, 2, 2, BLK])
        qk_s = sb("qk_s", [P, 2, 2, BLK])
        diff = sb("diff", [P, 2, 2, 2, BLK])
        grown = sb("grown", [P, 2, 2, 2, BLK])
        qk_l = sb("qk_l", [P, 2, 2, 2, BLK])
        v_tok = sb("v_tok", [P, 4, BLK])
        k_tok = sb("k_tok", [P, 2, BLK])
        part = sb("part", [P, 2, 4, BLK])
        score = sb("score", [P, 4, BLK])
        state = sb("state", [P, 2, BLK])
        ps_score = psum("score", [P, 2, 2, 512])
        ps_v = psum("v", [P, 4, BLK])
        ps_k = psum("k", [P, 4, BLK])
        ps_o = psum("o", [P, 2, 512])
        loaded, zeroed = core.sem(f"g{d}_loaded"), core.sem(f"g{d}_zeroed")
        dve_steps = ["summed", "q", "diff_s", "qk_s"]
        if d == 0:
            dve_steps += ["diff_level0"]
            for n in levels:
                dve_steps += ([f"diff_level{n + 1}"] if n < 6 else []) + [f"qk_level{n}", f"part_{scored[n]}"]
            dve_steps += ["part_level6"]
        dve_steps += ["state0", "state1"] + (["y0", "y1"] if d else [])
        act_steps = ["k", "v", "exp_s", "v_tok", "k_tok"] + [f"exp_level{n}" for n in levels] + (
            ["y0", "y1"] if d == 0 else [])
        dve_made = Marks(core.sem(f"g{d}_dve"), dve_steps)
        act_made = Marks(core.sem(f"g{d}_act"), act_steps)
        pool_made = Marks(core.sem(f"g{d}_pool"), [f"sum_{r}" for r in scored[1:]] or ["none"])
        pe_made = Marks(core.sem(f"g{d}_pe"), ["v_tok", "k_tok"] + [f"score_{r}" for r in scored] + ["out", "gain"])
        block = ctx.enter_context(nc.Block())

        def tokens(j):
            return ds(j * BLK if d == 0 else (NBLK - 1) * BLK - j * BLK, BLK)

        @block.sync
        def _(sp):
            c = CONST["gla_diag"] * P
            sp.dma_start(mask[:, :, :].rearrange("p a t -> p (a t)"), dram_const[:, c:c + 8 * P]).then_inc(loaded, 16)

        @block.scalar
        def _(act):
            act_made.begin(act)
            with act.Fori(0, NBLK) as j:
                act.wait_ge(*pe_made.before(j))
                act.wait_ge(*dve_made.before(j))
                act.copy(qk[:, 1], z[:, 2:4, tokens(j)]).then_inc(*act_made("k"))
                act.copy(v[:, :, :], z[:, 4:8, tokens(j)]).then_inc(*act_made("v"))
                act.wait_ge(*dve_made.by("diff_s", j))
                act.activation(grown_s[:, :, :, :], diff_s[:, :, :, :], ACT.Exp,
                               scale=1 / 16).then_inc(*act_made("exp_s"))
                act.wait_ge(*pe_made.by("v_tok", j))
                act.copy(v_tok[:, :, :], ps_v[:, :, :]).then_inc(*act_made("v_tok"))
                act.wait_ge(*pe_made.by("k_tok", j))
                act.copy(k_tok[:, :, :], ps_k[:, 0:2]).then_inc(*act_made("k_tok"))
                for n in levels:
                    act.wait_ge(*dve_made.by(f"diff_level{n}", j))
                    if n >= 2:
                        act.wait_ge(*dve_made.by(f"qk_level{n - 2}", j))
                    act.activation(grown[:, n % 2], diff[:, n % 2], ACT.Exp,
                                   scale=1 / 16).then_inc(*act_made(f"exp_level{n}"))
                if d == 0:
                    act.wait_ge(*pe_made.by("out", j))
                    for par in range(2):
                        act.copy(y[:, par:par + 3:2, tokens(j)],
                                 ps_o[:, par, 0:2 * BLK].rearrange("p (i t) -> p i t", i=2)
                                 ).then_inc(*act_made(f"y{par}"))

        @block.gpsimd
        def _(pool):
            if d == 0:
                pool_made.begin(pool)
                with pool.Fori(0, NBLK) as j:
                    for n, r in enumerate(scored[1:], 1):
                        pool.wait_ge(*dve_made.by(f"part_{r}", j))
                        if n == 1:
                            pool.wait_ge(*pe_made.before(j))
                            pool.tensor_tensor(score[:, :, :], part[:, 0], part[:, 1],
                                               ALU.add).then_inc(*pool_made(f"sum_{r}"))
                        else:
                            pool.wait_ge(*pool_made.by(f"sum_{scored[n - 1]}", j))
                            pool.tensor_tensor(score[:, :, :], score[:, :, :], part[:, n % 2],
                                               ALU.add).then_inc(*pool_made(f"sum_{r}"))

        @block.tensor
        def _(pe):
            pe_made.begin(pe)
            pe.wait_ge(zeroed, 1)
            with pe.Fori(0, NBLK) as j:
                pe.wait_ge(*act_made.by("v", j))
                for i in range(4):
                    mm = pe.transpose(ps_v[:, i], v[:, i], cst(core, "ident"))
                mm.then_inc(*pe_made("v_tok"))
                pe.wait_ge(*dve_made.by("qk_s", j))
                for i in range(2):
                    mm = pe.transpose(ps_k[:, i], qk_s[:, 1, i], cst(core, "ident"))
                mm.then_inc(*pe_made("k_tok"))
                for n, r in enumerate(scored):
                    if r == "diag":
                        pe.wait_ge(*act_made.by("k", j))
                        src = qk
                    else:
                        pe.wait_ge(*dve_made.by(f"qk_{r}", j))
                        src = qk_l[:, (n - 1) % 2]
                    if n >= 2:
                        pe.wait_ge(*dve_made.by(f"part_{scored[n - 2]}", j))
                    for par in range(2):
                        rows = slice(64 * par, 64 * par + 64)
                        for i in range(2):
                            mm = pe.matmul(ps_score[:, n % 2, par, i * BLK:(i + 1) * BLK], src[rows, 1, i],
                                           src[rows, 0, i], start=True, stop=True)
                    mm.then_inc(*pe_made(f"score_{r}"))
                pe.wait_ge(*act_made.by("k_tok", j))
                pe.wait_ge(*dve_made.before(j))
                if d == 0:
                    pe.wait_ge(*act_made.before(j))
                    pe.wait_ge(*pool_made.by(f"sum_{scored[-1]}", j))
                for par in range(2):
                    rows = slice(64 * par, 64 * par + 64)
                    for i in range(2):
                        out = ps_o[:, par, i * BLK:(i + 1) * BLK]
                        if d == 0:
                            pe.matmul(out, v_tok[:, 2 * i + par], score[:, 2 * par + i], start=True, stop=False)
                        mm = pe.matmul(out, state[rows, i], qk_s[rows, 0, i], start=(d == 1), stop=True)
                mm.then_inc(*pe_made("out"))
                for par in range(2):
                    for i in range(2):
                        mm = pe.matmul(ps_k[64 * par:64 * par + 64, 2 + i], k_tok[:, i, 64 * par:64 * par + 64],
                                       v_tok[:, 2 * i + par], start=True, stop=True)
                mm.then_inc(*pe_made("gain"))

        @block.vector
        def _(dve):
            dve_made.begin(dve)
            dve.memset(state[:, :, :], 0.0).then_inc(zeroed, 1)
            dve.wait_ge(zeroed, 1)
            dve.wait_ge(loaded, 16)

            def halves(x, s):
                return x.rearrange("p i (n o r) -> p (i n) o r", o=2, r=s)

            def level_diff(j, n):
                s = LEVELS[n]
                fwd, bwd = halves(summed[:, 0], s), halves(summed[:, 1], s)
                q_out, k_out = halves(diff[:, n % 2, 0], s), halves(diff[:, n % 2, 1], s)
                pairs = 2 * BLK // (2 * s)
                end = fwd[:, :, 0, s - 1:s].to_broadcast([P, pairs, s])
                start = bwd[:, :, 1, 0:1].to_broadcast([P, pairs, s])
                if n >= 2:
                    dve.wait_ge(*act_made.by(f"exp_level{n - 2}", j))
                dve.tensor_tensor(q_out[:, :, 0, :], bwd[:, :, 0, :], start, ALU.subtract)
                dve.tensor_tensor(q_out[:, :, 1, :], fwd[:, :, 1, :], end, ALU.subtract)
                dve.tensor_tensor(k_out[:, :, 0, :], end, fwd[:, :, 0, :], ALU.subtract)
                dve.tensor_tensor(k_out[:, :, 1, :], start, bwd[:, :, 1, :],
                                  ALU.subtract).then_inc(*dve_made(f"diff_level{n}"))

            def masked(j, n):
                r = scored[n]
                dve.wait_ge(*pe_made.by(f"score_{r}", j))
                if n >= 2:
                    dve.wait_ge(*pool_made.by(f"sum_{scored[max(n - 2, 1)]}", j))
                out = part[:, n % 2].rearrange("p (a i) t -> p a (i t)", a=2)
                dve.tensor_tensor(out.rearrange("p a (i t) -> p a i t", i=2),
                                  ps_score[:, n % 2, :, 0:2 * BLK].rearrange("p a (i t) -> p a i t", i=2),
                                  mask[:, n, :].rearrange("p (a i t) -> p a i t", a=1, i=1).to_broadcast([P, 2, 2, BLK]),
                                  ALU.mult).then_inc(*dve_made(f"part_{r}"))

            with dve.Fori(0, NBLK) as j:
                dve.tensor_copy(summed[:, :, :, :], sums[:, :, :, tokens(j)]).then_inc(*dve_made("summed"))
                dve.wait_ge(*pe_made.before(j))
                dve.tensor_scalar(qk[:, 0], z[:, 0:2, tokens(j)], 0.125, None, ALU.mult).then_inc(*dve_made("q"))
                dve.wait_ge(*dve_made.by("summed", j))
                last = BLK - 1 if d == 0 else 0
                dve.tensor_copy(diff_s[:, 0], summed[:, d])
                dve.tensor_tensor(diff_s[:, 1], summed[:, d, :, last:last + 1].to_broadcast([P, 2, BLK]), summed[:, d],
                                  ALU.subtract).then_inc(*dve_made("diff_s"))
                dve.wait_ge(*act_made.by("exp_s", j))
                dve.wait_ge(*dve_made.by("q", j))
                dve.tensor_tensor(qk_s[:, :, :, :], qk[:, :, :, :], grown_s[:, :, :, :],
                                  ALU.mult).then_inc(*dve_made("qk_s"))
                if d == 0:
                    level_diff(j, 0)
                for n in levels:
                    if n < 6:
                        level_diff(j, n + 1)
                    dve.wait_ge(*act_made.by(f"exp_level{n}", j))
                    if n >= 2:
                        dve.wait_ge(*pe_made.by(f"score_level{n - 2}", j))
                    dve.tensor_tensor(qk_l[:, n % 2], qk[:, :, :, :], grown[:, n % 2],
                                      ALU.mult).then_inc(*dve_made(f"qk_level{n}"))
                    masked(j, n)
                if d == 0:
                    masked(j, 7)
                dve.wait_ge(*pe_made.by("gain", j))
                for i in range(2):
                    dve.scalar_tensor_tensor(state[:, i], state[:, i], grown_s[:, 0, i, last:last + 1], ps_k[:, 2 + i],
                                             ALU.mult, ALU.add).then_inc(*dve_made(f"state{i}"))
                if d == 1:
                    for par in range(2):
                        out = y[:, par:par + 3:2, tokens(j)]
                        dve.tensor_tensor(out, out, ps_o[:, par, 0:2 * BLK].rearrange("p (i t) -> p i t", i=2),
                                          ALU.add).then_inc(*dve_made(f"y{par}"))


def gla_finish(core, z, y):
    nc = core.nc
    n_blocks = T // P
    with ExitStack() as ctx:
        sq = ctx.enter_context(nc.sbuf_tensor("gf_sq", [P, 2, T], F32))
        root = ctx.enter_context(nc.sbuf_tensor("gf_root", [P, 4, n_blocks], F32))
        sums = ctx.enter_context(nc.psum_tensor("gf_sums", [P, 2, T], F32))
        rs = ctx.enter_context(nc.psum_tensor("gf_rs", [P, 2, T], F32))
        squared, summed, rooted, recip, spread, scaled, gated = (
            core.sem(f"gf_{x}") for x in ("squared", "summed", "rooted", "recip", "spread", "scaled", "gated"))
        block = ctx.enter_context(nc.Block())

        @block.scalar
        def _(act):
            def make_root(m):
                act.wait_ge(summed, m + 1)
                act.activation(root[:, m], sums[:, m % 2, ::P], ACT.Sqrt, bias=eps(core, EPS_RMS),
                               scale=1.0 / P).then_inc(rooted, 1)
            for m in range(4):
                if m >= 2:
                    act.wait_ge(summed, m - 1)
                act.activation(sq[:, m % 2], y[:, m], ACT.Square).then_inc(squared, 1)
                if m >= 1:
                    make_root(m - 1)
            make_root(3)

        @block.tensor
        def _(pe):
            def spread_root(m):
                pe.wait_ge(recip, m + 1)
                if m >= 2:
                    pe.wait_ge(scaled, m - 1)
                for b in range(n_blocks):
                    mm = pe.matmul(rs[:, m % 2, b * P:(b + 1) * P], root[:, m, b:b + 1].to_broadcast([P, P]),
                                   cst(core, "ident"), start=True, stop=True)
                mm.then_inc(spread, 1)
            for m in range(4):
                pe.wait_ge(squared, m + 1)
                if m >= 2:
                    pe.wait_ge(rooted, m - 1)
                for b in range(n_blocks):
                    mm = pe.matmul(sums[:, m % 2, b * P:(b + 1) * P], sq[:, m % 2, b * P:(b + 1) * P],
                                   cst(core, "ones"), start=True, stop=True)
                mm.then_inc(summed, 1)
                if m >= 1:
                    spread_root(m - 1)
            spread_root(3)

        @block.vector
        def _(dve):
            def reciprocal(m):
                dve.wait_ge(rooted, m + 1)
                dve.reciprocal(root[:, m], root[:, m]).then_inc(recip, 1)
            reciprocal(0)
            for m in range(4):
                if m < 3:
                    reciprocal(m + 1)
                dve.wait_ge(spread, m + 1)
                dve.scalar_tensor_tensor(y[:, m], y[:, m], vec(core, "gla_norm"), rs[:, m % 2], ALU.mult,
                                         ALU.mult).then_inc(scaled, 1)
                dve.wait_ge(scaled, m + 1)
                dve.tensor_tensor(y[:, m], y[:, m], z[:, 8 + m], ALU.mult).then_inc(gated, 1)


def rwkv_project(core, w, xn_hi, xn_lo, z):
    nc = core.nc
    with ExitStack() as ctx:
        edge = ctx.enter_context(nc.sbuf_tensor("rp_edge", [P, 2, T + 2], F32))
        around = ctx.enter_context(nc.sbuf_tensor("rp_around", [P, 2, T], F32))
        share = ctx.enter_context(nc.sbuf_tensor("rp_share", [P, 2, NZR], F32))
        edged, around_ready, kept, mixed = (core.sem(f"rp_{x}") for x in ("edged", "around_ready", "kept", "mixed"))

        def dve_first(dve):
            mu = core.vec[:, VEC["mu"]:VEC["mu"] + NZR]
            dve.tensor_scalar(share[:, 0], mu, -1.0, 1.0, ALU.mult, ALU.add).then_inc(edged, 1)
            dve.tensor_scalar(share[:, 1], mu, 0.5, None, ALU.mult).then_inc(edged, 1)
            dve.memset(edge[:, :, :], 0.0).then_inc(edged, 1)
            dve.wait_ge(edged, 3)

        def column(n, m):
            return share[:, n, m:m + 1] if isinstance(m, int) else share[:, n, ds(m, 1)]

        def act_epilogue(act, m, r, kind, psum, filled, drained):
            act.wait_ge(filled, m + 1)
            if not (isinstance(m, int) and m < 2):
                act.wait_ge(mixed, m - 1)
            act.copy(edge[:, r % 2, 1:T + 1], psum).then_inc(drained, 1)

        def pool_epilogue(pool, m, r, kind, drained):
            pool.wait_ge(drained, m + 1)
            x = edge[:, r % 2]
            pool.tensor_tensor(around[:, r % 2], x[:, 0:T], x[:, 2:T + 2], ALU.add).then_inc(around_ready, 1)

        def dve_epilogue(dve, m, r, kind, drained):
            dve.wait_ge(drained, m + 1)
            out = tile_of(z, m)
            dve.tensor_scalar(out, edge[:, r % 2, 1:T + 1], column(0, m), None, ALU.mult).then_inc(kept, 1)
            dve.wait_ge(kept, m + 1)
            dve.wait_ge(around_ready, m + 1)
            dve.scalar_tensor_tensor(out, around[:, r % 2], column(1, m), out, ALU.mult, ALU.add).then_inc(mixed, 1)

        dense(core, "rp", w, xn_hi, xn_lo, [(0, NZR, None)], act_epilogue, dve_epilogue, pool_epilogue,
              act_first=lambda act: act.wait_ge(edged, 3), dve_first=dve_first)


def rwkv_mix(core, dram_const, dram_lora, dram_ada, z, gains):
    nc = core.nc
    levels = range(1, 6)
    with ExitStack() as ctx:
        def sb(name, shape):
            return ctx.enter_context(nc.sbuf_tensor(f"rw_{name}", shape, F32))
        n_masks = 16 + 4 + 4 + 5
        masks = sb("masks", [P, n_masks, P])
        keep = masks[:, 0:16].rearrange("p (d a) t -> p d (a t)", d=2)
        score_mask = masks[:, 16:20]
        level1_t, level1_m = masks[:, 20:22], masks[:, 22:24]
        level_mask = masks[:, 24:29].rearrange("p n (d c) -> p n d c", d=2)
        ident = cst(core, "ident")
        eye = ident.rearrange("p (a t) -> p a t", a=1).to_broadcast([P, 2, P])
        lora = sb("lora", [P, 2, P])
        spread_i = sb("spread_i", [32, P])
        kk_scale = z[0:32, 15]
        ka_rest = sb("ka_rest", [P, 4])
        sig = sb("sig", [P, 2, T])
        cum = sb("cum", [P, 2, T])
        kk = sb("kk", [P, T])
        b = sb("b", [P, T])
        y2 = sb("y2", [P, 2, T])
        rate, tmp = y2[:, 0], y2[:, 1]
        e_alpha = sb("e_alpha", [P, 2, BLK])
        e_rho = sb("e_rho", [P, 2, BLK])
        e_beta = sb("e_beta", [P, 2, BLK])
        v_b = sb("v_b", [P, 2, BLK])
        ar = sb("ar", [P, 2, 2, BLK])
        bk = sb("bk", [P, 2, 2, BLK])
        rho = sb("rho", [P, 2, 2, BLK])
        decay = sb("decay", [P, 2, 2, 2])
        beta_tok = sb("beta_tok", [P, 2, 2, BLK])
        kv_tok = sb("kv_tok", [P, 2, 4, BLK])
        an = sb("an", [P, 2, 2, 2, BLK])
        mp = sb("mp", [P, 2, 2, 2, 2, BLK])
        nq = sb("nq", [P, 2, 2, 2, 2, BLK])
        x = sb("x", [P, 2, 2, 2, BLK])
        xt = sb("xt", [P, 2, 2, 2, BLK])
        mx = sb("mx", [P, 5, 2, 2, BLK])
        wu = sb("wu", [P, 2, 2, BLK])
        rho2 = sb("rho2", [P, 2, BLK])
        carry = sb("carry", [P, 2, 2, CH])
        gain = sb("gain", [P, 2, 2, CH])
        state = sb("state", [P, 2, 2, CH])
        ada_ring = 3
        ada = sb("ada", [P, ada_ring, KD, P])
        c = sb("c", [P, KD])
        mod = sb("mod", [P, 6 * KD])
        ps = ctx.enter_context(nc.psum_tensor("rw_ps", [P, 8, 512], F32))
        loaded, setup, rest_ready = core.sem("rw_loaded"), core.sem("rw_setup"), core.sem("rw_rest_ready")
        lora_loaded, cleared, c_ready = core.sem("rw_lora_loaded"), core.sem("rw_cleared"), core.sem("rw_c_ready")
        ada_loaded = [core.sem(f"rw_ada_loaded{s}") for s in range(ada_ring)]
        ada_used, mod_ready = core.sem("rw_ada_used"), core.sem("rw_mod_ready")
        ada_summed = core.sem("rw_ada_summed")
        kk_squared, kk_summed, kk_scaled = (core.sem(f"rw_kk_{s}") for s in ("squared", "summed", "scaled"))
        k_ready, mod_copied = core.sem("rw_k_ready"), core.sem("rw_mod_copied")

        def bank(h, n):
            return ps[:, 4 * h + n]

        def pairs(a):
            return a.rearrange("p (d t) -> p d t", d=2)

        def joined(a, n, transposed=False):
            s = 2 ** n
            first, to_next = (s, P - s) if transposed else (0, P + s)
            return bass.AP(tensor=a.tensor, offset=a.offset + first, ap=[a.ap[0], [to_next, 2], [2 * s, P // (2 * s)], [1, s]])

        def joined_one(a, n, d, transposed=False):
            half = (1 - d) if transposed else d
            return a.rearrange("p (b two s) -> p b two s", two=2, s=2 ** n)[:, :, half]

        def halves(a, n):
            return a.rearrange("p (d b s) -> p d b s", d=2, s=2 ** n)

        heads = range(2)
        exp_made = Marks(core.sem("rw_exp"), ["e_rho", "e_beta", "v", "e_alpha"])
        ex_made = Marks(core.sem("rw_ex"), ["ex"])
        factor_made = Marks(core.sem("rw_factor"), ["ar_bk"])
        pe_front = Marks(core.sem("rw_pe_front"), ["tokens_a", "tokens_b"] +
                         [f"{s}{h}" for s in ("beta", "kappa", "nv", "m") for h in heads])
        act_front = Marks(core.sem("rw_act_front"), ["rho", "decay", "alpha_tok", "beta_tok", "kv_tok", "nv0", "nv1"])
        dve_front = Marks(core.sem("rw_dve_front"), ["mp0", "mp1", "nq0", "nq1", "xt0m", "xt1m", "xt0", "xt1",
                                                         "x0m", "x1m", "x0", "x1"])
        pe_steps, dve_steps = [], []
        for n in levels:
            pe_steps += [f"mx{n}_{h}" for h in heads]
            dve_steps += [f"mx{n}_{h}" for h in heads]
            both = [f"{s}{n}_{h}" for h in heads for s in (("x", "xt") if n < 5 else ("xt",))]
            pe_steps += both
            dve_steps += both
        pe_steps += [f"{s}{h}" for s in ("wu", "pw") for h in heads] + [f"chunk{c}_{h}" for h in heads for c in range(2)]
        pe_steps += ["state0_0", "state0_1"] + [f"{s}{h}" for h in heads for s in ("from_state", "state1_", "y")]
        act_steps = ["wu0", "wu1"] + [f"y{h}_{d}" for h in heads for d in range(2)]
        dve_steps += ["rho2_0", "rho2_1"] + [f"chunk{c}_{h}" for h in heads for c in range(2)] + \
            [f"state{m}_{h}" for m in range(2) for h in heads]
        pe_made, act_made, dve_made = (
            Marks(core.sem(f"rw_{n}"), s) for n, s in (("pe", pe_steps), ("act", act_steps), ("dve", dve_steps)))
        pe_pair = Marks(core.sem("rw_pe_pair"), ["kk_scale", "lora0", "lora1", "lora2"])
        act_pair = Marks(core.sem("rw_act_pair"), ["sig0", "sig1", "rate", "k_scale"])
        dve_pair = Marks(core.sem("rw_dve_pair"), ["spread", "kk", "cum0", "cum1", "b", "zero", "rk", "y"])
        block = ctx.enter_context(nc.Block())

        def tokens(d, j):
            return ds(j * BLK if d == 0 else (NBLK - 1) * BLK - j * BLK, BLK) if not isinstance(j, int) else \
                slice(j * BLK if d == 0 else (NBLK - 1 - j) * BLK, (j if d == 0 else NBLK - 1 - j) * BLK + BLK)

        def turns(e, i, turn):
            with e.Fori(0, NBLK // 2 - 1) as u:
                for par in range(2):
                    turn(u * 2 + par, i * NBLK + u * 2 + par, par, 2, i * (NBLK // 2) + u)
            for j in (NBLK - 2, NBLK - 1):
                turn(j, i * NBLK + j, j % 2, NBLK - 1 - j, i * (NBLK // 2) + j // 2)

        @block.sync
        def _(sp):
            at = CONST["chunk_keep"] * P
            sp.dma_start(masks[:, :, :].rearrange("p a t -> p (a t)"),
                         dram_const[:, at:at + n_masks * P]).then_inc(loaded, 16)
            for s in range(ada_ring):
                sp.dma_start(ada[:, s].rearrange("p k c -> p (k c)"), dram_ada[s]).then_inc(ada_loaded[s], 16)
            with sp.Fori(0, 6 * KD // ada_ring - 1) as q:
                for s in range(ada_ring):
                    sp.wait_ge(ada_used, q * ada_ring + s + 1)
                    sp.dma_start(ada[:, s].rearrange("p k c -> p (k c)"),
                                 dram_ada[ds(q * ada_ring + ada_ring + s, 1)].rearrange("a p k -> (a p) k")
                                 ).then_inc(ada_loaded[s], 16)

        @block.scalar
        def _(act):
            for made in (exp_made, act_front, act_made, act_pair):
                made.begin(act)
            act.activation(c[:, :], core.vec[:, VEC["c"]:VEC["c"] + KD], ACT.Silu).then_inc(c_ready, 1)
            act.activation(z[:, 12], z[:, 12], ACT.Tanh).then_inc(setup, 1)
            for n in range(HEAD_PAIRS):
                if n >= 2:
                    act.wait_ge(kk_summed, n - 1)
                act.activation(y2[:, n % 2], z[:, 4 + n], ACT.Square, scale=vec(core, "k_k", n)).then_inc(kk_squared, 1)
            act.wait_ge(kk_scaled, 1)
            act.activation(kk_scale, kk_scale, ACT.Sqrt).then_inc(setup, 1)
            act.wait_ge(rest_ready, 1)

            def front(t, par, last_used):
                act.wait_ge(*factor_made.by("ar_bk", t))
                act.copy(rho[:, par], ar[:, :, 1]).then_inc(*act_front("rho"))
                act.wait_ge(*last_used)
                act.copy(decay[:, par, 0], e_rho[:, 0, CH - 1::CH])
                act.copy(decay[:, par, 1], e_rho[:, 1, 0::CH]).then_inc(*act_front("decay"))
                act.wait_ge(*pe_front.by("tokens_a", t))
                act.copy(an[:, par, :, :, 0:CH].rearrange("p h d c -> p d h c"),
                         bank(0, 0)[:, 0:2 * P].rearrange("p (d h c) -> p d h c", d=2, h=2)
                         ).then_inc(*act_front("alpha_tok"))
                act.copy(beta_tok[:, par], pairs(bank(0, 0)[:, 2 * P:])).then_inc(*act_front("beta_tok"))
                act.wait_ge(*pe_front.by("tokens_b", t))
                act.copy(kv_tok[:, par].rearrange("p a t -> p (a t)"), bank(1, 0)).then_inc(*act_front("kv_tok"))

            def exps(i, j, t, decay_copied):
                act.wait_ge(*decay_copied)
                for d in range(2):
                    ins = act.activation(e_rho[:, d], cum[:, d, tokens(d, j)], ACT.Exp, scale=-DECAY)
                ins.then_inc(*exp_made("e_rho"))
                for d in range(2):
                    ins = act.activation(e_beta[:, d], cum[:, d, tokens(d, j)], ACT.Exp, scale=DECAY)
                ins.then_inc(*exp_made("e_beta"))
                for d in range(2):
                    ins = act.copy(v_b[:, d], tile_of(z, i + 8)[:, tokens(d, j)])
                ins.then_inc(*exp_made("v"))
                act.wait_ge(*ex_made.by("ex", t))
                act.activation(e_alpha[:, :, :], e_alpha[:, :, :], ACT.Exp, scale=-DECAY).then_inc(*exp_made("e_alpha"))

            def front_end(t, par):
                for h in heads:
                    act.wait_ge(*pe_front.by(f"nv{h}", t))
                    act.copy(an[:, par, h, :, CH:], pairs(bank(h, 0)[:, 0:2 * CH])).then_inc(*act_front(f"nv{h}"))

            with act.Fori(0, HEAD_PAIRS) as i:
                act.wait_ge(*dve_pair.before(i))
                for d in range(2):
                    act.wait_ge(*pe_pair.by(f"lora{d}", i))
                    act.activation(sig[:, d], ps[:, 2 * d:2 * d + 2].rearrange("p a t -> p (a t)"), ACT.Sigmoid,
                                   bias=vec(core, "w0", i + 4 * d)).then_inc(*act_pair(f"sig{d}"))
                act.wait_ge(*pe_pair.by("lora2", i))
                act.activation(rate, ps[:, 4:6].rearrange("p a t -> p (a t)"), ACT.Sigmoid,
                               bias=vec(core, "a0", i)).then_inc(*act_pair("rate"))
                act.wait_ge(*act_pair.by("rate", i))
                act.activation(tmp, rate, ACT.Identity, bias=ka_rest[:, ds(i, 1)], scale=vec(core, "k_a", i)
                               ).then_inc(*act_pair("k_scale"))
                act.wait_ge(*dve_pair.by("zero", i))
                exps(i, 0, i * NBLK, act_front.before(i * NBLK))
                front(i * NBLK, 0, dve_made.before(i * NBLK))
                front_end(i * NBLK, 0)
                exps(i, 1, i * NBLK + 1, act_front.by("decay", i * NBLK))

                def turn(j, t, par, ahead, two):
                    if ahead:
                        front(t + 1, 1 - par, dve_made.before(t))
                        if ahead > 1:
                            exps(i, j + 2, t + 2, act_front.by("decay", t + 1))
                        front_end(t + 1, 1 - par)
                    for h in heads:
                        act.wait_ge(*pe_made.by(f"wu{h}", t))
                        act.copy(wu[:, h], pairs(bank(h, 1)[:, 0:2 * P])).then_inc(*act_made(f"wu{h}"))
                    for h in heads:
                        rows = slice(64 * h, 64 * h + 64)
                        act.wait_ge(*pe_made.by(f"y{h}", t))
                        for d in range(2):
                            act.copy(y2[rows, d, tokens(d, j)],
                                     bank(h, 0)[rows, d * P:(d + 1) * P]).then_inc(*act_made(f"y{h}_{d}"))
                turns(act, i, turn)

        @block.gpsimd
        def _(pool):
            factor_made.begin(pool)
            pool.memset(mx[:, :, :, :, :].rearrange("p n h d t -> p (n h d t)"), 0.0).then_inc(cleared, 1)
            pool.wait_ge(loaded, 16)
            pool.wait_ge(c_ready, 1)
            with pool.Fori(0, HEAD_PAIRS) as i:
                pool.wait_ge(*pe_pair.before(i))
                pool.dma_start(lora[:, :, :], dram_lora[:, 0:2, ds(i * P, P)]).then_inc(lora_loaded, 16)
                r_i, k_i = tile_of(z, i + 0), tile_of(z, i + 4)
                pool.wait_ge(*act_pair.by("k_scale", i))
                pool.wait_ge(*dve_pair.by("kk", i))
                pool.tensor_tensor(k_i, k_i, tmp, ALU.mult).then_inc(k_ready, 1)
                with pool.Fori(0, NBLK // 2) as u:
                    for par in range(2):
                        j, t = u * 2 + par, i * NBLK + u * 2 + par
                        if par == 0:
                            pool.wait_ge(*dve_pair.by("zero", i))
                            pool.wait_ge(k_ready, i + 1)

                        pool.wait_ge(*exp_made.by("e_beta", t))
                        pool.wait_ge(*pe_front.before(t))
                        pool.wait_ge(*act_front.before(t))
                        for d in range(2):
                            at = tokens(d, j)
                            pool.tensor_tensor(ar[:, d, 1], r_i[:, at], e_rho[:, d], ALU.mult)
                            pool.tensor_tensor(bk[:, 0, d], b[:, at], e_beta[:, d], ALU.mult)
                            pool.tensor_tensor(bk[:, 1, d], k_i[:, at], e_beta[:, d], ALU.mult)
                        pool.wait_ge(*exp_made.by("e_alpha", t))
                        for d in range(2):
                            ins = pool.tensor_tensor(ar[:, d, 0], kk[:, tokens(d, j)], e_alpha[:, d], ALU.mult)
                        ins.then_inc(*factor_made("ar_bk"))

                        two = i * (NBLK // 2) + u
                        for s in ((0, 1), (2,))[par]:
                            done = (two * ada_ring + s) * 4
                            pool.wait_ge(ada_loaded[s], two * 16 + 16)
                            pool.tensor_tensor(ada[:, s], ada[:, s],
                                               c.rearrange("p (k a) -> p k a", a=1).to_broadcast([P, KD, P]), ALU.mult
                                               ).then_inc(ada_summed, 1)
                            for n, left in enumerate((4, 2, 1)):
                                pool.wait_ge(ada_summed, done + n + 1)
                                pool.tensor_tensor(ada[:, s, 0:left], ada[:, s, 0:left], ada[:, s, left:2 * left],
                                                   ALU.add).then_inc(ada_summed, 1)

        @block.tensor
        def _(pe):


            def front_tokens(t, drained):
                pe.wait_ge(*factor_made.by("ar_bk", t))
                pe.wait_ge(*drained)
                for d in range(2):
                    pe.transpose(bank(0, 0)[:, d * P:(d + 1) * P], ar[:, d, 0], ident)
                for d in range(2):
                    mm = pe.transpose(bank(0, 0)[:, (2 + d) * P:(3 + d) * P], bk[:, 0, d], ident)
                mm.then_inc(*pe_front("tokens_a"))
                pe.wait_ge(*exp_made.by("v", t))
                for d in range(2):
                    pe.transpose(bank(1, 0)[:, d * P:(d + 1) * P], bk[:, 1, d], ident)
                for d in range(2):
                    mm = pe.transpose(bank(1, 0)[:, (2 + d) * P:(3 + d) * P], v_b[:, d], ident)
                mm.then_inc(*pe_front("tokens_b"))

            def front_scores(t, n):
                for h in heads:
                    rows = slice(64 * h, 64 * h + 64)
                    if n == 0:
                        pe.wait_ge(*act_front.by(("beta_tok", "kv_tok")[h], t))
                    else:
                        pe.wait_ge(*dve_front.by(f"mp{h}", t))
                    for d in range(2):
                        mm = pe.matmul(bank(h, 0)[:, d * 2 * P:(d + 1) * 2 * P], bk[rows, n, d],
                                       ar[rows, d].rearrange("p a t -> p (a t)"), start=True, stop=True)
                    mm.then_inc(*pe_front(("beta", "kappa")[n] + str(h)))

            def front_nv(t, par):
                for h in heads:
                    pe.wait_ge(*dve_front.by(f"nq{h}", t))
                    for d in range(2):
                        mm = pe.matmul(bank(h, 0)[:, d * CH:(d + 1) * CH], nq[:, par, h, d, 0],
                                       kv_tok[:, par, 2 + d, h * CH:(h + 1) * CH], start=True, stop=True)
                    mm.then_inc(*pe_front(f"nv{h}"))

            def front_m(t):
                for h in heads:
                    rows = slice(64 * h, 64 * h + 64)
                    pe.wait_ge(*act_front.by(f"nv{h}", t))
                    for d in range(2):
                        mm = pe.matmul(bank(h, 0)[:, d * P:(d + 1) * P], ar[rows, d, 0], bk[rows, 0, d],
                                       start=True, stop=True)
                    mm.then_inc(*pe_front(f"m{h}"))

            def modulation_products(two, par):
                for s in ((0, 1), (2,))[par]:
                    pe.wait_ge(ada_summed, (two * ada_ring + s) * 4 + 4)
                    pe.matmul(bank(0, 3)[:, 256 + s:257 + s], ada[:, s, 0], cst(core, "ones")[:, 0:1],
                              start=True, stop=True).then_inc(ada_used, 1)

            for made in (pe_front, pe_made, pe_pair):
                made.begin(pe)
            for n in range(HEAD_PAIRS):
                pe.wait_ge(kk_squared, n + 1)
                for hf in range(2):
                    mm = pe.matmul(ps[0:32, hf], head_rows(core, n), y2[:, n % 2, hf * HALF:(hf + 1) * HALF],
                                   start=(n == 0), stop=(n == HEAD_PAIRS - 1))
                mm.then_inc(kk_summed, 1)
            pe.wait_ge(kk_scaled, 2)
            pe.wait_ge(setup, 2)

            pe.wait_ge(cleared, 1)
            with pe.Fori(0, HEAD_PAIRS) as i:
                pe.wait_ge(*dve_pair.by("spread", i))
                for hf in range(2):
                    mm = pe.matmul(ps[:, 6 + hf], spread_i[:, :], kk_scale[:, hf * HALF:(hf + 1) * HALF],
                                   start=True, stop=True)
                mm.then_inc(*pe_pair("kk_scale"))
                pe.wait_ge(lora_loaded, i * 16 + 16)
                for n, (rows, w_n, z_n) in enumerate(((slice(0, 64), 0, 12), (slice(64, 128), 0, 12),
                                                      (slice(0, 64), 1, 13))):
                    for hf in range(2):
                        mm = pe.matmul(ps[:, 2 * n + hf], lora[rows, w_n], z[rows, z_n, hf * HALF:(hf + 1) * HALF],
                                       start=True, stop=True)
                    mm.then_inc(*pe_pair(f"lora{n}"))
                first = i * NBLK
                front_tokens(first, act_made.before(first))
                front_scores(first, 0)
                front_scores(first, 1)
                front_nv(first, 0)
                front_m(first)

                def turn(j, t, par, ahead, two):
                    for n in levels:
                        for h in heads:
                            if n == 1:
                                pe.wait_ge(*dve_front.by(f"x{h}", t))
                                pe.wait_ge(*dve_made.before(t))
                            else:
                                pe.wait_ge(*dve_made.by(f"x{n - 1}_{h}", t))
                            for d in range(2):
                                mm = pe.matmul(bank(h, 1)[:, d * P:(d + 1) * P], mp[:, par, h, d, 0],
                                               x[:, par, h, d], start=True, stop=True)
                            mm.then_inc(*pe_made(f"mx{n}_{h}"))
                        if ahead:
                            if n == 1:
                                front_tokens(t + 1, act_made.before(t))
                            elif n == 2:
                                front_scores(t + 1, 0)
                            elif n == 3:
                                front_scores(t + 1, 1)
                            elif n == 4:
                                front_nv(t + 1, 1 - par)
                            elif n == 5:
                                front_m(t + 1)
                        for h in heads:
                            pe.wait_ge(*dve_made.by(f"mx{n}_{h}", t))
                            if n == 1:
                                pe.wait_ge(*dve_front.by(f"xt{h}", t))
                            else:
                                pe.wait_ge(*dve_made.by(f"xt{n - 1}_{h}", t))
                            if n < 5:
                                for d in range(2):
                                    mm = pe.matmul(bank(h, 2)[:, d * P:(d + 1) * P], xt[:, par, h, d],
                                                   mx[:, n - 1, h, d], start=True, stop=True)
                                mm.then_inc(*pe_made(f"x{n}_{h}"))
                            for d in range(2):
                                mm = pe.matmul(bank(h, 3)[:, d * P:(d + 1) * P], mx[:, n - 1, h, d],
                                               xt[:, par, h, d], start=True, stop=True)
                            mm.then_inc(*pe_made(f"xt{n}_{h}"))
                    for h in heads:
                        pe.wait_ge(*dve_made.by(f"xt5_{h}", t))
                        pe.wait_ge(*act_front.by(f"nv{h}", t))
                        for d in range(2):
                            mm = pe.matmul(bank(h, 1)[:, d * P:(d + 1) * P], xt[:, par, h, d], an[:, par, h, d],
                                           start=True, stop=True)
                        mm.then_inc(*pe_made(f"wu{h}"))
                    for h in heads:
                        rows = slice(64 * h, 64 * h + 64)
                        pe.wait_ge(*act_made.by(f"wu{h}", t))
                        for d in range(2):
                            mm = pe.matmul(bank(h, 1)[rows, d * P:(d + 1) * P], wu[:, h, d, 0:CH], mp[:, par, h, d, 1],
                                           start=True, stop=True)
                        mm.then_inc(*pe_made(f"pw{h}"))
                    for h in heads:
                        rows, cols = slice(64 * h, 64 * h + 64), slice(h * CH, (h + 1) * CH)
                        for c in range(2):
                            at = slice(64 * c, 64 * c + 64)
                            out = bank(h, 2 + c)
                            for d in range(2):
                                pe.matmul(out[rows, d * CH:(d + 1) * CH], wu[at, h, d, 0:CH], beta_tok[at, par, d, cols],
                                          start=True, stop=True)
                            for d in range(2):
                                here = out[rows, (2 + d) * CH:(3 + d) * CH]
                                pe.matmul(here, beta_tok[at, par, d, cols], wu[at, h, d, CH:], start=True, stop=False)
                                mm = pe.matmul(here, kv_tok[at, par, d, cols], kv_tok[at, par, 2 + d, cols],
                                               start=False, stop=True)
                            mm.then_inc(*pe_made(f"chunk{c}_{h}"))

                    def from_block(h, d, part):
                        rows, cols = slice(64 * h, 64 * h + 64), slice(h * CH, (h + 1) * CH)
                        out = bank(h, 0)[rows, d * P:(d + 1) * P]
                        if part == 0:
                            pe.matmul(out, wu[:, h, d, CH:], mp[:, par, h, d, 1], start=(d == 0), stop=False)
                        else:
                            pe.matmul(out, kv_tok[:, par, 2 + d, cols], nq[:, par, h, d, 1], start=False, stop=False)

                    def next_state(h, m):
                        rows = slice(64 * h, 64 * h + 64)
                        for d in range(2):
                            mm = pe.matmul(bank(h, 1)[rows, (2 * m + d) * CH:(2 * m + d + 1) * CH],
                                           carry[rows, m if d == 0 else 1 - m, d], state[rows, m, d],
                                           start=True, stop=True)
                        mm.then_inc(*pe_made(f"state{m}_{h}"))

                    def from_state(h, m, mark):
                        rows = slice(64 * h, 64 * h + 64)
                        for d in range(2):
                            c = m if d == 0 else 1 - m
                            mm = pe.matmul(bank(h, 0)[rows, d * P + c * CH:d * P + (c + 1) * CH],
                                           state[rows, m, d], rho2[rows, d, c * CH:(c + 1) * CH],
                                           start=False, stop=(m == 1 and d == 1))
                        mm.then_inc(*pe_made(mark))

                    pe.wait_ge(*act_made.before(t))
                    for h in heads:
                        if ahead:
                            pe.wait_ge(*dve_front.by(f"x{h}", t + 1))
                        from_block(h, 0, 0)
                    for h in heads:
                        pe.wait_ge(*dve_made.by(f"chunk1_{h}", t))
                        from_block(h, 0, 1)
                        next_state(h, 0)
                        from_block(h, 1, 0)
                    for h in heads:
                        pe.wait_ge(*dve_made.by(f"state0_{h}", t))
                        from_block(h, 1, 1)
                        from_state(h, 0, f"from_state{h}")
                        next_state(h, 1)
                        from_state(h, 1, f"y{h}")
                    modulation_products(two, par)
                turns(pe, i, turn)

        @block.vector
        def _(dve):
            for made in (ex_made, dve_front, dve_made, dve_pair):
                made.begin(dve)
            dve.tensor_scalar(ka_rest[:, :], core.vec[:, VEC["k_a"]:VEC["k_a"] + 4], -1.0, 1.0, ALU.mult,
                              ALU.add).then_inc(rest_ready, 1)
            dve.wait_ge(rest_ready, 1)
            dve.wait_ge(loaded, 16)

            dve.wait_ge(kk_summed, HEAD_PAIRS)
            dve.tensor_scalar(kk_scale, ps[0:32, 0:2].rearrange("p a t -> p (a t)"), 1e-24, None, ALU.max
                              ).then_inc(kk_scaled, 1)
            dve.wait_ge(setup, 2)
            dve.reciprocal(kk_scale, kk_scale).then_inc(kk_scaled, 1)

            def front_scores(t, par, n):
                s, dst = (("mp", mp), ("nq", nq))[n]
                for h in heads:
                    dve.wait_ge(*pe_front.by(("beta", "kappa")[n] + str(h), t))
                    dve.tensor_tensor(dst[:, par, h].rearrange("p d a t -> p (d a t)"), bank(h, 0),
                                      score_mask.rearrange("p a t -> p (a t)"), ALU.mult
                                      ).then_inc(*dve_front(f"{s}{h}"))

            def before_token(t, j, last_used):
                dve.wait_ge(*last_used)
                for d in range(2):
                    at = tokens(d, j)
                    ins = dve.tensor_tensor(e_alpha[:, d], cum[:, d, at], sig[:, d, at], ALU.subtract)
                ins.then_inc(*ex_made("ex"))

            def front_xt(t, par):
                for h in heads:
                    dve.wait_ge(*dve_front.by(f"mp{h}", t))
                    dve.tensor_tensor(xt[:, par, h], mp[:, par, h, :, 0], level1_t, ALU.mult
                                      ).then_inc(*dve_front(f"xt{h}m"))
                for h in heads:
                    dve.wait_ge(*dve_front.by(f"xt{h}m", t))
                    dve.tensor_tensor(xt[:, par, h], xt[:, par, h], eye, ALU.add).then_inc(*dve_front(f"xt{h}"))

            def front_x(t, par):
                for h in heads:
                    dve.wait_ge(*pe_front.by(f"m{h}", t))
                    dve.tensor_tensor(x[:, par, h], pairs(bank(h, 0)[:, 0:2 * P]), level1_m, ALU.mult
                                      ).then_inc(*dve_front(f"x{h}m"))
                for h in heads:
                    dve.wait_ge(*dve_front.by(f"x{h}m", t))
                    dve.tensor_tensor(x[:, par, h], x[:, par, h], eye, ALU.add).then_inc(*dve_front(f"x{h}"))

            with dve.Fori(0, HEAD_PAIRS) as i:
                r_i, k_i = tile_of(z, i + 0), tile_of(z, i + 4)
                dve.wait_ge(*pe_pair.before(i))
                dve.tensor_copy(spread_i[:, :], cst(core, "spread", i)[0:32]).then_inc(*dve_pair("spread"))
                dve.wait_ge(*pe_pair.by("kk_scale", i))
                dve.scalar_tensor_tensor(kk[:, :], k_i, vec(core, "k_k", i), ps[:, 6:8].rearrange("p a t -> p (a t)"),
                                         ALU.mult, ALU.mult).then_inc(*dve_pair("kk"))
                dve.wait_ge(*act_pair.by("sig0", i))
                dve.tensor_tensor_scan(cum[:, 0], keep[:, 0], sig[:, 0], 0.0, ALU.mult, ALU.add
                                       ).then_inc(*dve_pair("cum0"))
                dve.wait_ge(*act_pair.by("sig1", i))
                dve.tensor_tensor_scan(cum[:, 1, ::-1], keep[:, 1, ::-1], sig[:, 1, ::-1], 0.0, ALU.mult, ALU.add
                                       ).then_inc(*dve_pair("cum1"))
                dve.wait_ge(*act_pair.by("rate", i))
                dve.wait_ge(*dve_pair.by("kk", i))
                dve.scalar_tensor_tensor(b[:, :], kk[:, :], -1.0, rate, ALU.mult, ALU.mult).then_inc(*dve_pair("b"))
                dve.memset(state[:, 0], 0.0).then_inc(*dve_pair("zero"))
                dve.wait_ge(*dve_pair.by("zero", i))
                before_token(i * NBLK, 0, factor_made.before(i * NBLK))
                front_scores(i * NBLK, 0, 0)
                before_token(i * NBLK + 1, 1, factor_made.by("ar_bk", i * NBLK))
                front_scores(i * NBLK, 0, 1)
                front_xt(i * NBLK, 0)
                front_x(i * NBLK, 0)

                def turn(j, t, par, ahead, two):
                    for n in levels:
                        for h in heads:
                            dve.wait_ge(*pe_made.by(f"mx{n}_{h}", t))
                            dve.tensor_tensor(joined(mx[:, n - 1, h], n), joined(pairs(bank(h, 1)[:, 0:2 * P]), n),
                                              level_mask[:, n - 1].rearrange("p d (b s) -> p d b s", s=2 ** n), ALU.mult
                                              ).then_inc(*dve_made(f"mx{n}_{h}"))
                        for h in heads:
                            if n < 5:
                                dve.wait_ge(*pe_made.by(f"x{n}_{h}", t))
                                at = joined(x[:, par, h], n)
                                dve.tensor_tensor(at, at, joined(pairs(bank(h, 2)[:, 0:2 * P]), n), ALU.add
                                                  ).then_inc(*dve_made(f"x{n}_{h}"))
                            dve.wait_ge(*pe_made.by(f"xt{n}_{h}", t))

                            at = joined(xt[:, par, h], n, True)
                            dve.tensor_tensor(at, at, joined(pairs(bank(h, 3)[:, 0:2 * P]), n, True), ALU.add
                                              ).then_inc(*dve_made(f"xt{n}_{h}"))
                        if ahead and n in (2, 3):
                            front_scores(t + 1, 1 - par, n - 2)
                        if ahead and n == 4:
                            front_xt(t + 1, 1 - par)
                        if ahead > 1 and n == 1:
                            before_token(t + 2, j + 2, factor_made.by("ar_bk", t + 1))
                        if ahead and n == 5:
                            front_x(t + 1, 1 - par)
                    for h in heads:
                        rows = slice(64 * h, 64 * h + 64)
                        dve.wait_ge(*pe_made.by(f"pw{h}", t))
                        dve.wait_ge(*act_front.by("decay", t))
                        dve.tensor_tensor(rho2[rows], pairs(bank(h, 1)[rows, 0:2 * P]), rho[rows, par], ALU.add
                                          ).then_inc(*dve_made(f"rho2_{h}"))
                    for h in heads:
                        rows = slice(64 * h, 64 * h + 64)
                        eye64 = cst(core, "eye64")[rows, 0:CH].rearrange("p (a c) -> p a c", a=1).to_broadcast([64, 2, CH])
                        for c in range(2):
                            dve.wait_ge(*pe_made.by(f"chunk{c}_{h}", t))
                            dve.tensor_tensor(carry[rows, c], pairs(bank(h, 2 + c)[rows, 0:2 * CH]), eye64, ALU.add)
                            for d in range(2):
                                ins = dve.tensor_scalar(gain[rows, c, d], bank(h, 2 + c)[rows, (2 + d) * CH:(3 + d) * CH],
                                                        decay[rows, par, d, c:c + 1], None, ALU.mult)
                            ins.then_inc(*dve_made(f"chunk{c}_{h}"))
                    for m in range(2):
                        for h in heads:
                            rows = slice(64 * h, 64 * h + 64)
                            dve.wait_ge(*pe_made.by(f"state{m}_{h}", t))
                            if m == 0:
                                dve.wait_ge(*dve_made.by(f"chunk1_{h}", t))
                            else:
                                dve.wait_ge(*pe_made.by(f"from_state{h}", t))
                            for d in range(2):
                                c = m if d == 0 else 1 - m
                                ins = dve.scalar_tensor_tensor(
                                    state[rows, 1 - m, d], bank(h, 1)[rows, (2 * m + d) * CH:(2 * m + d + 1) * CH],
                                    decay[rows, par, d, c:c + 1], gain[rows, c, d], ALU.mult, ALU.add)
                            ins.then_inc(*dve_made(f"state{m}_{h}"))
                    first, count = (0, 2) if par == 0 else (2, 1)
                    dve.wait_ge(ada_used, two * ada_ring + first + count)
                    dve.tensor_copy(mod[:, ds(two * ada_ring + first, count)],
                                    bank(0, 3)[:, 256 + first:256 + first + count]).then_inc(mod_copied, 1)

                turns(dve, i, turn)
                dve.scalar_tensor_tensor(r_i, r_i, vec(core, "r_k", i), k_i, ALU.mult, ALU.mult).then_inc(*dve_pair("rk"))
                dve.wait_ge(*act_made.before((i + 1) * NBLK))
                dve.wait_ge(*dve_pair.by("rk", i))
                dve.tensor_tensor(k_i, y2[:, 0], y2[:, 1], ALU.add).then_inc(*dve_pair("y"))

            dve.wait_ge(mod_copied, HEAD_PAIRS * NBLK)
            dve.tensor_tensor(mod[:, :], mod[:, :], core.vec[:, VEC["ada_b"]:VEC["ada_b"] + 6 * KD], ALU.add
                              ).then_inc(mod_ready, 1)
            dve.wait_ge(mod_ready, 1)
            own = core.vec[:, VEC["gains2"]:VEC["gains2"] + 4 * KD].rearrange("p (a k) -> p a k", k=KD)
            for half in range(2):
                shift, scale, gate = (mod[:, (3 * half + n) * KD:(3 * half + n + 1) * KD] for n in range(3))
                dve.scalar_tensor_tensor(gains[:, 3 * half], scale, 1.0, own[:, 2 * half], ALU.add, ALU.mult)
                dve.tensor_copy(gains[:, 3 * half + 1], shift)
                dve.tensor_tensor(gains[:, 3 * half + 2], gate, own[:, 2 * half + 1], ALU.mult).then_inc(mod_ready, 1)


def rwkv_finish(core, dram_lora, z, y_gla, hi, lo):
    nc = core.nc
    with ExitStack() as ctx:
        gate_lora = ctx.enter_context(nc.sbuf_tensor("rf_gate_lora", [P, 512], F32))
        square = ctx.enter_context(nc.sbuf_tensor("rf_square", [P, 2, T], F32))
        scale = ctx.enter_context(nc.sbuf_tensor("rf_scale", [32, T], F32))
        ps = ctx.enter_context(nc.psum_tensor("rf_ps", [P, 8, 512], F32))
        loaded = core.sem("rf_loaded")
        summed, centred, squared, var_summed = (core.sem(f"rf_{n}") for n in ("summed", "centred", "squared", "var_summed"))
        bonus_summed, bonus, shifted = (core.sem(f"rf_{n}") for n in ("bonus_summed", "bonus", "shifted"))
        hi_gla, hi_rwkv, lo_done = (core.sem(f"rf_{n}") for n in ("hi_gla", "hi_rwkv", "lo_done"))
        lo_gla_done = core.sem("rf_lo_gla_done")
        gate_lora_ready, rooted, scale_ready = (core.sem(f"rf_{n}") for n in ("gate_lora_ready", "rooted", "scale_ready"))
        spread, gated, scaled, joined, done = (core.sem(f"rf_{n}") for n in ("spread", "gated", "scaled", "joined", "done"))
        block = ctx.enter_context(nc.Block())
        tiles = range(HEAD_PAIRS)

        def wide(first_bank):
            return ps[:, first_bank:first_bank + 2].rearrange("p a t -> p (a t)")

        def low_part(e, n, src, tile, hi_made):
            e.wait_ge(hi_made, n + 1)
            e.tensor_tensor(lo[:, tile], src, hi[:, tile].bitcast(F32), ALU.subtract).then_inc(
                lo_done if hi_made is hi_rwkv else lo_gla_done, 1)

        def finish(dve, n):
            dve.wait_ge(joined, n + 1)
            dve.wait_ge(gated, n + 1)
            dve.tensor_tensor(z[:, n], z[:, 4 + n], wide((0, 2)[n % 2]), ALU.mult).then_inc(done, 1)

        @block.sync
        def _(sp):
            sp.dma_start(gate_lora[:, :], dram_lora[:, 2]).then_inc(loaded, 16)

        @block.tensor
        def _(pe):
            def product(lhs, rhs, first_bank, **flags):
                for hf in range(2):
                    mm = pe.matmul(ps[0:lhs.shape[-1], first_bank + hf], lhs, rhs[:, hf * HALF:(hf + 1) * HALF], **flags)
                return mm

            once = {"start": True, "stop": True}
            def var_sum(n):
                pe.wait_ge(squared, n + 1)
                product(head_rows(core, n), square[:, n % 2], 4, start=(n == 0), stop=(n == HEAD_PAIRS - 1)
                        ).then_inc(var_summed, 1)

            for n in tiles:
                if n >= 2:
                    pe.wait_ge(centred, n - 1)
                product(cst(core, "head_ones"), z[:, 4 + n], (0, 6)[n % 2], **once).then_inc(summed, 1)
                if n >= 1:
                    pe.wait_ge(bonus, n)
                product(cst(core, "head_ones"), z[:, n], 2, **once).then_inc(bonus_summed, 1)
                if n >= 1:
                    var_sum(n - 1)
            var_sum(HEAD_PAIRS - 1)
            pe.wait_ge(loaded, 16)
            pe.wait_ge(gate_lora_ready, 1)
            pe.wait_ge(centred, HEAD_PAIRS)
            pe.wait_ge(bonus, HEAD_PAIRS)
            for n in tiles:
                if n >= 2:
                    pe.wait_ge(done, n - 1)
                product(gate_lora[:, n * P:(n + 1) * P], z[:, 14], (0, 2)[n % 2], **once).then_inc(gated, 1)
                pe.wait_ge(scale_ready, 1)
                if n >= 2:
                    pe.wait_ge(scaled, n - 1)
                product(head_spread(core, n), scale, (4, 6)[n % 2], **once).then_inc(spread, 1)

        @block.scalar
        def _(act):
            act.activation(z[:, 14], z[:, 14], ACT.Sigmoid).then_inc(gate_lora_ready, 1)
            for n in tiles:
                act.copy(hi[:, 4 + n], y_gla[:, n]).then_inc(hi_gla, 1)
                act.wait_ge(centred, n + 1)
                if n >= 2:
                    act.wait_ge(var_summed, n - 1)
                act.activation(square[:, n % 2], z[:, 4 + n], ACT.Square).then_inc(squared, 1)
                act.wait_ge(bonus, n + 1)
                act.activation(z[:, 8 + n], z[:, 8 + n], ACT.Identity, bias=vec(core, "ln_b", n)).then_inc(shifted, 1)
            act.wait_ge(var_summed, HEAD_PAIRS)
            act.activation(scale[:, :], wide(4)[0:32], ACT.Sqrt, bias=eps(core, EPS_GN)[0:32], scale=1.0 / CH
                           ).then_inc(rooted, 1)
            for n in tiles:
                act.wait_ge(done, n + 1)
                act.copy(hi[:, n], z[:, n]).then_inc(hi_rwkv, 1)

        @block.vector
        def _(dve):
            for n in tiles:
                dve.wait_ge(summed, n + 1)
                dve.scalar_tensor_tensor(z[:, 4 + n], wide((0, 6)[n % 2]), 1.0 / CH, z[:, 4 + n], ALU.mult, ALU.subtract
                                         ).then_inc(centred, 1)
                dve.wait_ge(bonus_summed, n + 1)
                dve.tensor_tensor(z[:, 8 + n], wide(2), z[:, 8 + n], ALU.mult).then_inc(bonus, 1)
            dve.wait_ge(rooted, 1)
            dve.reciprocal(scale[:, :], scale[:, :]).then_inc(scale_ready, 1)
            for n in tiles:
                dve.wait_ge(spread, n + 1)
                dve.scalar_tensor_tensor(z[:, 4 + n], z[:, 4 + n], vec(core, "ln_w", n), wide((4, 6)[n % 2]),
                                         ALU.mult, ALU.mult).then_inc(scaled, 1)
                if n >= 1:
                    finish(dve, n - 1)
                if n >= 2:
                    low_part(dve, n - 2, z[:, n - 2], n - 2, hi_rwkv)
            finish(dve, HEAD_PAIRS - 1)
            for n in (HEAD_PAIRS - 2, HEAD_PAIRS - 1):
                low_part(dve, n, z[:, n], n, hi_rwkv)

        @block.gpsimd
        def _(pool):
            for n in tiles:
                low_part(pool, n, y_gla[:, n], 4 + n, hi_gla)
            for n in tiles:
                pool.wait_ge(scaled, n + 1)
                pool.wait_ge(shifted, n + 1)
                pool.tensor_tensor(z[:, 4 + n], z[:, 4 + n], z[:, 8 + n], ALU.add).then_inc(joined, 1)


def split_tiles(core, name, sources, hi, lo):
    hi_done, lo_done = core.sem(f"{name}_hi"), [core.sem(f"{name}_lo"), core.sem(f"{name}_lo_pool")]
    with core.nc.Block() as block:
        def low_part(e, n, done):
            e.wait_ge(hi_done, n + 1)
            e.tensor_tensor(lo[:, n], sources[n], hi[:, n].bitcast(F32), ALU.subtract).then_inc(done, 1)

        @block.scalar
        def _(act):
            for n, src in enumerate(sources):
                act.copy(hi[:, n], src).then_inc(hi_done, 1)

        @block.vector
        def _(dve):
            for n in range(len(sources)):
                if n % 3 != 1:
                    low_part(dve, n, lo_done[0])

        @block.gpsimd
        def _(pool):
            for n in range(1, len(sources), 3):
                low_part(pool, n, lo_done[1])


def swiglu(core, name, w_gate, w_up, w_down, x_hi, x_lo, f, spare):
    nc = core.nc
    with ExitStack() as ctx:
        def sbr(n, shape):
            return ctx.enter_context(nc.sbuf_tensor(f"{name}_{n}", shape, F32R))
        raw = {s: spare[:, n] for n, s in enumerate(("gate", "up", "down"))}
        silu = spare[:, 3]
        w_hi = {s: sbr(f"{s}_hi", [P, KD, P]) for s in raw}
        w_lo = {s: sbr(f"{s}_lo", [P, KD, P]) for s in raw}
        a_hi, a_lo = sbr("a_hi", [P, 2, T]), sbr("a_lo", [P, 2, T])
        a = ctx.enter_context(nc.sbuf_tensor(f"{name}_a", [P, T], F32))
        acc = {s: ctx.enter_context(nc.psum_tensor(f"{name}_ps_{s}", [P, T], F32)) for s in ("gate", "up")}
        acc_down = ctx.enter_context(nc.psum_tensor(f"{name}_ps_down", [P, 2, T], F32))
        dram = {"gate": w_gate, "up": w_up, "down": w_down}
        loaded = {s: core.sem(f"{name}_{s}_loaded") for s in raw}
        hi_ready = {s: core.sem(f"{name}_{s}_hi_ready") for s in raw}
        lo_ready = {s: core.sem(f"{name}_{s}_lo_ready") for s in raw}
        filled = {s: core.sem(f"{name}_{s}_filled") for s in raw}
        zeroed, silu_ready, a_ready, a_hi_ready, a_lo_ready, added = (
            core.sem(f"{name}_{n}") for n in ("zeroed", "silu_ready", "a_ready", "a_hi_ready", "a_lo_ready", "added"))
        block = ctx.enter_context(nc.Block())

        def cycles(e, body):
            body(0, 0)
            body(1, 1)
            with e.Fori(0, (NF - 4) // 2) as i:
                body(i * 2 + 2, 0)
                body(i * 2 + 3, 1)
            body(NF - 2, 0)
            body(NF - 1, 1)

        def more(j):
            return not (isinstance(j, int) and j == NF - 1)

        @block.sync
        def _(sp):
            def body(j, par):
                for s in raw:
                    sp.wait_ge(lo_ready[s], j)
                    src = dram[s][j] if isinstance(j, int) else dram[s][ds(j, 1)].rearrange("a p k -> (a p) k")
                    sp.dma_start(raw[s], src).then_inc(loaded[s], 16)
            cycles(sp, body)

        def split_hi(act, s, j):
            act.wait_ge(loaded[s], j * 16 + 16)
            act.wait_ge(filled[s], j * (KD if s == "down" else 1))
            act.copy(w_hi[s][:, :, :].rearrange("p k c -> p (k c)"), raw[s]).then_inc(hi_ready[s], 1)

        def split_lo(dve, s, j):
            dve.wait_ge(hi_ready[s], j + 1)
            dve.tensor_tensor(w_lo[s][:, :, :].rearrange("p k c -> p (k c)"), raw[s],
                              w_hi[s][:, :, :].rearrange("p k c -> p (k c)").bitcast(F32),
                              ALU.subtract).then_inc(lo_ready[s], 1)

        @block.scalar
        def _(act):
            split_hi(act, "gate", 0)
            split_hi(act, "up", 0)

            def body(j, par):
                act.wait_ge(filled["gate"], j + 1)
                act.wait_ge(a_ready, j)
                act.activation(silu, acc["gate"][:, :], ACT.Silu).then_inc(silu_ready, 1)
                if more(j):
                    split_hi(act, "gate", j + 1)
                    split_hi(act, "up", j + 1)
                act.wait_ge(a_ready, j + 1)
                act.copy(a_hi[:, par], a[:, :]).then_inc(a_hi_ready, 1)
                split_hi(act, "down", j)
            cycles(act, body)

        @block.vector
        def _(dve):
            split_lo(dve, "gate", 0)
            split_lo(dve, "up", 0)
            dve.wait_ge(zeroed, 1)

            def add_down(j):
                for n in range(KD):
                    dve.wait_ge(filled["down"], j * KD + n + 1)
                    dve.tensor_tensor(f[:, n], f[:, n], acc_down[:, n % 2], ALU.add).then_inc(added, 1)

            def body(j, par):
                if more(j):
                    split_lo(dve, "gate", j + 1)
                dve.wait_ge(silu_ready, j + 1)
                dve.wait_ge(filled["up"], j + 1)
                dve.wait_ge(a_lo_ready, j)
                dve.tensor_tensor(a[:, :], silu, acc["up"][:, :], ALU.mult).then_inc(a_ready, 1)
                if not (isinstance(j, int) and j == 0):
                    add_down(j - 1)
                if more(j):
                    split_lo(dve, "up", j + 1)
                dve.wait_ge(a_hi_ready, j + 1)
                dve.tensor_tensor(a_lo[:, par], a[:, :], a_hi[:, par].bitcast(F32), ALU.subtract).then_inc(a_lo_ready, 1)
                split_lo(dve, "down", j)
            cycles(dve, body)
            add_down(NF - 1)

        @block.gpsimd
        def _(pool):
            pool.memset(f, 0.0).then_inc(zeroed, 1)

        @block.tensor
        def _(pe):
            def down(j, par):
                pe.wait_ge(a_lo_ready, j + 1)
                pe.wait_ge(lo_ready["down"], j + 1)
                for n in range(KD):
                    if not (isinstance(j, int) and j == 0 and n < 2):
                        pe.wait_ge(added, j * KD + (n - 1))
                    for w, x in ((w_hi, a_hi), (w_hi, a_lo), (w_lo, a_hi)):
                        for h in range(2):
                            mm = pe.matmul(acc_down[:, n % 2, h * HALF:(h + 1) * HALF], w["down"][:, n],
                                           x[:, par, h * HALF:(h + 1) * HALF],
                                           start=(w is w_hi and x is a_hi), stop=(w is w_lo))
                    mm.then_inc(filled["down"], 1)

            def body(j, par):
                for s in ("gate", "up"):
                    pe.wait_ge(lo_ready[s], j + 1)
                    pe.wait_ge(silu_ready if s == "gate" else a_ready, j)
                    for k in range(KD):
                        for w, x in ((w_hi, x_hi), (w_hi, x_lo), (w_lo, x_hi)):
                            for h in range(2):
                                mm = pe.matmul(acc[s][:, h * HALF:(h + 1) * HALF], w[s][:, k],
                                               x[:, k, h * HALF:(h + 1) * HALF],
                                               start=(k == 0 and w is w_hi and x is x_hi),
                                               stop=(k == KD - 1 and w is w_lo))
                    mm.then_inc(filled[s], 1)
                if not (isinstance(j, int) and j == 0):
                    down(j - 1, 1 - par)
            cycles(pe, body)
            down(NF - 1, 1)


def project(core, name, w, x_hi, x_lo, out, load=None):
    def act_epilogue(act, m, r, kind, psum, filled, drained):
        act.wait_ge(filled, m + 1)
        act.copy(tile_of(out, m), psum).then_inc(drained, 1)
    dense(core, name, w, x_hi, x_lo, [(0, KD, None)], act_epilogue, load=load)


def embedding_gate(core, w, h_hi, h_lo, e):
    nc = core.nc
    with ExitStack() as ctx:
        gate = ctx.enter_context(nc.sbuf_tensor("eg_gate", [P, 2, T], F32))
        gated = core.sem("eg_gated")

        def act_epilogue(act, m, r, kind, psum, filled, drained):
            act.wait_ge(filled, m + 1)
            if not (isinstance(m, int) and m < 2):
                act.wait_ge(gated, m - 1)
            act.activation(gate[:, r % 2], psum, ACT.Sigmoid, bias=vec(core, "ple_b", m)).then_inc(drained, 1)

        def dve_epilogue(dve, m, r, kind, drained):
            dve.wait_ge(drained, m + 1)
            dve.tensor_tensor(tile_of(e, m), tile_of(e, m), gate[:, r % 2], ALU.mult).then_inc(gated, 1)

        dense(core, "eg", w, h_hi, h_lo, [(0, KD, None)], act_epilogue, dve_epilogue)


def short_conv(core, w, x_hi, x_lo, y):
    nc = core.nc
    with ExitStack() as ctx:
        cvb = ctx.enter_context(nc.sbuf_tensor("sc_cvb", [P, 3, T], F32))
        u = ctx.enter_context(nc.sbuf_tensor("sc_u", [P, T + 2], F32))
        conv = ctx.enter_context(nc.sbuf_tensor("sc_conv", [P, T], F32))
        padded = core.sem("sc_padded")
        dve_made = Marks(core.sem("sc_dve"), ["u", "tap0", "tap1", "conv", "y"])

        def act_epilogue(act, m, r, jt, psum, filled, drained):
            act.wait_ge(filled, m + 1)
            if not (isinstance(m, int) and m < 3):
                act.wait_ge(*dve_made.by("u" if r % 3 < 2 else "y", jt - 1))
            act.copy(cvb[:, r % 3], psum).then_inc(drained, 1)

        def dve_epilogue(dve, m, r, jt, drained):
            if r % 3 == 1:
                dve.wait_ge(drained, m + 1)
                dve.tensor_tensor(u[:, 2:T + 2], cvb[:, 0], cvb[:, 1], ALU.mult).then_inc(*dve_made("u"))
                dve.wait_ge(*dve_made.by("u", jt))
                dve.tensor_scalar(conv[:, :], u[:, 0:T], vec(core, "conv2", jt), None, ALU.mult
                                  ).then_inc(*dve_made("tap0"))
                dve.wait_ge(*dve_made.by("tap0", jt))
                dve.scalar_tensor_tensor(conv[:, :], u[:, 1:T + 1], vec(core, "conv2", KD + jt), conv[:, :],
                                         ALU.mult, ALU.add).then_inc(*dve_made("tap1"))
                dve.wait_ge(*dve_made.by("tap1", jt))
                dve.scalar_tensor_tensor(conv[:, :], u[:, 2:T + 2], vec(core, "conv2", 2 * KD + jt), conv[:, :],
                                         ALU.mult, ALU.add).then_inc(*dve_made("conv"))
            if r % 3 == 2:
                dve.wait_ge(drained, m + 1)
                dve.wait_ge(*dve_made.by("conv", jt))
                dve.tensor_tensor(tile_of(y, jt), cvb[:, 2], conv[:, :], ALU.mult).then_inc(*dve_made("y"))

        def dve_first(dve):
            dve_made.begin(dve)
            dve.memset(u[:, :], 0.0).then_inc(padded, 1)
            dve.wait_ge(padded, 1)

        dense(core, "sc", w, x_hi, x_lo, [(0, 3 * KD, "third")], act_epilogue, dve_epilogue, unroll=6,
              dve_first=dve_first)


def load_inputs(core, d_vec, d_const, d_x, h):
    nc = core.nc
    loaded = core.sem("in_loaded")
    with nc.Block() as block:
        @block.sync
        def _(sp):
            sp.dma_start(core.vec[:, :], d_vec).then_inc(loaded, 16)
            sp.dma_start(core.const[:, :], d_const[:, 0:N_STAY * P]).then_inc(loaded, 16)
            sp.dma_start(h, d_x).then_inc(loaded, 16)
            sp.wait_ge(loaded, 48)


def build(nc, a, out, tap=None, stop=None):
    with ExitStack() as ctx:
        core = Core(nc, ctx)
        core.vec = ctx.enter_context(nc.sbuf_tensor("vec", [P, NVEC], F32))
        core.const = ctx.enter_context(nc.sbuf_tensor("const", [P, N_STAY * P], F32))
        big = ctx.enter_context(nc.sbuf_tensor("big", [P, 20, T], F32))
        z, y_gla = big[:, 0:16], big[:, 16:20]

        def dump(view):
            done = core.sem("dumped")
            with nc.Block() as block:
                @block.sync
                def _(sp):
                    sp.dma_start(tap, view).then_inc(done, 16)
                    sp.wait_ge(done, 16)

        h = z[:, 0:8]
        load_inputs(core, a["vec"], a["const"], a["x"], h)
        with ExitStack() as scope:
            xn_hi = scope.enter_context(nc.sbuf_tensor("xn_hi", [P, KD, T], F32R))
            xn_lo = scope.enter_context(nc.sbuf_tensor("xn_lo", [P, KD, T], F32R))
            joint(core, "pre", None, None, h, core.vec[:, VEC["norm_mix_pre"]:VEC["norm_mix_pre"] + 8], None,
                  xn_hi, xn_lo)
            gla_project(core, a["w_gla"], xn_hi, xn_lo, z, z[:, 12])
            with ExitStack() as inner:
                sums = inner.enter_context(nc.sbuf_tensor("gla_sums", [P, 2, 2, T], F32))
                gla_decay(core, a["const"], a["gla_a_up"], z[:, 12], sums)
                gla_direction(core, a["const"], z, sums, y_gla, 0)
                gla_direction(core, a["const"], z, sums, y_gla, 1)
            gla_finish(core, z, y_gla)
            if stop == "gla":
                return dump(y_gla)
            rwkv_project(core, a["w_rwkv"], xn_hi, xn_lo, z)
            if stop == "zr":
                return dump(z[:, 0:15])
        gains = ctx.enter_context(nc.sbuf_tensor("gains", [P, 6, KD], F32))
        rwkv_mix(core, a["const"], a["lora"], a["ada"], z, gains)
        core.clear_sems()
        x_hi = ctx.enter_context(nc.sbuf_tensor("x_hi", [P, KD, T], F32R))
        x_lo = ctx.enter_context(nc.sbuf_tensor("x_lo", [P, KD, T], F32R))
        rwkv_finish(core, a["lora"], z, y_gla, x_hi, x_lo)
        if stop == "rwkv":
            return dump(z[:, 0:4])
        core.clear_sems()

        def own(name):
            return core.vec[:, VEC[name]:VEC[name] + KD]

        y, spare = z[:, 8:16], big[:, 16:20]
        project(core, "wo", a["w_out"], x_hi, x_lo, y, load=(h, a["x"]))
        joint(core, "mix", y, own("norm_mix_post"), h, own("norm_ffn_pre"), None, x_hi, x_lo)
        if stop == "h1":
            return dump(h)
        swiglu(core, "f1", a["ffn_gate"], a["ffn_up"], a["ffn_down"], x_hi, x_lo, y, spare)
        joint(core, "ffn", y, own("norm_ffn_post"), h, None, None, x_hi, x_lo,
              load=(spare[:, 0:2], a["p"]))
        if stop == "h2":
            return dump(h)
        with ExitStack() as scope:
            p_hi = scope.enter_context(nc.sbuf_tensor("p_hi", [P, 2, T], F32R))
            p_lo = scope.enter_context(nc.sbuf_tensor("p_lo", [P, 2, T], F32R))
            split_tiles(core, "ps", [spare[:, 0], spare[:, 1]], p_hi, p_lo)
            project(core, "pe", a["ple_proj"], p_hi, p_lo, y)
        embedding_gate(core, a["ple_gate"], x_hi, x_lo, y)
        joint(core, "ple", y, own("norm_ple"), h, gains[:, 0], gains[:, 1], x_hi, x_lo)
        if stop == "h3":
            return dump(h)
        short_conv(core, a["conv_in"], x_hi, x_lo, y)
        split_tiles(core, "cs", [y[:, n] for n in range(KD)], x_hi, x_lo)
        project(core, "co", a["conv_out"], x_hi, x_lo, y)
        joint(core, "conv", y, gains[:, 2], h, gains[:, 3], gains[:, 4], x_hi, x_lo)
        swiglu(core, "f2", a["ffn2_gate"], a["ffn2_up"], a["ffn2_down"], x_hi, x_lo, y, spare)
        joint(core, "out", y, gains[:, 5], h, None, None, None, None, store=out)


def tiled(w):
    k, n = w.shape
    nt = -(-n // P)
    full = np.zeros((k, nt * P), w.dtype)
    full[:, :n] = w
    return np.ascontiguousarray(full.reshape(k // P, P, nt, P).transpose(2, 1, 0, 3).reshape(nt, P, k))


def by_tile(v):
    return np.ascontiguousarray(np.asarray(v).reshape(-1, P).T)


def channels_first(x):
    t, c = x.shape
    return np.ascontiguousarray(x.T.reshape(c // P, P, t).transpose(1, 0, 2))


def laid_out(i):
    w_in, mu = i["w_in"][0], i["rwkv_mu"][0]
    zero = lambda n: np.zeros((w_in.shape[0], n), w_in.dtype)
    w_rwkv = np.concatenate([w_in[:, :1728], zero(64), w_in[:, 1728:1856]], axis=1)
    g = w_in[:, 1856:]
    w_gla = np.concatenate([g[:, :1536], g[:, 1536:1552], zero(16), g[:, 1552:1568], zero(80)], axis=1)
    a = {"x": channels_first(i["x"][0]), "p": channels_first(i["p"][0, 0]), "const": constants()}
    a["w_rwkv"], a["w_gla"] = tiled(w_rwkv), tiled(w_gla)
    up = np.zeros((P, 256), w_in.dtype)
    up[0:16], up[32:48] = i["gla_a_up"][0, 0], i["gla_a_up"][0, 1]
    a["gla_a_up"] = up
    lora = np.zeros((P, 3, 512), w_in.dtype)
    lora[:, 0] = i["rwkv_w_up"][0].reshape(P, 512)
    lora[0:64, 1] = i["rwkv_a_up"][0]
    lora[:, 2] = i["rwkv_g_up"][0]
    a["lora"] = lora
    a["w_out"] = tiled(i["w_out"][0])
    for n in ("gate", "up"):
        a[f"ffn_{n}"] = tiled(i[f"ffn_{n}"][0])
    a["ffn_down"] = np.ascontiguousarray(i["ffn_down"][0].reshape(NF, P, D))
    a["ple_proj"], a["ple_gate"] = tiled(i["ple_proj"][0]), tiled(i["ple_gate"][0])
    a["ada"] = tiled(i["ada_w_2"][0])
    c_in = i["conv_w_in_2"][0].reshape(D, 3, KD, P)
    a["conv_in"] = tiled(c_in[:, [1, 2, 0]].transpose(0, 2, 1, 3).reshape(D, 3 * D))
    a["conv_out"] = tiled(i["conv_w_out_2"][0])
    gu = i["ffn_w_gate_up_2"][0]
    a["ffn2_gate"], a["ffn2_up"] = tiled(gu[:, :FF]), tiled(gu[:, FF:])
    a["ffn2_down"] = np.ascontiguousarray(i["ffn_w_down_2"][0].reshape(NF, P, D))
    mu_l = np.concatenate([mu[:1728], np.zeros(64, mu.dtype), mu[1728:]])
    fields = {
        "norm_mix_pre": i["norm_mix_pre"], "norm_mix_post": i["norm_mix_post"], "norm_ffn_pre": i["norm_ffn_pre"],
        "norm_ffn_post": i["norm_ffn_post"], "norm_ple": i["norm_ple"], "mu": mu_l, "w0": i["rwkv_w0"],
        "a0": i["rwkv_a0"], "k_k": i["rwkv_k_k"], "k_a": i["rwkv_k_a"], "r_k": i["rwkv_r_k"],
        "ln_w": i["rwkv_ln_w"], "ln_b": i["rwkv_ln_b"], "conv": i["gla_conv"], "a_b": i["gla_a_b"],
        "gla_norm": i["gla_norm"], "ple_b": i["ple_gate_b"], "c": i["c_2"], "ada_b": i["ada_b_2"],
        "gains2": i["norm_gains_2"], "conv2": i["conv_w_2"],
    }
    a["vec"] = np.concatenate([by_tile(fields[n]) for n, _ in VEC_FIELDS], axis=1)
    return a


def kernel(**inputs):
    import concourse.bacc as bacc
    from concourse.bass_utils import run_bass_kernel_spmd

    nc = bacc.Bacc("TRN2", target_bir_lowering=False, num_devices=1)
    arrays = {f"in_{n}": v for n, v in laid_out({n: np.asarray(v) for n, v in inputs.items()}).items()}
    aps = {n[3:]: nc.dram_tensor(n, v.shape, mybir.dt.from_np(v.dtype), kind="ExternalInput").ap()
           for n, v in arrays.items()}
    out = nc.dram_tensor("out", (P, KD, T), F32, kind="ExternalOutput").ap()
    build(nc, aps, out)
    r = run_bass_kernel_spmd(nc, [arrays], core_ids=[0])
    got = r.results[0]["out"]
    return np.ascontiguousarray(got.transpose(2, 1, 0)).reshape(1, T, D)
```

```python
from contextlib import ExitStack

import numpy as np

import concourse.bass as bass
from concourse import mybir

P = 128
T = 1024
D = 1024
KD = D // P
HALF = 512
FF = 2816
NF = FF // P
HEAD_PAIRS = 4
BLK = 128
NBLK = T // BLK
CH = 64
NZR = 15
NZG = 13
DECAY = float(np.exp(-0.5))
LEVELS = [1, 2, 4, 8, 16, 32, 64]

F32 = mybir.dt.float32
F32R = mybir.dt.float32r
ALU = mybir.AluOpType
ACT = mybir.ActivationFunctionType
ds = bass.ds

VEC_FIELDS = [
    ("norm_mix_pre", 8), ("norm_mix_post", 8), ("norm_ffn_pre", 8), ("norm_ffn_post", 8), ("norm_ple", 8),
    ("mu", NZR), ("w0", 8), ("a0", 4), ("k_k", 4), ("k_a", 4), ("r_k", 4), ("ln_w", 4), ("ln_b", 4),
    ("conv", 24), ("a_b", 4), ("gla_norm", 1), ("ple_b", 8), ("c", 8), ("ada_b", 48), ("gains2", 32),
    ("conv2", 24),
]
VEC = {}
_at = 0
for _name, _n in VEC_FIELDS:
    VEC[_name] = _at
    _at += _n
NVEC = _at

CONST_FIELDS = [("ident", 1), ("ones", 1), ("head_ones", 1), ("eye64", 1), ("eps", 1), ("head_rows", 1), ("spread", 4),
                ("chunk_keep", 16), ("score_mask", 4), ("level1_t", 2), ("level1_m", 2), ("level_m", 5),
                ("block_keep", 16), ("gla_diag", 1), ("gla_level", 7)]
CONST = {}
_at = 0
for _name, _n in CONST_FIELDS:
    CONST[_name] = _at
    _at += _n
NCONST = _at
N_STAY = CONST["chunk_keep"]
EPS_RMS, EPS_GN, EPS_ZERO = 0, 1, 2


def constants():
    out = np.zeros((P, NCONST, P), np.float32)
    p, j = np.arange(P)[:, None], np.arange(P)[None, :]
    out[:, CONST["ident"]] = p == j
    out[:, CONST["ones"]] = 1
    out[:, CONST["head_ones"]] = p // 64 == j // 64
    out[:, CONST["eye64"]] = p % 64 == j % 64
    out[:, CONST["eps"], EPS_RMS] = 1e-6
    out[:, CONST["eps"], EPS_GN] = 64e-5
    for n in range(HEAD_PAIRS):
        out[:, CONST["head_rows"], 32 * n:32 * n + 32] = np.arange(32)[None] == 2 * n + p // 64
        out[:, CONST["spread"] + n] = -1.0 * (p == 2 * n + j // 64)
    t = np.arange(T)
    out[:, CONST["chunk_keep"]:CONST["chunk_keep"] + 8] = (t % CH != 0).reshape(8, P)[None]
    out[:, CONST["chunk_keep"] + 8:CONST["chunk_keep"] + 16] = (t % CH != CH - 1).reshape(8, P)[None]
    out[:, CONST["block_keep"]:CONST["block_keep"] + 8] = (t % BLK != 0).reshape(8, P)[None]
    out[:, CONST["block_keep"] + 8:CONST["block_keep"] + 16] = (t % BLK != BLK - 1).reshape(8, P)[None]
    same = p // CH == j // CH
    for d in range(2):
        before = (p < j) if d == 0 else (p > j)
        out[:, CONST["score_mask"] + 2 * d] = same & before
        out[:, CONST["score_mask"] + 2 * d + 1] = same & (before | (p == j))
        out[:, CONST["level1_t"] + d] = (p // 2 == j // 2) & before
        for n, s in enumerate(LEVELS[1:6]):
            col = np.arange(P).reshape(P // (2 * s), 2, s)[:, d].reshape(-1)
            out[:, CONST["level_m"] + n, d * CH:(d + 1) * CH] = (p // (2 * s) == col // (2 * s)) & (p // s != col // s)
        out[:, CONST["level1_m"] + d] = (p // 2 == j // 2) & ((p > j) if d == 0 else (p < j))
    for n, s in enumerate(LEVELS):
        out[:, CONST["gla_level"] + n] = (p // (2 * s) == j // (2 * s)) & (p // s != j // s)
    out[:, CONST["gla_diag"]] = 2.0 * (p == j)
    return out.reshape(P, NCONST * P)


class Core:

    def __init__(self, nc, ctx):
        self.nc, self.ctx, self.sems = nc, ctx, []

    def sem(self, name):
        self.sems.append(self.nc.alloc_semaphore(name=name))
        return self.sems[-1]

    def clear_sems(self):
        self.nc.clear_and_free_semaphores(self.sems)
        self.nc.all_engine_barrier()
        self.sems = []


def cst(core, name, n=0):
    a = CONST[name]
    return core.const[:, (a + n) * P:(a + n + 1) * P] if isinstance(n, int) else core.const[:, ds((n + a) * P, P)]


def head_rows(core, n):
    return cst(core, "head_rows")[:, 32 * n:32 * n + 32]


def head_spread(core, n):
    return cst(core, "spread", n)[0:32]


class Marks:

    def __init__(self, sem, names):
        self.sem, self.names, self.next = sem, names, 0

    def begin(self, engine):
        engine.sem_inc(self.sem, 1)

    def before(self, turn):
        return self.sem, turn * len(self.names) + 1

    def __call__(self, name):
        assert self.names[self.next % len(self.names)] == name, (name, self.names[self.next % len(self.names)])
        self.next += 1
        return self.sem, 1

    def by(self, name, turn=0):
        return self.sem, turn * len(self.names) + (self.names.index(name) + 2)


def eps(core, which):
    a = CONST["eps"] * P + which
    return core.const[:, a:a + 1]


def vec(core, name, n=0):
    return core.vec[:, ds(VEC[name] + n, 1)] if not isinstance(n, int) else core.vec[:, VEC[name] + n:VEC[name] + n + 1]


def tile_of(buf, n):
    if isinstance(n, int):
        return buf[:, n, :]
    return buf[:, ds(n, 1), :].rearrange("p a t -> p (a t)")


def walk(e, segments, unroll, body):
    total = segments[-1][1]
    for a, b, kind in segments:
        m = a
        while m < min(b, unroll if a == 0 else a):
            body(m, m % 6, m // 3 if kind == "third" else kind)
            m += 1
        last = b - 1 if b == total else b
        turns = max(0, (last - m) // unroll)
        if turns > 1:
            with e.Fori(0, turns) as i:
                for u in range(unroll):
                    body(i * unroll + (m + u), (m + u) % 6 if unroll == 6 else (m + u) % 2,
                         i * 2 + (m + u) // 3 if kind == "third" else kind)
            m += turns * unroll
        while m < b:
            body(m, m % 6, m // 3 if kind == "third" else kind)
            m += 1


class Ahead:

    def __init__(self, tiles):
        self.tiles = tiles

    def load(self, sp):
        for src, raw, hi, lo, loaded, hi_ready, lo_ready in self.tiles:
            sp.dma_start(raw, src).then_inc(loaded, 16)

    def hi(self, act):
        for src, raw, hi, lo, loaded, hi_ready, lo_ready in self.tiles:
            act.wait_ge(loaded, 16)
            act.copy(hi, raw).then_inc(hi_ready, 1)

    def lo(self, dve):
        for src, raw, hi, lo, loaded, hi_ready, lo_ready in self.tiles:
            dve.wait_ge(hi_ready, 1)
            dve.tensor_tensor(lo, raw, hi.bitcast(F32), ALU.subtract).then_inc(lo_ready, 1)


class DenseWeights:

    def __init__(self, core, ctx, name, weights):
        self.weights, self.kt = weights, weights.shape[2] // P
        self.raw = ctx.enter_context(core.nc.sbuf_tensor(f"{name}_raw", [P, 2, self.kt, P], F32))
        self.hi = ctx.enter_context(core.nc.sbuf_tensor(f"{name}_whi", [P, 2, self.kt, P], F32R))
        self.lo = ctx.enter_context(core.nc.sbuf_tensor(f"{name}_wlo", [P, 2, self.kt, P], F32R))
        self.loaded = [core.sem(f"{name}_loaded{s}") for s in range(2)]
        self.hi_ready, self.lo_ready = core.sem(f"{name}_hi_ready"), core.sem(f"{name}_lo_ready")

        def flat(x):
            return x[:, 0].rearrange("p k c -> p (k c)")
        self.ahead = Ahead([(weights[0], flat(self.raw), flat(self.hi), flat(self.lo), self.loaded[0],
                             self.hi_ready, self.lo_ready)])


def dense(core, name, w, act_hi, act_lo, segments, act_epilogue, dve_epilogue=None, pool_epilogue=None,
          unroll=2, act_first=None, dve_first=None, pool_first=None, load=None):
    nc = core.nc
    total = segments[-1][1]
    weights, kt = w.weights, w.kt
    raw, w_hi, w_lo, loaded, hi_ready, lo_ready = w.raw, w.hi, w.lo, w.loaded, w.hi_ready, w.lo_ready
    with ExitStack() as ctx:
        acc = ctx.enter_context(nc.psum_tensor(f"{name}_acc", [P, 2, T], F32))
        filled, drained, other_loaded = (core.sem(f"{name}_{x}") for x in ("filled", "drained", "other_loaded"))
        block = ctx.enter_context(nc.Block())

        @block.sync
        def _(sp):
            def load_weights(m, r, kind):
                if not (isinstance(m, int) and m < 2):
                    sp.wait_ge(lo_ready, m - 1)
                src = weights[m] if isinstance(m, int) else weights[ds(m, 1)].rearrange("a p k -> (a p) k")
                sp.dma_start(raw[:, r % 2].rearrange("p k c -> p (k c)"), src).then_inc(loaded[r % 2], 16)
            load_weights(1, 1, None)
            if load is not None:
                sp.dma_start(*load).then_inc(other_loaded, 16)
            walk(sp, [(2, total, None)], 2, load_weights)
            if load is not None:
                sp.wait_ge(other_loaded, 16)

        @block.scalar
        def _(act):
            if act_first:
                act_first(act)

            def split_hi(m, slot, first):
                act.wait_ge(loaded[slot], (m - slot) * 8 + 16)
                if not first:
                    act.wait_ge(filled, m - 1)
                act.copy(w_hi[:, slot], raw[:, slot]).then_inc(hi_ready, 1)

            def body(m, r, kind):
                if not (isinstance(m, int) and m + 1 >= total):
                    split_hi(m + 1, (r + 1) % 2, isinstance(m, int) and m == 0)
                act_epilogue(act, m, r, kind, acc[:, r % 2], filled, drained)
            walk(act, segments, unroll, body)

        @block.vector
        def _(dve):
            if dve_first:
                dve_first(dve)

            def split_lo(m, slot):
                dve.wait_ge(hi_ready, m + 1)
                dve.tensor_tensor(w_lo[:, slot], raw[:, slot], w_hi[:, slot].bitcast(F32),
                                  ALU.subtract).then_inc(lo_ready, 1)

            def body(m, r, kind):
                if not (isinstance(m, int) and m + 1 >= total):
                    split_lo(m + 1, (r + 1) % 2)
                if dve_epilogue:
                    dve_epilogue(dve, m, r, kind, drained)
            walk(dve, segments, unroll, body)

        @block.gpsimd
        def _(pool):
            if pool_first:
                pool_first(pool)
            if pool_epilogue:
                walk(pool, segments, unroll, lambda m, r, kind: pool_epilogue(pool, m, r, kind, drained))

        @block.tensor
        def _(pe):
            def body(m, r, kind):
                slot = r % 2
                pe.wait_ge(lo_ready, m + 1)
                if not (isinstance(m, int) and m < 2):
                    pe.wait_ge(drained, m - 1)
                for k in range(kt):
                    for part, x in ((w_hi, act_hi), (w_hi, act_lo), (w_lo, act_hi)):
                        for h in range(2):
                            mm = pe.matmul(acc[:, slot, h * HALF:(h + 1) * HALF], part[:, slot, k],
                                           x[:, k, h * HALF:(h + 1) * HALF],
                                           start=(k == 0 and part is w_hi and x is act_hi),
                                           stop=(k == kt - 1 and part is w_lo))
                mm.then_inc(filled, 1)
            walk(pe, segments, unroll, body)


def joint(core, name, y, y_gain, h, gain, shift, hi, lo, store=None, load=None, ahead=None,
          source=None):
    nc = core.nc
    groups = [("y", hf) for hf in range(2)] if y is not None else []
    groups += [("h", hf) for hf in range(2)] if hi is not None and gain is not None else []
    n_blocks, slots = HALF // P, 4
    with ExitStack() as ctx:
        sq = ctx.enter_context(nc.sbuf_tensor(f"{name}_sq", [P, slots, HALF], F32))
        tmp = ctx.enter_context(nc.sbuf_tensor(f"{name}_tmp", [P, slots, HALF], F32))
        root = ctx.enter_context(nc.sbuf_tensor(f"{name}_root", [P, len(groups), n_blocks], F32))
        sums = ctx.enter_context(nc.psum_tensor(f"{name}_sums", [P, len(groups), HALF], F32))
        rs = ctx.enter_context(nc.psum_tensor(f"{name}_rs", [P, len(groups), HALF], F32))
        sq_ready, sq_used, root_ready, recip, spread, scaled, normed, hi_done, stored = (
            core.sem(f"{name}_{x}") for x in ("sq_ready", "sq_used", "root_ready", "recip", "spread", "scaled",
                                              "normed", "hi_done", "stored"))
        loaded = core.sem(f"{name}_loaded")
        h_loaded = [core.sem(f"{name}_h_loaded{hf}") for hf in range(2)]
        h_ready = [core.sem(f"{name}_h_even"), core.sem(f"{name}_h_odd")]
        lo_done = [core.sem(f"{name}_lo_even"), core.sem(f"{name}_lo_odd")]
        block = ctx.enter_context(nc.Block())
        pool_lo = shift is None

        def cols(hf):
            return slice(hf * HALF, (hf + 1) * HALF)

        def wait_h(e, hf, m):
            if y is not None:
                e.wait_ge(h_ready[m % 2], hf * (KD // 2) + m // 2 + 1)

        def normed_tile(hf, m):
            return tmp[:, m % slots] if gain is not None else h[:, m, cols(hf)]

        def low_part(e, hf, m):
            e.wait_ge(hi_done, hf * KD + m + 1)
            hi_m = hi[:, m, cols(hf)].bitcast(F32)
            if shift is None:
                ins = e.tensor_tensor(lo[:, m, cols(hf)], normed_tile(hf, m), hi_m, ALU.subtract)
            else:
                ins = e.scalar_tensor_tensor(lo[:, m, cols(hf)], normed_tile(hf, m), shift[:, m:m + 1], hi_m,
                                             ALU.add, ALU.subtract)
            ins.then_inc(lo_done[m % 2 if pool_lo else 0], 1)

        @block.scalar
        def _(act):
            count = 0
            for n, (stage, hf) in enumerate(groups):
                if source is not None:
                    act.wait_ge(h_loaded[hf], 16)
                for m in range(KD):
                    if count >= slots:
                        act.wait_ge(sq_used, count - slots + 1)
                    if stage == "h":
                        wait_h(act, hf, m)
                    src = y if stage == "y" else h
                    act.activation(sq[:, count % slots], src[:, m, cols(hf)], ACT.Square).then_inc(sq_ready, 1)
                    count += 1
                act.wait_ge(sq_used, count)
                act.activation(root[:, n], sums[:, n, ::P], ACT.Sqrt, bias=eps(core, EPS_RMS), scale=1.0 / D
                               ).then_inc(root_ready, 1)
                if n == 0 and ahead is not None:
                    ahead.hi(act)
            if hi is not None:
                for hf in range(2):
                    for m in range(KD):
                        if gain is not None:
                            act.wait_ge(normed, hf * KD + m + 1)
                        else:
                            wait_h(act, hf, m)
                        act.activation(hi[:, m, cols(hf)], normed_tile(hf, m), ACT.Identity,
                                       bias=shift[:, m:m + 1] if shift is not None else 0.0).then_inc(hi_done, 1)

        @block.tensor
        def _(pe):
            count = 0
            for n in range(len(groups)):
                for m in range(KD):
                    pe.wait_ge(sq_ready, count + 1)
                    for b in range(n_blocks):
                        mm = pe.matmul(sums[:, n, b * P:(b + 1) * P], sq[:, count % slots, b * P:(b + 1) * P],
                                       cst(core, "ones"), start=(m == 0 and b == 0),
                                       stop=(m == KD - 1 and b == n_blocks - 1))
                    mm.then_inc(sq_used, 1)
                    count += 1
                pe.wait_ge(recip, n + 1)
                for b in range(n_blocks):
                    mm = pe.matmul(rs[:, n, b * P:(b + 1) * P], root[:, n, b:b + 1].to_broadcast([P, P]),
                                   cst(core, "ident"), start=True, stop=True)
                mm.then_inc(spread, 1)

        @block.vector
        def _(dve):
            def reciprocal(n):
                if n < len(groups):
                    dve.wait_ge(root_ready, n + 1)
                    dve.reciprocal(root[:, n], root[:, n]).then_inc(recip, 1)

            reciprocal(0)
            if ahead is not None:
                ahead.lo(dve)
            for n, (stage, hf) in enumerate(groups):
                dve.wait_ge(spread, n + 1)
                for m in range(KD):
                    if m == KD // 2:
                        reciprocal(n + 1)
                    if stage == "y":
                        dve.scalar_tensor_tensor(y[:, m, cols(hf)], y[:, m, cols(hf)], y_gain[:, m:m + 1], rs[:, n],
                                                 ALU.mult, ALU.mult).then_inc(scaled, 1)
                        if m % 2 == 0:
                            dve.wait_ge(scaled, hf * KD + m + 1)
                            dve.tensor_tensor(h[:, m, cols(hf)], h[:, m, cols(hf)], y[:, m, cols(hf)],
                                              ALU.add).then_inc(h_ready[0], 1)
                        continue
                    tile = hf * KD + m
                    if tile >= slots:
                        if pool_lo:
                            dve.wait_ge(lo_done[m % 2], (tile - slots) // 2 + 1)
                        else:
                            dve.wait_ge(lo_done[0], tile - slots + 1)
                    wait_h(dve, hf, m)
                    dve.scalar_tensor_tensor(tmp[:, m % slots], h[:, m, cols(hf)], gain[:, m:m + 1], rs[:, n],
                                             ALU.mult, ALU.mult).then_inc(normed, 1)
                    if m >= 1 and (m % 2 == 1 or not pool_lo):
                        low_part(dve, hf, m - 1)
                if stage == "h" and not pool_lo:
                    low_part(dve, hf, KD - 1)
            if hi is not None and gain is None:
                for hf in range(2):
                    for m in range(0, KD, 2):
                        low_part(dve, hf, m)

        @block.gpsimd
        def _(pool):
            if y is not None:
                for hf in range(2):
                    for m in range(1, KD, 2):
                        pool.wait_ge(scaled, hf * KD + m + 1)
                        pool.tensor_tensor(h[:, m, cols(hf)], h[:, m, cols(hf)], y[:, m, cols(hf)],
                                           ALU.add).then_inc(h_ready[1], 1)
            if hi is not None and pool_lo:
                for hf in range(2):
                    for m in range(1, KD, 2):
                        low_part(pool, hf, m)

        @block.sync
        def _(sp):
            if source is not None:
                for hf in range(2):
                    sp.dma_start(h[:, :, cols(hf)], source[:, :, cols(hf)]).then_inc(h_loaded[hf], 16)
            if ahead is not None:
                ahead.load(sp)
            if load is not None:
                sp.dma_start(*load).then_inc(loaded, 16)
                sp.wait_ge(loaded, 16)
            if store is not None:
                for hf in range(2):
                    for half_tiles in h_ready:
                        sp.wait_ge(half_tiles, (hf + 1) * KD // 2)
                    sp.dma_start(store[:, :, cols(hf)], h[:, :, cols(hf)]).then_inc(stored, 16)
                sp.wait_ge(stored, 32)


def gla_project(core, w, xn_hi, xn_lo, z, lora):
    nc = core.nc
    with ExitStack() as ctx:
        edge = ctx.enter_context(nc.sbuf_tensor("gp_edge", [P, 2, T + 2], F32))
        mix = ctx.enter_context(nc.sbuf_tensor("gp_mix", [P, T], F32))
        edged, raw_z, part, mixed, used = (core.sem(f"gp_{x}") for x in ("edged", "raw_z", "part", "mixed", "used"))
        segments = [(0, 8, "conv"), (8, 12, "gate"), (12, 13, "lora")]

        def dve_first(dve):
            dve.memset(edge[:, :, :], 0.0).then_inc(edged, 1)

        def act_first(act):
            act.wait_ge(edged, 1)

        def act_epilogue(act, m, r, kind, psum, filled, drained):
            act.wait_ge(filled, m + 1)
            if kind == "conv":
                act.copy(edge[:, r % 2, 1:T + 1], psum).then_inc(drained, 1)
                act.wait_ge(drained, m + 1)
                act.wait_ge(mixed, m + 1)
                act.activation(tile_of(z, m), mix[:, :], ACT.Silu).then_inc(used, 1)
            elif kind == "gate":
                act.activation(tile_of(z, m), psum, ACT.Silu).then_inc(drained, 1)
            else:
                act.copy(lora, psum).then_inc(drained, 1)

        def dve_epilogue(dve, m, r, kind, drained):
            if kind != "conv":
                return
            x = edge[:, r % 2]
            dve.wait_ge(drained, m + 1)
            if not (isinstance(m, int) and m == 0):
                dve.wait_ge(used, m)
            taps = [vec(core, "conv", t * 8 + m) for t in range(3)]
            dve.tensor_scalar(mix[:, :], x[:, 0:T], taps[0], None, ALU.mult).then_inc(part, 1)
            dve.wait_ge(part, m * 2 + 1)
            dve.scalar_tensor_tensor(mix[:, :], x[:, 1:T + 1], taps[1], mix[:, :], ALU.mult,
                                     ALU.add).then_inc(part, 1)
            dve.wait_ge(part, m * 2 + 2)
            dve.scalar_tensor_tensor(mix[:, :], x[:, 2:T + 2], taps[2], mix[:, :], ALU.mult,
                                     ALU.add).then_inc(mixed, 1)

        dense(core, "gp", w, xn_hi, xn_lo, segments, act_epilogue, dve_epilogue, act_first=act_first,
              dve_first=dve_first)


def gla_decay(core, dram_const, dram_a_up, lora, sums):
    nc = core.nc
    with ExitStack() as ctx:
        a_up = ctx.enter_context(nc.sbuf_tensor("gd_aup", [P, 2 * P], F32))
        keep = ctx.enter_context(nc.sbuf_tensor("gd_keep", [P, 2, T], F32))
        away = ctx.enter_context(nc.sbuf_tensor("gd_away", [P, T], F32))
        low = ctx.enter_context(nc.sbuf_tensor("gd_low", [P, 2, T], F32))
        gate = ctx.enter_context(nc.psum_tensor("gd_gate", [P, 4, T], F32))
        loaded, products, act_did, dve_did = (core.sem(f"gd_{x}") for x in ("loaded", "products", "act", "dve"))
        cases = [(d, i) for d in range(2) for i in range(2)]
        act_made = Marks(act_did, ["abs", "exp", "ln"])
        dve_made = Marks(dve_did, ["min", "log_sigmoid", "scan"])
        block = ctx.enter_context(nc.Block())

        @block.sync
        def _(sp):
            sp.dma_start(a_up[:, :], dram_a_up).then_inc(loaded, 16)
            c = CONST["block_keep"] * P
            sp.dma_start(keep[:, :, :].rearrange("p d t -> p (d t)"), dram_const[:, c:c + 2 * T]).then_inc(loaded, 16)

        @block.tensor
        def _(pe):
            pe.wait_ge(loaded, 32)
            for n, (d, i) in enumerate(cases):
                rows = slice(32 * d, 32 * d + 16)
                for h in range(2):
                    mm = pe.matmul(gate[:, n, h * HALF:(h + 1) * HALF], a_up[rows, i * P:(i + 1) * P],
                                   lora[rows, h * HALF:(h + 1) * HALF], start=True, stop=True)
                mm.then_inc(products, 1)

        @block.scalar
        def _(act):
            act_made.begin(act)
            for n, (d, i) in enumerate(cases):
                act.wait_ge(products, n + 1)
                if n:
                    act.wait_ge(*dve_made.by("log_sigmoid", n - 1))
                act.activation(away[:, :], gate[:, n], ACT.Abs, bias=vec(core, "a_b", n)).then_inc(*act_made("abs"))
                act.wait_ge(*act_made.by("abs", n))
                act.activation(away[:, :], away[:, :], ACT.Exp, scale=-1.0).then_inc(*act_made("exp"))
                act.wait_ge(*act_made.by("exp", n))
                act.activation(away[:, :], away[:, :], ACT.Ln, bias=1.0).then_inc(*act_made("ln"))

        @block.vector
        def _(dve):
            dve_made.begin(dve)
            dve.wait_ge(loaded, 32)
            for n, (d, i) in enumerate(cases):
                ls = low[:, n % 2]
                dve.wait_ge(*act_made.by("abs", n))
                dve.tensor_scalar(ls, gate[:, n], vec(core, "a_b", n), 0.0, ALU.add,
                                  ALU.min).then_inc(*dve_made("min"))
                dve.wait_ge(*dve_made.by("min", n))
                dve.wait_ge(*act_made.by("ln", n))
                dve.tensor_tensor(ls, ls, away[:, :], ALU.subtract).then_inc(*dve_made("log_sigmoid"))
                dve.wait_ge(*dve_made.by("log_sigmoid", n))
                out = sums[:, d, i]
                if d == 0:
                    dve.tensor_tensor_scan(out, keep[:, 0], ls, 0.0, ALU.mult, ALU.add).then_inc(*dve_made("scan"))
                else:
                    dve.tensor_tensor_scan(out[:, ::-1], keep[:, 1, ::-1], ls[:, ::-1], 0.0, ALU.mult,
                                           ALU.add).then_inc(*dve_made("scan"))


def gla_mix(core, dram_const, z, sums, y, room):
    nc = core.nc
    levels = range(7)
    scored = ["diag"] + [f"level{n}" for n in levels]
    with ExitStack() as ctx:
        def sb(name, shape):
            return ctx.enter_context(nc.sbuf_tensor(f"gm_{name}", shape, F32))

        def psum(name, shape):
            return ctx.enter_context(nc.psum_tensor(f"gm_ps_{name}", shape, F32))
        used = [0]

        def both(name, tiles, a=1):
            at = used[0]
            used[0] += tiles * BLK
            own = sb(name, [P, tiles * BLK])[:, :]
            views = (own, room[:, at:at + tiles * BLK])
            if a == 1:
                return [x.rearrange("p (i t) -> p i t", t=BLK) for x in views]
            return [x.rearrange("p (a i t) -> p a i t", a=a, t=BLK) for x in views]

        mask = sb("mask", [P, 8, BLK])
        summed = sb("summed", [P, 2, 2, BLK])
        summed_d = both("summed_d", 2)
        qk = both("qk", 4, 2)
        v = both("v", 4)
        diff_s = both("diff_s", 4, 2)
        grown_s = both("grown_s", 4, 2)
        qk_s = both("qk_s", 4, 2)
        v_tok = both("v_tok", 4)
        k_tok = both("k_tok", 2)
        state = both("state", 2)
        diff = sb("diff", [P, 2, 2, 2, BLK])
        grown = sb("grown", [P, 2, 2, 2, BLK])
        qk_l = sb("qk_l", [P, 2, 2, 2, BLK])
        part = sb("part", [P, 2, 4, BLK])
        score = sb("score", [P, 4, BLK])
        ps_score = psum("score", [P, 2, 2, 512])
        ps_v = psum("v", [P, 4, BLK])
        ps_k = psum("k", [P, 4, BLK])
        ps_o = psum("o", [P, 2, 512])
        loaded, zeroed, y_zeroed = core.sem("gm_loaded"), core.sem("gm_zeroed"), core.sem("gm_y_zeroed")

        def state_steps(d):
            return [f"state0_{d}", f"state1_{d}"]

        def y_steps(d):
            return [f"y0_{d}", f"y1_{d}"]
        dve_steps = ["q_0", "block_sums", "summed_0", "diff_s_0", "q_1", "summed_1", "diff_s_1", "diff_level0"]
        dve_steps += ["qk_s_0", "qk_s_1"]
        for n in levels:
            dve_steps += ([f"diff_level{n + 1}"] if n < 6 else []) + [f"qk_level{n}", f"part_{scored[n]}"]
            dve_steps += {2: state_steps(1) + y_steps(1), 5: state_steps(0)}.get(n, [])
        dve_steps += ["part_level6"] + y_steps(0)
        act_steps = ["k_0", "v_0", "k_1", "v_1", "exp_s_0", "exp_s_1", "exp_level0", "v_tok_0", "k_tok_0", "exp_level1",
                     "v_tok_1", "k_tok_1"] + [f"exp_level{n}" for n in levels[2:]]
        pe_steps = ["v_tok_0", "k_tok_0", "score_diag", "v_tok_1", "k_tok_1", "score_level0", "score_level1", "out_1",
                    "gain_1"] + [f"score_level{n}" for n in (2, 3, 4)] + ["gain_0", "score_level5", "score_level6", "out_0"]
        dve_made = Marks(core.sem("gm_dve"), dve_steps)
        act_made = Marks(core.sem("gm_act"), act_steps)
        pool_made = Marks(core.sem("gm_pool"), [f"sum_{r}" for r in scored[1:]])
        pe_made = Marks(core.sem("gm_pe"), pe_steps)
        block = ctx.enter_context(nc.Block())

        def tokens(d, j):
            return ds(j * BLK if d == 0 else (NBLK - 1) * BLK - j * BLK, BLK)

        @block.sync
        def _(sp):
            c = CONST["gla_diag"] * P
            sp.dma_start(mask[:, :, :].rearrange("p a t -> p (a t)"), dram_const[:, c:c + 8 * P]).then_inc(loaded, 16)

        @block.scalar
        def _(act):
            act_made.begin(act)

            def level_exp(j, n):
                act.wait_ge(*dve_made.by(f"diff_level{n}", j))
                if n >= 2:
                    act.wait_ge(*dve_made.by(f"qk_level{n - 2}", j))
                act.activation(grown[:, n % 2], diff[:, n % 2], ACT.Exp, scale=1 / 16).then_inc(*act_made(f"exp_level{n}"))

            with act.Fori(0, NBLK) as j:
                act.wait_ge(*pe_made.before(j))
                act.wait_ge(*dve_made.before(j))
                for d in range(2):
                    act.copy(qk[d][:, 1], z[:, 2:4, tokens(d, j)]).then_inc(*act_made(f"k_{d}"))
                    act.copy(v[d], z[:, 4:8, tokens(d, j)]).then_inc(*act_made(f"v_{d}"))
                for d in range(2):
                    act.wait_ge(*dve_made.by(f"diff_s_{d}", j))
                    act.activation(grown_s[d], diff_s[d], ACT.Exp, scale=1 / 16).then_inc(*act_made(f"exp_s_{d}"))
                for d in range(2):
                    level_exp(j, d)
                    act.wait_ge(*pe_made.by(f"v_tok_{d}", j))
                    act.copy(v_tok[d], ps_v[:, :, :]).then_inc(*act_made(f"v_tok_{d}"))
                    act.wait_ge(*pe_made.by(f"k_tok_{d}", j))
                    act.copy(k_tok[d], ps_k[:, 0:2]).then_inc(*act_made(f"k_tok_{d}"))
                for n in levels[2:]:
                    level_exp(j, n)

        @block.gpsimd
        def _(pool):
            pool_made.begin(pool)
            pool.memset(y, 0.0).then_inc(y_zeroed, 1)
            with pool.Fori(0, NBLK) as j:
                for n, r in enumerate(scored[1:], 1):
                    pool.wait_ge(*dve_made.by(f"part_{r}", j))
                    if n == 1:
                        pool.wait_ge(*pe_made.before(j))
                        pool.tensor_tensor(score[:, :, :], part[:, 0], part[:, 1],
                                           ALU.add).then_inc(*pool_made(f"sum_{r}"))
                    else:
                        pool.wait_ge(*pool_made.by(f"sum_{scored[n - 1]}", j))
                        pool.tensor_tensor(score[:, :, :], score[:, :, :], part[:, n % 2],
                                           ALU.add).then_inc(*pool_made(f"sum_{r}"))

        @block.tensor
        def _(pe):
            pe_made.begin(pe)
            pe.wait_ge(zeroed, 2)

            def transposes(j, d):
                pe.wait_ge(*act_made.by(f"v_{d}", j))
                if d == 1:
                    pe.wait_ge(*act_made.by("k_tok_0", j))
                for i in range(4):
                    mm = pe.transpose(ps_v[:, i], v[d][:, i], cst(core, "ident"))
                mm.then_inc(*pe_made(f"v_tok_{d}"))
                pe.wait_ge(*dve_made.by(f"qk_s_{d}", j))
                for i in range(2):
                    mm = pe.transpose(ps_k[:, i], qk_s[d][:, 1, i], cst(core, "ident"))
                mm.then_inc(*pe_made(f"k_tok_{d}"))

            def scores(j, n):
                r = scored[n]
                if r == "diag":
                    src = qk[0]
                else:
                    pe.wait_ge(*dve_made.by(f"qk_{r}", j))
                    src = qk_l[:, (n - 1) % 2]
                if n >= 2:
                    pe.wait_ge(*dve_made.by(f"part_{scored[n - 2]}", j))
                for par in range(2):
                    rows = slice(64 * par, 64 * par + 64)
                    for i in range(2):
                        mm = pe.matmul(ps_score[:, n % 2, par, i * BLK:(i + 1) * BLK], src[rows, 1, i],
                                       src[rows, 0, i], start=True, stop=True)
                mm.then_inc(*pe_made(f"score_{r}"))

            def outputs_of_block(j):
                pe.wait_ge(*pool_made.by(f"sum_{scored[-1]}", j))
                for par in range(2):
                    for i in range(2):
                        mm = pe.matmul(ps_o[:, par, i * BLK:(i + 1) * BLK], v_tok[0][:, 2 * i + par],
                                       score[:, 2 * par + i], start=False, stop=(i == 1))
                mm.then_inc(*pe_made("out_0"))

            def outputs_of_state(j, d):
                pe.wait_ge(*act_made.by(f"k_tok_{d}", j))
                if d == 0:
                    pe.wait_ge(*dve_made.by("y1_1", j))
                else:
                    pe.wait_ge(*dve_made.before(j))
                for par in range(2):
                    rows = slice(64 * par, 64 * par + 64)
                    for i in range(2):
                        mm = pe.matmul(ps_o[:, par, i * BLK:(i + 1) * BLK], state[d][rows, i], qk_s[d][rows, 0, i],
                                       start=(i == 0), stop=(d == 1 and i == 1))
                if d == 1:
                    mm.then_inc(*pe_made("out_1"))
                for par in range(2):
                    for i in range(2):
                        mm = pe.matmul(ps_k[64 * par:64 * par + 64, 2 + i], k_tok[d][:, i, 64 * par:64 * par + 64],
                                       v_tok[d][:, 2 * i + par], start=True, stop=True)
                mm.then_inc(*pe_made(f"gain_{d}"))

            with pe.Fori(0, NBLK) as j:
                transposes(j, 0)
                scores(j, 0)
                transposes(j, 1)
                scores(j, 1)
                scores(j, 2)
                outputs_of_state(j, 1)
                for n in range(3, 8):
                    scores(j, n)
                    if n == 5:
                        outputs_of_state(j, 0)
                outputs_of_block(j)

        @block.vector
        def _(dve):
            dve_made.begin(dve)
            for d in range(2):
                dve.memset(state[d], 0.0).then_inc(zeroed, 1)
            dve.wait_ge(zeroed, 2)
            dve.wait_ge(loaded, 16)
            dve.wait_ge(y_zeroed, 1)

            def halves(x, s):
                return x.rearrange("p i (n o r) -> p (i n) o r", o=2, r=s)

            def level_diff(j, n):
                s = LEVELS[n]
                fwd, bwd = halves(summed[:, 0], s), halves(summed[:, 1], s)
                q_out, k_out = halves(diff[:, n % 2, 0], s), halves(diff[:, n % 2, 1], s)
                pairs = 2 * BLK // (2 * s)
                end = fwd[:, :, 0, s - 1:s].to_broadcast([P, pairs, s])
                start = bwd[:, :, 1, 0:1].to_broadcast([P, pairs, s])
                if n >= 2:
                    dve.wait_ge(*act_made.by(f"exp_level{n - 2}", j))
                dve.tensor_tensor(q_out[:, :, 0, :], bwd[:, :, 0, :], start, ALU.subtract)
                dve.tensor_tensor(q_out[:, :, 1, :], fwd[:, :, 1, :], end, ALU.subtract)
                dve.tensor_tensor(k_out[:, :, 0, :], end, fwd[:, :, 0, :], ALU.subtract)
                dve.tensor_tensor(k_out[:, :, 1, :], start, bwd[:, :, 1, :],
                                  ALU.subtract).then_inc(*dve_made(f"diff_level{n}"))

            def masked(j, n):
                r = scored[n]
                dve.wait_ge(*pe_made.by(f"score_{r}", j))
                if n >= 2:
                    dve.wait_ge(*pool_made.by(f"sum_{scored[max(n - 2, 1)]}", j))
                out = part[:, n % 2].rearrange("p (a i) t -> p a (i t)", a=2)
                dve.tensor_tensor(out.rearrange("p a (i t) -> p a i t", i=2),
                                  ps_score[:, n % 2, :, 0:2 * BLK].rearrange("p a (i t) -> p a i t", i=2),
                                  mask[:, n, :].rearrange("p (a i t) -> p a i t", a=1, i=1).to_broadcast([P, 2, 2, BLK]),
                                  ALU.mult).then_inc(*dve_made(f"part_{r}"))

            def next_state(j, d):
                dve.wait_ge(*pe_made.by(f"gain_{d}", j))
                last = BLK - 1 if d == 0 else 0
                for i in range(2):
                    dve.scalar_tensor_tensor(state[d][:, i], state[d][:, i], grown_s[d][:, 0, i, last:last + 1],
                                             ps_k[:, 2 + i], ALU.mult, ALU.add).then_inc(*dve_made(f"state{i}_{d}"))
            def add_outputs(j, d):
                dve.wait_ge(*pe_made.by(f"out_{d}", j))
                for par in range(2):
                    out = y[:, par:par + 3:2, tokens(d, j)]
                    dve.tensor_tensor(out, out, ps_o[:, par, 0:2 * BLK].rearrange("p (i t) -> p i t", i=2),
                                      ALU.add).then_inc(*dve_made(f"y{par}_{d}"))

            with dve.Fori(0, NBLK) as j:
                dve.wait_ge(*dve_made.before(j))
                dve.wait_ge(*pe_made.before(j))
                for d in range(2):
                    dve.tensor_scalar(qk[d][:, 0], z[:, 0:2, tokens(d, j)], 0.125, None, ALU.mult
                                      ).then_inc(*dve_made(f"q_{d}"))
                    if d == 0:
                        dve.tensor_copy(summed[:, :, :, :], sums[:, :, :, tokens(0, j)]
                                        ).then_inc(*dve_made("block_sums"))
                    dve.tensor_copy(summed_d[d], sums[:, d, :, tokens(d, j)]).then_inc(*dve_made(f"summed_{d}"))
                    dve.wait_ge(*dve_made.by(f"summed_{d}", j))
                    last = BLK - 1 if d == 0 else 0
                    dve.tensor_copy(diff_s[d][:, 0], summed_d[d])
                    dve.tensor_tensor(diff_s[d][:, 1], summed_d[d][:, :, last:last + 1].to_broadcast([P, 2, BLK]),
                                      summed_d[d], ALU.subtract).then_inc(*dve_made(f"diff_s_{d}"))
                level_diff(j, 0)
                for d in range(2):
                    dve.wait_ge(*act_made.by(f"exp_s_{d}", j))
                    dve.tensor_tensor(qk_s[d], qk[d], grown_s[d], ALU.mult).then_inc(*dve_made(f"qk_s_{d}"))
                for n in levels:
                    if n < 6:
                        level_diff(j, n + 1)
                    dve.wait_ge(*act_made.by(f"exp_level{n}", j))
                    if n >= 2:
                        dve.wait_ge(*pe_made.by(f"score_level{n - 2}", j))
                    dve.tensor_tensor(qk_l[:, n % 2], qk[0], grown[:, n % 2],
                                      ALU.mult).then_inc(*dve_made(f"qk_level{n}"))
                    masked(j, n)
                    if n == 2:
                        next_state(j, 1)
                        add_outputs(j, 1)
                    if n == 5:
                        next_state(j, 0)
                masked(j, 7)
                add_outputs(j, 0)


def gla_finish(core, z, y, ahead):
    nc = core.nc
    n_blocks = T // P
    with ExitStack() as ctx:
        sq = ctx.enter_context(nc.sbuf_tensor("gf_sq", [P, 2, T], F32))
        root = ctx.enter_context(nc.sbuf_tensor("gf_root", [P, 4, n_blocks], F32))
        sums = ctx.enter_context(nc.psum_tensor("gf_sums", [P, 2, T], F32))
        rs = ctx.enter_context(nc.psum_tensor("gf_rs", [P, 2, T], F32))
        squared, summed, rooted, recip, spread, scaled, gated = (
            core.sem(f"gf_{x}") for x in ("squared", "summed", "rooted", "recip", "spread", "scaled", "gated"))
        block = ctx.enter_context(nc.Block())

        @block.sync
        def _(sp):
            ahead.load(sp)

        @block.scalar
        def _(act):
            def make_root(m):
                act.wait_ge(summed, m + 1)
                act.activation(root[:, m], sums[:, m % 2, ::P], ACT.Sqrt, bias=eps(core, EPS_RMS),
                               scale=1.0 / P).then_inc(rooted, 1)
            for m in range(4):
                if m >= 2:
                    act.wait_ge(summed, m - 1)
                act.activation(sq[:, m % 2], y[:, m], ACT.Square).then_inc(squared, 1)
                if m >= 1:
                    make_root(m - 1)
            make_root(3)
            ahead.hi(act)

        @block.tensor
        def _(pe):
            def spread_root(m):
                pe.wait_ge(recip, m + 1)
                if m >= 2:
                    pe.wait_ge(scaled, m - 1)
                for b in range(n_blocks):
                    mm = pe.matmul(rs[:, m % 2, b * P:(b + 1) * P], root[:, m, b:b + 1].to_broadcast([P, P]),
                                   cst(core, "ident"), start=True, stop=True)
                mm.then_inc(spread, 1)
            for m in range(4):
                pe.wait_ge(squared, m + 1)
                if m >= 2:
                    pe.wait_ge(rooted, m - 1)
                for b in range(n_blocks):
                    mm = pe.matmul(sums[:, m % 2, b * P:(b + 1) * P], sq[:, m % 2, b * P:(b + 1) * P],
                                   cst(core, "ones"), start=True, stop=True)
                mm.then_inc(summed, 1)
                if m >= 1:
                    spread_root(m - 1)
            spread_root(3)

        @block.vector
        def _(dve):
            def reciprocal(m):
                dve.wait_ge(rooted, m + 1)
                dve.reciprocal(root[:, m], root[:, m]).then_inc(recip, 1)
            reciprocal(0)
            for m in range(4):
                if m < 3:
                    reciprocal(m + 1)
                dve.wait_ge(spread, m + 1)
                dve.scalar_tensor_tensor(y[:, m], y[:, m], vec(core, "gla_norm"), rs[:, m % 2], ALU.mult,
                                         ALU.mult).then_inc(scaled, 1)
                dve.wait_ge(scaled, m + 1)
                dve.tensor_tensor(y[:, m], y[:, m], z[:, 8 + m], ALU.mult).then_inc(gated, 1)
            ahead.lo(dve)


def rwkv_project(core, w, xn_hi, xn_lo, z):
    nc = core.nc
    with ExitStack() as ctx:
        edge = ctx.enter_context(nc.sbuf_tensor("rp_edge", [P, 2, T + 2], F32))
        around = ctx.enter_context(nc.sbuf_tensor("rp_around", [P, 2, T], F32))
        share = ctx.enter_context(nc.sbuf_tensor("rp_share", [P, 2, NZR], F32))
        edged, around_ready, kept, mixed = (core.sem(f"rp_{x}") for x in ("edged", "around_ready", "kept", "mixed"))

        def dve_first(dve):
            mu = core.vec[:, VEC["mu"]:VEC["mu"] + NZR]
            dve.tensor_scalar(share[:, 0], mu, -1.0, 1.0, ALU.mult, ALU.add).then_inc(edged, 1)
            dve.tensor_scalar(share[:, 1], mu, 0.5, None, ALU.mult).then_inc(edged, 1)
            dve.memset(edge[:, :, :], 0.0).then_inc(edged, 1)
            dve.wait_ge(edged, 3)

        def column(n, m):
            return share[:, n, m:m + 1] if isinstance(m, int) else share[:, n, ds(m, 1)]

        def act_epilogue(act, m, r, kind, psum, filled, drained):
            act.wait_ge(filled, m + 1)
            if not (isinstance(m, int) and m < 2):
                act.wait_ge(mixed, m - 1)
            act.copy(edge[:, r % 2, 1:T + 1], psum).then_inc(drained, 1)

        def pool_epilogue(pool, m, r, kind, drained):
            pool.wait_ge(drained, m + 1)
            x = edge[:, r % 2]
            pool.tensor_tensor(around[:, r % 2], x[:, 0:T], x[:, 2:T + 2], ALU.add).then_inc(around_ready, 1)

        def dve_epilogue(dve, m, r, kind, drained):
            dve.wait_ge(drained, m + 1)
            out = tile_of(z, m)
            dve.tensor_scalar(out, edge[:, r % 2, 1:T + 1], column(0, m), None, ALU.mult).then_inc(kept, 1)
            dve.wait_ge(kept, m + 1)
            dve.wait_ge(around_ready, m + 1)
            dve.scalar_tensor_tensor(out, around[:, r % 2], column(1, m), out, ALU.mult, ALU.add).then_inc(mixed, 1)

        dense(core, "rp", w, xn_hi, xn_lo, [(0, NZR, None)], act_epilogue, dve_epilogue, pool_epilogue,
              act_first=lambda act: act.wait_ge(edged, 3), dve_first=dve_first)


def rwkv_mix(core, dram_const, dram_lora, dram_ada, z, gains):
    nc = core.nc
    levels = range(1, 6)
    with ExitStack() as ctx:
        def sb(name, shape):
            return ctx.enter_context(nc.sbuf_tensor(f"rw_{name}", shape, F32))
        n_masks = 16 + 4 + 4 + 5
        masks = sb("masks", [P, n_masks, P])
        keep = masks[:, 0:16].rearrange("p (d a) t -> p d (a t)", d=2)
        score_mask = masks[:, 16:20]
        level1_t, level1_m = masks[:, 20:22], masks[:, 22:24]
        level_mask = masks[:, 24:29].rearrange("p n (d c) -> p n d c", d=2)
        ident = cst(core, "ident")
        eye = ident.rearrange("p (a t) -> p a t", a=1).to_broadcast([P, 2, P])
        lora = sb("lora", [P, 2, P])
        spread_i = sb("spread_i", [32, P])
        kk_scale = z[0:32, 15]
        ka_rest = sb("ka_rest", [P, 4])
        sig = sb("sig", [P, 2, T])
        cum = sb("cum", [P, 2, T])
        kk = sb("kk", [P, T])
        b = sb("b", [P, T])
        y2 = sb("y2", [P, 2, T])
        rate, tmp = y2[:, 0], y2[:, 1]
        e_alpha = sb("e_alpha", [P, 2, BLK])
        e_rho = sb("e_rho", [P, 2, BLK])
        e_beta = sb("e_beta", [P, 2, BLK])
        v_b = sb("v_b", [P, 2, BLK])
        ar = sb("ar", [P, 2, 2, BLK])
        bk = sb("bk", [P, 2, 2, BLK])
        rho = sb("rho", [P, 2, 2, BLK])
        decay = sb("decay", [P, 2, 2, 2])
        beta_tok = sb("beta_tok", [P, 2, 2, BLK])
        kv_tok = sb("kv_tok", [P, 2, 4, BLK])
        an = sb("an", [P, 2, 2, 2, BLK])
        mp = sb("mp", [P, 2, 2, 2, 2, BLK])
        nq = sb("nq", [P, 2, 2, 2, 2, BLK])
        x = sb("x", [P, 2, 2, 2, BLK])
        xt = sb("xt", [P, 2, 2, 2, BLK])
        mx = sb("mx", [P, 5, 2, 2, BLK])
        wu = sb("wu", [P, 2, 2, BLK])
        rho2 = sb("rho2", [P, 2, BLK])
        carry = sb("carry", [P, 2, 2, CH])
        gain = sb("gain", [P, 2, 2, CH])
        state = sb("state", [P, 2, 2, CH])
        ada_ring = 3
        ada = sb("ada", [P, ada_ring, KD, P])
        c = sb("c", [P, KD])
        mod = sb("mod", [P, 6 * KD])
        ps = ctx.enter_context(nc.psum_tensor("rw_ps", [P, 8, 512], F32))
        loaded, setup, rest_ready = core.sem("rw_loaded"), core.sem("rw_setup"), core.sem("rw_rest_ready")
        lora_loaded, cleared, c_ready = core.sem("rw_lora_loaded"), core.sem("rw_cleared"), core.sem("rw_c_ready")
        ada_loaded = [core.sem(f"rw_ada_loaded{s}") for s in range(ada_ring)]
        ada_used, mod_ready = core.sem("rw_ada_used"), core.sem("rw_mod_ready")
        ada_summed = core.sem("rw_ada_summed")
        kk_squared, kk_summed, kk_scaled = (core.sem(f"rw_kk_{s}") for s in ("squared", "summed", "scaled"))
        k_ready, mod_copied = core.sem("rw_k_ready"), core.sem("rw_mod_copied")

        def bank(h, n):
            return ps[:, 4 * h + n]

        def pairs(a):
            return a.rearrange("p (d t) -> p d t", d=2)

        def joined(a, n, transposed=False):
            s = 2 ** n
            first, to_next = (s, P - s) if transposed else (0, P + s)
            return bass.AP(tensor=a.tensor, offset=a.offset + first, ap=[a.ap[0], [to_next, 2], [2 * s, P // (2 * s)], [1, s]])

        def joined_one(a, n, d, transposed=False):
            half = (1 - d) if transposed else d
            return a.rearrange("p (b two s) -> p b two s", two=2, s=2 ** n)[:, :, half]

        def halves(a, n):
            return a.rearrange("p (d b s) -> p d b s", d=2, s=2 ** n)

        heads = range(2)
        exp_made = Marks(core.sem("rw_exp"), ["e_rho", "e_beta", "v", "e_alpha"])
        ex_made = Marks(core.sem("rw_ex"), ["ex"])
        factor_made = Marks(core.sem("rw_factor"), ["ar_bk"])
        pe_front = Marks(core.sem("rw_pe_front"), ["tokens_a", "tokens_b"] +
                         [f"{s}{h}" for s in ("beta", "kappa", "nv", "m") for h in heads])
        act_front = Marks(core.sem("rw_act_front"), ["rho", "decay", "alpha_tok", "beta_tok", "kv_tok", "nv0", "nv1"])
        dve_front = Marks(core.sem("rw_dve_front"), ["mp0", "mp1", "nq0", "nq1", "xt0m", "xt1m", "xt0", "xt1",
                                                         "x0m", "x1m", "x0", "x1"])
        pe_steps, dve_steps = [], []
        for n in levels:
            pe_steps += [f"mx{n}_{h}" for h in heads]
            dve_steps += [f"mx{n}_{h}" for h in heads]
            both = [f"{s}{n}_{h}" for h in heads for s in (("x", "xt") if n < 5 else ("xt",))]
            pe_steps += both
            dve_steps += both
        pe_steps += [f"{s}{h}" for s in ("wu", "pw") for h in heads] + [f"chunk{c}_{h}" for h in heads for c in range(2)]
        pe_steps += ["state0_0", "state0_1"] + [f"{s}{h}" for h in heads for s in ("from_state", "state1_", "y")]
        act_steps = ["wu0", "wu1"] + [f"y{h}_{d}" for h in heads for d in range(2)]
        dve_steps += ["rho2_0", "rho2_1"] + [f"chunk{c}_{h}" for h in heads for c in range(2)] + \
            [f"state{m}_{h}" for m in range(2) for h in heads]
        pe_made, act_made, dve_made = (
            Marks(core.sem(f"rw_{n}"), s) for n, s in (("pe", pe_steps), ("act", act_steps), ("dve", dve_steps)))
        pe_pair = Marks(core.sem("rw_pe_pair"), ["kk_scale", "lora_rate", "lora0", "lora1"])
        act_pair = Marks(core.sem("rw_act_pair"), ["rate", "k_scale", "sig0", "sig1"])
        dve_pair = Marks(core.sem("rw_dve_pair"), ["spread", "kk", "b", "cum0", "cum1", "zero", "rk", "y"])
        block = ctx.enter_context(nc.Block())

        def tokens(d, j):
            return ds(j * BLK if d == 0 else (NBLK - 1) * BLK - j * BLK, BLK) if not isinstance(j, int) else \
                slice(j * BLK if d == 0 else (NBLK - 1 - j) * BLK, (j if d == 0 else NBLK - 1 - j) * BLK + BLK)

        def turns(e, i, turn):
            with e.Fori(0, NBLK // 2 - 1) as u:
                for par in range(2):
                    turn(u * 2 + par, i * NBLK + u * 2 + par, par, 2, i * (NBLK // 2) + u)
            for j in (NBLK - 2, NBLK - 1):
                turn(j, i * NBLK + j, j % 2, NBLK - 1 - j, i * (NBLK // 2) + j // 2)

        @block.sync
        def _(sp):
            at = CONST["chunk_keep"] * P
            sp.dma_start(masks[:, :, :].rearrange("p a t -> p (a t)"),
                         dram_const[:, at:at + n_masks * P]).then_inc(loaded, 16)
            for s in range(ada_ring):
                sp.dma_start(ada[:, s].rearrange("p k c -> p (k c)"), dram_ada[s]).then_inc(ada_loaded[s], 16)
            with sp.Fori(0, 6 * KD // ada_ring - 1) as q:
                for s in range(ada_ring):
                    sp.wait_ge(ada_used, q * ada_ring + s + 1)
                    sp.dma_start(ada[:, s].rearrange("p k c -> p (k c)"),
                                 dram_ada[ds(q * ada_ring + ada_ring + s, 1)].rearrange("a p k -> (a p) k")
                                 ).then_inc(ada_loaded[s], 16)

        @block.scalar
        def _(act):
            for made in (exp_made, act_front, act_made, act_pair):
                made.begin(act)
            act.activation(c[:, :], core.vec[:, VEC["c"]:VEC["c"] + KD], ACT.Silu).then_inc(c_ready, 1)
            act.activation(z[:, 12], z[:, 12], ACT.Tanh).then_inc(setup, 1)
            for n in range(HEAD_PAIRS):
                if n >= 2:
                    act.wait_ge(kk_summed, n - 1)
                act.activation(y2[:, n % 2], z[:, 4 + n], ACT.Square, scale=vec(core, "k_k", n)).then_inc(kk_squared, 1)
            act.wait_ge(kk_scaled, 1)
            act.activation(kk_scale, kk_scale, ACT.Sqrt).then_inc(setup, 1)
            act.wait_ge(rest_ready, 1)

            def front(t, par, last_used):
                act.wait_ge(*factor_made.by("ar_bk", t))
                act.copy(rho[:, par], ar[:, :, 1]).then_inc(*act_front("rho"))
                act.wait_ge(*last_used)
                act.copy(decay[:, par, 0], e_rho[:, 0, CH - 1::CH])
                act.copy(decay[:, par, 1], e_rho[:, 1, 0::CH]).then_inc(*act_front("decay"))
                act.wait_ge(*pe_front.by("tokens_a", t))
                act.copy(an[:, par, :, :, 0:CH].rearrange("p h d c -> p d h c"),
                         bank(0, 0)[:, 0:2 * P].rearrange("p (d h c) -> p d h c", d=2, h=2)
                         ).then_inc(*act_front("alpha_tok"))
                act.copy(beta_tok[:, par], pairs(bank(0, 0)[:, 2 * P:])).then_inc(*act_front("beta_tok"))
                act.wait_ge(*pe_front.by("tokens_b", t))
                act.copy(kv_tok[:, par].rearrange("p a t -> p (a t)"), bank(1, 0)).then_inc(*act_front("kv_tok"))

            def exps(i, j, t, decay_copied):
                act.wait_ge(*decay_copied)
                for d in range(2):
                    ins = act.activation(e_rho[:, d], cum[:, d, tokens(d, j)], ACT.Exp, scale=-DECAY)
                ins.then_inc(*exp_made("e_rho"))
                for d in range(2):
                    ins = act.activation(e_beta[:, d], cum[:, d, tokens(d, j)], ACT.Exp, scale=DECAY)
                ins.then_inc(*exp_made("e_beta"))
                for d in range(2):
                    ins = act.copy(v_b[:, d], tile_of(z, i + 8)[:, tokens(d, j)])
                ins.then_inc(*exp_made("v"))
                act.wait_ge(*ex_made.by("ex", t))
                act.activation(e_alpha[:, :, :], e_alpha[:, :, :], ACT.Exp, scale=-DECAY).then_inc(*exp_made("e_alpha"))

            def front_end(t, par):
                for h in heads:
                    act.wait_ge(*pe_front.by(f"nv{h}", t))
                    act.copy(an[:, par, h, :, CH:], pairs(bank(h, 0)[:, 0:2 * CH])).then_inc(*act_front(f"nv{h}"))

            with act.Fori(0, HEAD_PAIRS) as i:
                act.wait_ge(*dve_pair.before(i))
                act.wait_ge(*pe_pair.by("lora_rate", i))
                act.activation(rate, ps[:, 4:6].rearrange("p a t -> p (a t)"), ACT.Sigmoid,
                               bias=vec(core, "a0", i)).then_inc(*act_pair("rate"))
                act.wait_ge(*act_pair.by("rate", i))
                act.activation(tmp, rate, ACT.Identity, bias=ka_rest[:, ds(i, 1)], scale=vec(core, "k_a", i)
                               ).then_inc(*act_pair("k_scale"))
                for d in range(2):
                    act.wait_ge(*pe_pair.by(f"lora{d}", i))
                    act.activation(sig[:, d], ps[:, 2 * d:2 * d + 2].rearrange("p a t -> p (a t)"), ACT.Sigmoid,
                                   bias=vec(core, "w0", i + 4 * d)).then_inc(*act_pair(f"sig{d}"))
                act.wait_ge(*dve_pair.by("zero", i))
                exps(i, 0, i * NBLK, act_front.before(i * NBLK))
                front(i * NBLK, 0, dve_made.before(i * NBLK))
                front_end(i * NBLK, 0)
                exps(i, 1, i * NBLK + 1, act_front.by("decay", i * NBLK))

                def turn(j, t, par, ahead, two):
                    if ahead:
                        front(t + 1, 1 - par, dve_made.before(t))
                        if ahead > 1:
                            exps(i, j + 2, t + 2, act_front.by("decay", t + 1))
                        front_end(t + 1, 1 - par)
                    for h in heads:
                        act.wait_ge(*pe_made.by(f"wu{h}", t))
                        act.copy(wu[:, h], pairs(bank(h, 1)[:, 0:2 * P])).then_inc(*act_made(f"wu{h}"))
                    for h in heads:
                        rows = slice(64 * h, 64 * h + 64)
                        act.wait_ge(*pe_made.by(f"y{h}", t))
                        for d in range(2):
                            act.copy(y2[rows, d, tokens(d, j)],
                                     bank(h, 0)[rows, d * P:(d + 1) * P]).then_inc(*act_made(f"y{h}_{d}"))
                turns(act, i, turn)

        @block.gpsimd
        def _(pool):
            factor_made.begin(pool)
            pool.memset(mx[:, :, :, :, :].rearrange("p n h d t -> p (n h d t)"), 0.0).then_inc(cleared, 1)
            pool.wait_ge(loaded, 16)
            pool.wait_ge(c_ready, 1)
            with pool.Fori(0, HEAD_PAIRS) as i:
                pool.wait_ge(*pe_pair.before(i))
                pool.dma_start(lora[:, :, :], dram_lora[:, 0:2, ds(i * P, P)]).then_inc(lora_loaded, 16)
                r_i, k_i = tile_of(z, i + 0), tile_of(z, i + 4)
                pool.wait_ge(*act_pair.by("k_scale", i))
                pool.wait_ge(*dve_pair.by("kk", i))
                pool.tensor_tensor(k_i, k_i, tmp, ALU.mult).then_inc(k_ready, 1)
                with pool.Fori(0, NBLK // 2) as u:
                    for par in range(2):
                        j, t = u * 2 + par, i * NBLK + u * 2 + par
                        if par == 0:
                            pool.wait_ge(*dve_pair.by("zero", i))
                            pool.wait_ge(k_ready, i + 1)

                        pool.wait_ge(*exp_made.by("e_beta", t))
                        pool.wait_ge(*pe_front.before(t))
                        pool.wait_ge(*act_front.before(t))
                        for d in range(2):
                            at = tokens(d, j)
                            pool.tensor_tensor(ar[:, d, 1], r_i[:, at], e_rho[:, d], ALU.mult)
                            pool.tensor_tensor(bk[:, 0, d], b[:, at], e_beta[:, d], ALU.mult)
                            pool.tensor_tensor(bk[:, 1, d], k_i[:, at], e_beta[:, d], ALU.mult)
                        pool.wait_ge(*exp_made.by("e_alpha", t))
                        for d in range(2):
                            ins = pool.tensor_tensor(ar[:, d, 0], kk[:, tokens(d, j)], e_alpha[:, d], ALU.mult)
                        ins.then_inc(*factor_made("ar_bk"))

                        two = i * (NBLK // 2) + u
                        for s in ((0, 1), (2,))[par]:
                            done = (two * ada_ring + s) * 4
                            pool.wait_ge(ada_loaded[s], two * 16 + 16)
                            pool.tensor_tensor(ada[:, s], ada[:, s],
                                               c.rearrange("p (k a) -> p k a", a=1).to_broadcast([P, KD, P]), ALU.mult
                                               ).then_inc(ada_summed, 1)
                            for n, left in enumerate((4, 2, 1)):
                                pool.wait_ge(ada_summed, done + n + 1)
                                pool.tensor_tensor(ada[:, s, 0:left], ada[:, s, 0:left], ada[:, s, left:2 * left],
                                                   ALU.add).then_inc(ada_summed, 1)

        @block.tensor
        def _(pe):


            def front_tokens(t, drained):
                pe.wait_ge(*factor_made.by("ar_bk", t))
                pe.wait_ge(*drained)
                for d in range(2):
                    pe.transpose(bank(0, 0)[:, d * P:(d + 1) * P], ar[:, d, 0], ident)
                for d in range(2):
                    mm = pe.transpose(bank(0, 0)[:, (2 + d) * P:(3 + d) * P], bk[:, 0, d], ident)
                mm.then_inc(*pe_front("tokens_a"))
                pe.wait_ge(*exp_made.by("v", t))
                for d in range(2):
                    pe.transpose(bank(1, 0)[:, d * P:(d + 1) * P], bk[:, 1, d], ident)
                for d in range(2):
                    mm = pe.transpose(bank(1, 0)[:, (2 + d) * P:(3 + d) * P], v_b[:, d], ident)
                mm.then_inc(*pe_front("tokens_b"))

            def front_scores(t, n):
                for h in heads:
                    rows = slice(64 * h, 64 * h + 64)
                    if n == 0:
                        pe.wait_ge(*act_front.by(("beta_tok", "kv_tok")[h], t))
                    else:
                        pe.wait_ge(*dve_front.by(f"mp{h}", t))
                    for d in range(2):
                        mm = pe.matmul(bank(h, 0)[:, d * 2 * P:(d + 1) * 2 * P], bk[rows, n, d],
                                       ar[rows, d].rearrange("p a t -> p (a t)"), start=True, stop=True)
                    mm.then_inc(*pe_front(("beta", "kappa")[n] + str(h)))

            def front_nv(t, par):
                for h in heads:
                    pe.wait_ge(*dve_front.by(f"nq{h}", t))
                    for d in range(2):
                        mm = pe.matmul(bank(h, 0)[:, d * CH:(d + 1) * CH], nq[:, par, h, d, 0],
                                       kv_tok[:, par, 2 + d, h * CH:(h + 1) * CH], start=True, stop=True)
                    mm.then_inc(*pe_front(f"nv{h}"))

            def front_m(t):
                for h in heads:
                    rows = slice(64 * h, 64 * h + 64)
                    pe.wait_ge(*act_front.by(f"nv{h}", t))
                    for d in range(2):
                        mm = pe.matmul(bank(h, 0)[:, d * P:(d + 1) * P], ar[rows, d, 0], bk[rows, 0, d],
                                       start=True, stop=True)
                    mm.then_inc(*pe_front(f"m{h}"))

            def modulation_products(two, par):
                for s in ((0, 1), (2,))[par]:
                    pe.wait_ge(ada_summed, (two * ada_ring + s) * 4 + 4)
                    pe.matmul(bank(0, 3)[:, 256 + s:257 + s], ada[:, s, 0], cst(core, "ones")[:, 0:1],
                              start=True, stop=True).then_inc(ada_used, 1)

            for made in (pe_front, pe_made, pe_pair):
                made.begin(pe)
            for n in range(HEAD_PAIRS):
                pe.wait_ge(kk_squared, n + 1)
                for hf in range(2):
                    mm = pe.matmul(ps[0:32, hf], head_rows(core, n), y2[:, n % 2, hf * HALF:(hf + 1) * HALF],
                                   start=(n == 0), stop=(n == HEAD_PAIRS - 1))
                mm.then_inc(kk_summed, 1)
            pe.wait_ge(kk_scaled, 2)
            pe.wait_ge(setup, 2)

            pe.wait_ge(cleared, 1)
            with pe.Fori(0, HEAD_PAIRS) as i:
                pe.wait_ge(*dve_pair.by("spread", i))
                for hf in range(2):
                    mm = pe.matmul(ps[:, 6 + hf], spread_i[:, :], kk_scale[:, hf * HALF:(hf + 1) * HALF],
                                   start=True, stop=True)
                mm.then_inc(*pe_pair("kk_scale"))
                pe.wait_ge(lora_loaded, i * 16 + 16)
                for n, rows, w_n, z_n in ((2, slice(0, 64), 1, 13), (0, slice(0, 64), 0, 12),
                                          (1, slice(64, 128), 0, 12)):
                    for hf in range(2):
                        mm = pe.matmul(ps[:, 2 * n + hf], lora[rows, w_n], z[rows, z_n, hf * HALF:(hf + 1) * HALF],
                                       start=True, stop=True)
                    mm.then_inc(*pe_pair(("lora0", "lora1", "lora_rate")[n]))
                first = i * NBLK
                front_tokens(first, act_made.before(first))
                front_scores(first, 0)
                front_scores(first, 1)
                front_nv(first, 0)
                front_m(first)

                def turn(j, t, par, ahead, two):
                    for n in levels:
                        for h in heads:
                            if n == 1:
                                pe.wait_ge(*dve_front.by(f"x{h}", t))
                                pe.wait_ge(*dve_made.before(t))
                            else:
                                pe.wait_ge(*dve_made.by(f"x{n - 1}_{h}", t))
                            for d in range(2):
                                mm = pe.matmul(bank(h, 1)[:, d * P:(d + 1) * P], mp[:, par, h, d, 0],
                                               x[:, par, h, d], start=True, stop=True)
                            mm.then_inc(*pe_made(f"mx{n}_{h}"))
                        if ahead:
                            if n == 1:
                                front_tokens(t + 1, act_made.before(t))
                            elif n == 2:
                                front_scores(t + 1, 0)
                            elif n == 3:
                                front_scores(t + 1, 1)
                            elif n == 4:
                                front_nv(t + 1, 1 - par)
                            elif n == 5:
                                front_m(t + 1)
                        for h in heads:
                            pe.wait_ge(*dve_made.by(f"mx{n}_{h}", t))
                            if n == 1:
                                pe.wait_ge(*dve_front.by(f"xt{h}", t))
                            else:
                                pe.wait_ge(*dve_made.by(f"xt{n - 1}_{h}", t))
                            if n < 5:
                                for d in range(2):
                                    mm = pe.matmul(bank(h, 2)[:, d * P:(d + 1) * P], xt[:, par, h, d],
                                                   mx[:, n - 1, h, d], start=True, stop=True)
                                mm.then_inc(*pe_made(f"x{n}_{h}"))
                            for d in range(2):
                                mm = pe.matmul(bank(h, 3)[:, d * P:(d + 1) * P], mx[:, n - 1, h, d],
                                               xt[:, par, h, d], start=True, stop=True)
                            mm.then_inc(*pe_made(f"xt{n}_{h}"))
                    for h in heads:
                        pe.wait_ge(*dve_made.by(f"xt5_{h}", t))
                        pe.wait_ge(*act_front.by(f"nv{h}", t))
                        for d in range(2):
                            mm = pe.matmul(bank(h, 1)[:, d * P:(d + 1) * P], xt[:, par, h, d], an[:, par, h, d],
                                           start=True, stop=True)
                        mm.then_inc(*pe_made(f"wu{h}"))
                    for h in heads:
                        rows = slice(64 * h, 64 * h + 64)
                        pe.wait_ge(*act_made.by(f"wu{h}", t))
                        for d in range(2):
                            mm = pe.matmul(bank(h, 1)[rows, d * P:(d + 1) * P], wu[:, h, d, 0:CH], mp[:, par, h, d, 1],
                                           start=True, stop=True)
                        mm.then_inc(*pe_made(f"pw{h}"))
                    for h in heads:
                        rows, cols = slice(64 * h, 64 * h + 64), slice(h * CH, (h + 1) * CH)
                        for c in range(2):
                            at = slice(64 * c, 64 * c + 64)
                            out = bank(h, 2 + c)
                            for d in range(2):
                                pe.matmul(out[rows, d * CH:(d + 1) * CH], wu[at, h, d, 0:CH], beta_tok[at, par, d, cols],
                                          start=True, stop=True)
                            for d in range(2):
                                here = out[rows, (2 + d) * CH:(3 + d) * CH]
                                pe.matmul(here, beta_tok[at, par, d, cols], wu[at, h, d, CH:], start=True, stop=False)
                                mm = pe.matmul(here, kv_tok[at, par, d, cols], kv_tok[at, par, 2 + d, cols],
                                               start=False, stop=True)
                            mm.then_inc(*pe_made(f"chunk{c}_{h}"))

                    def from_block(h, d, part):
                        rows, cols = slice(64 * h, 64 * h + 64), slice(h * CH, (h + 1) * CH)
                        out = bank(h, 0)[rows, d * P:(d + 1) * P]
                        if part == 0:
                            pe.matmul(out, wu[:, h, d, CH:], mp[:, par, h, d, 1], start=(d == 0), stop=False)
                        else:
                            pe.matmul(out, kv_tok[:, par, 2 + d, cols], nq[:, par, h, d, 1], start=False, stop=False)

                    def next_state(h, m):
                        rows = slice(64 * h, 64 * h + 64)
                        for d in range(2):
                            mm = pe.matmul(bank(h, 1)[rows, (2 * m + d) * CH:(2 * m + d + 1) * CH],
                                           carry[rows, m if d == 0 else 1 - m, d], state[rows, m, d],
                                           start=True, stop=True)
                        mm.then_inc(*pe_made(f"state{m}_{h}"))

                    def from_state(h, m, mark):
                        rows = slice(64 * h, 64 * h + 64)
                        for d in range(2):
                            c = m if d == 0 else 1 - m
                            mm = pe.matmul(bank(h, 0)[rows, d * P + c * CH:d * P + (c + 1) * CH],
                                           state[rows, m, d], rho2[rows, d, c * CH:(c + 1) * CH],
                                           start=False, stop=(m == 1 and d == 1))
                        mm.then_inc(*pe_made(mark))

                    pe.wait_ge(*act_made.before(t))
                    for h in heads:
                        if ahead:
                            pe.wait_ge(*dve_front.by(f"x{h}", t + 1))
                        from_block(h, 0, 0)
                    for h in heads:
                        pe.wait_ge(*dve_made.by(f"chunk1_{h}", t))
                        from_block(h, 0, 1)
                        next_state(h, 0)
                        from_block(h, 1, 0)
                    for h in heads:
                        pe.wait_ge(*dve_made.by(f"state0_{h}", t))
                        from_block(h, 1, 1)
                        from_state(h, 0, f"from_state{h}")
                        next_state(h, 1)
                        from_state(h, 1, f"y{h}")
                    modulation_products(two, par)
                turns(pe, i, turn)

        @block.vector
        def _(dve):
            for made in (ex_made, dve_front, dve_made, dve_pair):
                made.begin(dve)
            dve.tensor_scalar(ka_rest[:, :], core.vec[:, VEC["k_a"]:VEC["k_a"] + 4], -1.0, 1.0, ALU.mult,
                              ALU.add).then_inc(rest_ready, 1)
            dve.wait_ge(rest_ready, 1)
            dve.wait_ge(loaded, 16)

            dve.wait_ge(kk_summed, HEAD_PAIRS)
            dve.tensor_scalar(kk_scale, ps[0:32, 0:2].rearrange("p a t -> p (a t)"), 1e-24, None, ALU.max
                              ).then_inc(kk_scaled, 1)
            dve.wait_ge(setup, 2)
            dve.reciprocal(kk_scale, kk_scale).then_inc(kk_scaled, 1)

            def front_scores(t, par, n):
                s, dst = (("mp", mp), ("nq", nq))[n]
                for h in heads:
                    dve.wait_ge(*pe_front.by(("beta", "kappa")[n] + str(h), t))
                    dve.tensor_tensor(dst[:, par, h].rearrange("p d a t -> p (d a t)"), bank(h, 0),
                                      score_mask.rearrange("p a t -> p (a t)"), ALU.mult
                                      ).then_inc(*dve_front(f"{s}{h}"))

            def before_token(t, j, last_used):
                dve.wait_ge(*last_used)
                for d in range(2):
                    at = tokens(d, j)
                    ins = dve.tensor_tensor(e_alpha[:, d], cum[:, d, at], sig[:, d, at], ALU.subtract)
                ins.then_inc(*ex_made("ex"))

            def front_xt(t, par):
                for h in heads:
                    dve.wait_ge(*dve_front.by(f"mp{h}", t))
                    dve.tensor_tensor(xt[:, par, h], mp[:, par, h, :, 0], level1_t, ALU.mult
                                      ).then_inc(*dve_front(f"xt{h}m"))
                for h in heads:
                    dve.wait_ge(*dve_front.by(f"xt{h}m", t))
                    dve.tensor_tensor(xt[:, par, h], xt[:, par, h], eye, ALU.add).then_inc(*dve_front(f"xt{h}"))

            def front_x(t, par):
                for h in heads:
                    dve.wait_ge(*pe_front.by(f"m{h}", t))
                    dve.tensor_tensor(x[:, par, h], pairs(bank(h, 0)[:, 0:2 * P]), level1_m, ALU.mult
                                      ).then_inc(*dve_front(f"x{h}m"))
                for h in heads:
                    dve.wait_ge(*dve_front.by(f"x{h}m", t))
                    dve.tensor_tensor(x[:, par, h], x[:, par, h], eye, ALU.add).then_inc(*dve_front(f"x{h}"))

            with dve.Fori(0, HEAD_PAIRS) as i:
                r_i, k_i = tile_of(z, i + 0), tile_of(z, i + 4)
                dve.wait_ge(*pe_pair.before(i))
                dve.tensor_copy(spread_i[:, :], cst(core, "spread", i)[0:32]).then_inc(*dve_pair("spread"))
                dve.wait_ge(*pe_pair.by("kk_scale", i))
                dve.scalar_tensor_tensor(kk[:, :], k_i, vec(core, "k_k", i), ps[:, 6:8].rearrange("p a t -> p (a t)"),
                                         ALU.mult, ALU.mult).then_inc(*dve_pair("kk"))
                dve.wait_ge(*act_pair.by("rate", i))
                dve.wait_ge(*dve_pair.by("kk", i))
                dve.scalar_tensor_tensor(b[:, :], kk[:, :], -1.0, rate, ALU.mult, ALU.mult).then_inc(*dve_pair("b"))
                dve.wait_ge(*act_pair.by("sig0", i))
                dve.tensor_tensor_scan(cum[:, 0], keep[:, 0], sig[:, 0], 0.0, ALU.mult, ALU.add
                                       ).then_inc(*dve_pair("cum0"))
                dve.wait_ge(*act_pair.by("sig1", i))
                dve.tensor_tensor_scan(cum[:, 1, ::-1], keep[:, 1, ::-1], sig[:, 1, ::-1], 0.0, ALU.mult, ALU.add
                                       ).then_inc(*dve_pair("cum1"))
                dve.memset(state[:, 0], 0.0).then_inc(*dve_pair("zero"))
                dve.wait_ge(*dve_pair.by("zero", i))
                before_token(i * NBLK, 0, factor_made.before(i * NBLK))
                front_scores(i * NBLK, 0, 0)
                before_token(i * NBLK + 1, 1, factor_made.by("ar_bk", i * NBLK))
                front_scores(i * NBLK, 0, 1)
                front_xt(i * NBLK, 0)
                front_x(i * NBLK, 0)

                def turn(j, t, par, ahead, two):
                    for n in levels:
                        for h in heads:
                            dve.wait_ge(*pe_made.by(f"mx{n}_{h}", t))
                            dve.tensor_tensor(joined(mx[:, n - 1, h], n), joined(pairs(bank(h, 1)[:, 0:2 * P]), n),
                                              level_mask[:, n - 1].rearrange("p d (b s) -> p d b s", s=2 ** n), ALU.mult
                                              ).then_inc(*dve_made(f"mx{n}_{h}"))
                        for h in heads:
                            if n < 5:
                                dve.wait_ge(*pe_made.by(f"x{n}_{h}", t))
                                at = joined(x[:, par, h], n)
                                dve.tensor_tensor(at, at, joined(pairs(bank(h, 2)[:, 0:2 * P]), n), ALU.add
                                                  ).then_inc(*dve_made(f"x{n}_{h}"))
                            dve.wait_ge(*pe_made.by(f"xt{n}_{h}", t))

                            at = joined(xt[:, par, h], n, True)
                            dve.tensor_tensor(at, at, joined(pairs(bank(h, 3)[:, 0:2 * P]), n, True), ALU.add
                                              ).then_inc(*dve_made(f"xt{n}_{h}"))
                        if ahead and n in (2, 3):
                            front_scores(t + 1, 1 - par, n - 2)
                        if ahead and n == 4:
                            front_xt(t + 1, 1 - par)
                        if ahead > 1 and n == 1:
                            before_token(t + 2, j + 2, factor_made.by("ar_bk", t + 1))
                        if ahead and n == 5:
                            front_x(t + 1, 1 - par)
                    for h in heads:
                        rows = slice(64 * h, 64 * h + 64)
                        dve.wait_ge(*pe_made.by(f"pw{h}", t))
                        dve.wait_ge(*act_front.by("decay", t))
                        dve.tensor_tensor(rho2[rows], pairs(bank(h, 1)[rows, 0:2 * P]), rho[rows, par], ALU.add
                                          ).then_inc(*dve_made(f"rho2_{h}"))
                    for h in heads:
                        rows = slice(64 * h, 64 * h + 64)
                        eye64 = cst(core, "eye64")[rows, 0:CH].rearrange("p (a c) -> p a c", a=1).to_broadcast([64, 2, CH])
                        for c in range(2):
                            dve.wait_ge(*pe_made.by(f"chunk{c}_{h}", t))
                            dve.tensor_tensor(carry[rows, c], pairs(bank(h, 2 + c)[rows, 0:2 * CH]), eye64, ALU.add)
                            for d in range(2):
                                ins = dve.tensor_scalar(gain[rows, c, d], bank(h, 2 + c)[rows, (2 + d) * CH:(3 + d) * CH],
                                                        decay[rows, par, d, c:c + 1], None, ALU.mult)
                            ins.then_inc(*dve_made(f"chunk{c}_{h}"))
                    for m in range(2):
                        for h in heads:
                            rows = slice(64 * h, 64 * h + 64)
                            dve.wait_ge(*pe_made.by(f"state{m}_{h}", t))
                            if m == 0:
                                dve.wait_ge(*dve_made.by(f"chunk1_{h}", t))
                            else:
                                dve.wait_ge(*pe_made.by(f"from_state{h}", t))
                            for d in range(2):
                                c = m if d == 0 else 1 - m
                                ins = dve.scalar_tensor_tensor(
                                    state[rows, 1 - m, d], bank(h, 1)[rows, (2 * m + d) * CH:(2 * m + d + 1) * CH],
                                    decay[rows, par, d, c:c + 1], gain[rows, c, d], ALU.mult, ALU.add)
                            ins.then_inc(*dve_made(f"state{m}_{h}"))
                    first, count = (0, 2) if par == 0 else (2, 1)
                    dve.wait_ge(ada_used, two * ada_ring + first + count)
                    dve.tensor_copy(mod[:, ds(two * ada_ring + first, count)],
                                    bank(0, 3)[:, 256 + first:256 + first + count]).then_inc(mod_copied, 1)

                turns(dve, i, turn)
                dve.scalar_tensor_tensor(r_i, r_i, vec(core, "r_k", i), k_i, ALU.mult, ALU.mult).then_inc(*dve_pair("rk"))
                dve.wait_ge(*act_made.before((i + 1) * NBLK))
                dve.wait_ge(*dve_pair.by("rk", i))
                dve.tensor_tensor(k_i, y2[:, 0], y2[:, 1], ALU.add).then_inc(*dve_pair("y"))

            dve.wait_ge(mod_copied, HEAD_PAIRS * NBLK)
            dve.tensor_tensor(mod[:, :], mod[:, :], core.vec[:, VEC["ada_b"]:VEC["ada_b"] + 6 * KD], ALU.add
                              ).then_inc(mod_ready, 1)
            dve.wait_ge(mod_ready, 1)
            own = core.vec[:, VEC["gains2"]:VEC["gains2"] + 4 * KD].rearrange("p (a k) -> p a k", k=KD)
            for half in range(2):
                shift, scale, gate = (mod[:, (3 * half + n) * KD:(3 * half + n + 1) * KD] for n in range(3))
                dve.scalar_tensor_tensor(gains[:, 3 * half], scale, 1.0, own[:, 2 * half], ALU.add, ALU.mult)
                dve.tensor_copy(gains[:, 3 * half + 1], shift)
                dve.tensor_tensor(gains[:, 3 * half + 2], gate, own[:, 2 * half + 1], ALU.mult).then_inc(mod_ready, 1)


def rwkv_finish(core, dram_lora, z, y_gla, hi, lo, ahead):
    nc = core.nc
    with ExitStack() as ctx:
        gate_lora = ctx.enter_context(nc.sbuf_tensor("rf_gate_lora", [P, 512], F32))
        square = ctx.enter_context(nc.sbuf_tensor("rf_square", [P, 2, T], F32))
        scale = ctx.enter_context(nc.sbuf_tensor("rf_scale", [32, T], F32))
        ps = ctx.enter_context(nc.psum_tensor("rf_ps", [P, 8, 512], F32))
        loaded = core.sem("rf_loaded")
        summed, centred, squared, var_summed = (core.sem(f"rf_{n}") for n in ("summed", "centred", "squared", "var_summed"))
        bonus_summed, bonus, shifted = (core.sem(f"rf_{n}") for n in ("bonus_summed", "bonus", "shifted"))
        hi_gla, hi_rwkv, lo_done = (core.sem(f"rf_{n}") for n in ("hi_gla", "hi_rwkv", "lo_done"))
        lo_gla_done = core.sem("rf_lo_gla_done")
        gate_lora_ready, rooted, scale_ready = (core.sem(f"rf_{n}") for n in ("gate_lora_ready", "rooted", "scale_ready"))
        spread, gated, scaled, joined, done = (core.sem(f"rf_{n}") for n in ("spread", "gated", "scaled", "joined", "done"))
        block = ctx.enter_context(nc.Block())
        tiles = range(HEAD_PAIRS)

        def wide(first_bank):
            return ps[:, first_bank:first_bank + 2].rearrange("p a t -> p (a t)")

        def low_part(e, n, src, tile, hi_made):
            e.wait_ge(hi_made, n + 1)
            e.tensor_tensor(lo[:, tile], src, hi[:, tile].bitcast(F32), ALU.subtract).then_inc(
                lo_done if hi_made is hi_rwkv else lo_gla_done, 1)

        def finish(dve, n):
            dve.wait_ge(joined, n + 1)
            dve.wait_ge(gated, n + 1)
            dve.tensor_tensor(z[:, n], z[:, 4 + n], wide((0, 2)[n % 2]), ALU.mult).then_inc(done, 1)

        @block.sync
        def _(sp):
            sp.dma_start(gate_lora[:, :], dram_lora[:, 2]).then_inc(loaded, 16)
            ahead.load(sp)

        @block.tensor
        def _(pe):
            def product(lhs, rhs, first_bank, **flags):
                for hf in range(2):
                    mm = pe.matmul(ps[0:lhs.shape[-1], first_bank + hf], lhs, rhs[:, hf * HALF:(hf + 1) * HALF], **flags)
                return mm

            once = {"start": True, "stop": True}
            def var_sum(n):
                pe.wait_ge(squared, n + 1)
                product(head_rows(core, n), square[:, n % 2], 4, start=(n == 0), stop=(n == HEAD_PAIRS - 1)
                        ).then_inc(var_summed, 1)

            for n in tiles:
                if n >= 2:
                    pe.wait_ge(centred, n - 1)
                product(cst(core, "head_ones"), z[:, 4 + n], (0, 6)[n % 2], **once).then_inc(summed, 1)
                if n >= 1:
                    pe.wait_ge(bonus, n)
                product(cst(core, "head_ones"), z[:, n], 2, **once).then_inc(bonus_summed, 1)
                if n >= 1:
                    var_sum(n - 1)
            var_sum(HEAD_PAIRS - 1)
            pe.wait_ge(loaded, 16)
            pe.wait_ge(gate_lora_ready, 1)
            pe.wait_ge(centred, HEAD_PAIRS)
            pe.wait_ge(bonus, HEAD_PAIRS)
            for n in tiles:
                if n >= 2:
                    pe.wait_ge(done, n - 1)
                product(gate_lora[:, n * P:(n + 1) * P], z[:, 14], (0, 2)[n % 2], **once).then_inc(gated, 1)
                pe.wait_ge(scale_ready, 1)
                if n >= 2:
                    pe.wait_ge(scaled, n - 1)
                product(head_spread(core, n), scale, (4, 6)[n % 2], **once).then_inc(spread, 1)

        @block.scalar
        def _(act):
            act.activation(z[:, 14], z[:, 14], ACT.Sigmoid).then_inc(gate_lora_ready, 1)
            for n in tiles:
                act.copy(hi[:, 4 + n], y_gla[:, n]).then_inc(hi_gla, 1)
                act.wait_ge(centred, n + 1)
                if n >= 2:
                    act.wait_ge(var_summed, n - 1)
                act.activation(square[:, n % 2], z[:, 4 + n], ACT.Square).then_inc(squared, 1)
                act.wait_ge(bonus, n + 1)
                act.activation(z[:, 8 + n], z[:, 8 + n], ACT.Identity, bias=vec(core, "ln_b", n)).then_inc(shifted, 1)
            act.wait_ge(var_summed, HEAD_PAIRS)
            act.activation(scale[:, :], wide(4)[0:32], ACT.Sqrt, bias=eps(core, EPS_GN)[0:32], scale=1.0 / CH
                           ).then_inc(rooted, 1)
            ahead.hi(act)
            for n in tiles:
                act.wait_ge(done, n + 1)
                act.copy(hi[:, n], z[:, n]).then_inc(hi_rwkv, 1)

        @block.vector
        def _(dve):
            for n in tiles:
                dve.wait_ge(summed, n + 1)
                dve.scalar_tensor_tensor(z[:, 4 + n], wide((0, 6)[n % 2]), 1.0 / CH, z[:, 4 + n], ALU.mult, ALU.subtract
                                         ).then_inc(centred, 1)
                dve.wait_ge(bonus_summed, n + 1)
                dve.tensor_tensor(z[:, 8 + n], wide(2), z[:, 8 + n], ALU.mult).then_inc(bonus, 1)
            dve.wait_ge(rooted, 1)
            dve.reciprocal(scale[:, :], scale[:, :]).then_inc(scale_ready, 1)
            ahead.lo(dve)
            for n in tiles:
                dve.wait_ge(spread, n + 1)
                dve.scalar_tensor_tensor(z[:, 4 + n], z[:, 4 + n], vec(core, "ln_w", n), wide((4, 6)[n % 2]),
                                         ALU.mult, ALU.mult).then_inc(scaled, 1)
                if n >= 1:
                    finish(dve, n - 1)
                if n >= 2:
                    low_part(dve, n - 2, z[:, n - 2], n - 2, hi_rwkv)
            finish(dve, HEAD_PAIRS - 1)
            for n in (HEAD_PAIRS - 2, HEAD_PAIRS - 1):
                low_part(dve, n, z[:, n], n, hi_rwkv)

        @block.gpsimd
        def _(pool):
            for n in tiles:
                low_part(pool, n, y_gla[:, n], 4 + n, hi_gla)
            for n in tiles:
                pool.wait_ge(scaled, n + 1)
                pool.wait_ge(shifted, n + 1)
                pool.tensor_tensor(z[:, 4 + n], z[:, 4 + n], z[:, 8 + n], ALU.add).then_inc(joined, 1)


def split_tiles(core, name, sources, hi, lo, ahead):
    hi_done, lo_done = core.sem(f"{name}_hi"), [core.sem(f"{name}_lo"), core.sem(f"{name}_lo_pool")]
    with core.nc.Block() as block:
        def low_part(e, n, done):
            e.wait_ge(hi_done, n + 1)
            e.tensor_tensor(lo[:, n], sources[n], hi[:, n].bitcast(F32), ALU.subtract).then_inc(done, 1)

        @block.sync
        def _(sp):
            ahead.load(sp)

        @block.scalar
        def _(act):
            for n, src in enumerate(sources):
                act.copy(hi[:, n], src).then_inc(hi_done, 1)
            ahead.hi(act)

        @block.vector
        def _(dve):
            for n in range(len(sources)):
                if n % 3 != 1:
                    low_part(dve, n, lo_done[0])
            ahead.lo(dve)

        @block.gpsimd
        def _(pool):
            for n in range(1, len(sources), 3):
                low_part(pool, n, lo_done[1])


class SwigluWeights:

    def __init__(self, core, ctx, name, w_gate, w_up, w_down, spare):
        def sbr(n):
            return ctx.enter_context(core.nc.sbuf_tensor(f"{name}_{n}", [P, KD, P], F32R))
        self.dram = {"gate": w_gate, "up": w_up, "down": w_down}
        self.raw = {s: spare[:, n] for n, s in enumerate(self.dram)}
        self.silu = spare[:, 3]
        self.hi = {s: sbr(f"{s}_hi") for s in self.dram}
        self.lo = {s: sbr(f"{s}_lo") for s in self.dram}
        self.loaded = {s: core.sem(f"{name}_{s}_loaded") for s in self.dram}
        self.hi_ready = {s: core.sem(f"{name}_{s}_hi_ready") for s in self.dram}
        self.lo_ready = {s: core.sem(f"{name}_{s}_lo_ready") for s in self.dram}

        def flat(x):
            return x[:, :, :].rearrange("p k c -> p (k c)")
        self.ahead = Ahead([(self.dram[s][0], self.raw[s], flat(self.hi[s]), flat(self.lo[s]), self.loaded[s],
                             self.hi_ready[s], self.lo_ready[s]) for s in ("gate", "up")])


def swiglu(core, name, w, x_hi, x_lo, f):
    nc = core.nc
    raw, silu, dram, w_hi, w_lo = w.raw, w.silu, w.dram, w.hi, w.lo
    loaded, hi_ready, lo_ready = w.loaded, w.hi_ready, w.lo_ready
    with ExitStack() as ctx:
        def sbr(n, shape):
            return ctx.enter_context(nc.sbuf_tensor(f"{name}_{n}", shape, F32R))
        a_hi, a_lo = sbr("a_hi", [P, 2, T]), sbr("a_lo", [P, 2, T])
        a = ctx.enter_context(nc.sbuf_tensor(f"{name}_a", [P, T], F32))
        acc = {s: ctx.enter_context(nc.psum_tensor(f"{name}_ps_{s}", [P, T], F32)) for s in ("gate", "up")}
        acc_down = ctx.enter_context(nc.psum_tensor(f"{name}_ps_down", [P, 2, T], F32))
        filled = {s: core.sem(f"{name}_{s}_filled") for s in raw}
        zeroed, silu_ready, a_ready, a_hi_ready, a_lo_ready, added = (
            core.sem(f"{name}_{n}") for n in ("zeroed", "silu_ready", "a_ready", "a_hi_ready", "a_lo_ready", "added"))
        block = ctx.enter_context(nc.Block())

        def cycles(e, body):
            body(0, 0)
            body(1, 1)
            with e.Fori(0, (NF - 4) // 2) as i:
                body(i * 2 + 2, 0)
                body(i * 2 + 3, 1)
            body(NF - 2, 0)
            body(NF - 1, 1)

        def more(j):
            return not (isinstance(j, int) and j == NF - 1)

        @block.sync
        def _(sp):
            def body(j, par):
                for s in raw:
                    if isinstance(j, int) and j == 0 and s != "down":
                        continue
                    sp.wait_ge(lo_ready[s], j)
                    src = dram[s][j] if isinstance(j, int) else dram[s][ds(j, 1)].rearrange("a p k -> (a p) k")
                    sp.dma_start(raw[s], src).then_inc(loaded[s], 16)
            cycles(sp, body)

        def split_hi(act, s, j):
            act.wait_ge(loaded[s], j * 16 + 16)
            act.wait_ge(filled[s], j * (KD if s == "down" else 1))
            act.copy(w_hi[s][:, :, :].rearrange("p k c -> p (k c)"), raw[s]).then_inc(hi_ready[s], 1)

        def split_lo(dve, s, j):
            dve.wait_ge(hi_ready[s], j + 1)
            dve.tensor_tensor(w_lo[s][:, :, :].rearrange("p k c -> p (k c)"), raw[s],
                              w_hi[s][:, :, :].rearrange("p k c -> p (k c)").bitcast(F32),
                              ALU.subtract).then_inc(lo_ready[s], 1)

        @block.scalar
        def _(act):
            def body(j, par):
                act.wait_ge(filled["gate"], j + 1)
                act.wait_ge(a_ready, j)
                act.activation(silu, acc["gate"][:, :], ACT.Silu).then_inc(silu_ready, 1)
                if more(j):
                    split_hi(act, "gate", j + 1)
                    split_hi(act, "up", j + 1)
                act.wait_ge(a_ready, j + 1)
                act.copy(a_hi[:, par], a[:, :]).then_inc(a_hi_ready, 1)
                split_hi(act, "down", j)
            cycles(act, body)

        @block.vector
        def _(dve):
            dve.wait_ge(zeroed, 1)

            def add_down(j):
                for n in range(KD):
                    dve.wait_ge(filled["down"], j * KD + n + 1)
                    dve.tensor_tensor(f[:, n], f[:, n], acc_down[:, n % 2], ALU.add).then_inc(added, 1)

            def body(j, par):
                if more(j):
                    split_lo(dve, "gate", j + 1)
                dve.wait_ge(silu_ready, j + 1)
                dve.wait_ge(filled["up"], j + 1)
                dve.wait_ge(a_lo_ready, j)
                dve.tensor_tensor(a[:, :], silu, acc["up"][:, :], ALU.mult).then_inc(a_ready, 1)
                if not (isinstance(j, int) and j == 0):
                    add_down(j - 1)
                if more(j):
                    split_lo(dve, "up", j + 1)
                dve.wait_ge(a_hi_ready, j + 1)
                dve.tensor_tensor(a_lo[:, par], a[:, :], a_hi[:, par].bitcast(F32), ALU.subtract).then_inc(a_lo_ready, 1)
                split_lo(dve, "down", j)
            cycles(dve, body)
            add_down(NF - 1)

        @block.gpsimd
        def _(pool):
            pool.memset(f, 0.0).then_inc(zeroed, 1)

        @block.tensor
        def _(pe):
            def down(j, par):
                pe.wait_ge(a_lo_ready, j + 1)
                pe.wait_ge(lo_ready["down"], j + 1)
                for n in range(KD):
                    if not (isinstance(j, int) and j == 0 and n < 2):
                        pe.wait_ge(added, j * KD + (n - 1))
                    for part, x in ((w_hi, a_hi), (w_hi, a_lo), (w_lo, a_hi)):
                        for h in range(2):
                            mm = pe.matmul(acc_down[:, n % 2, h * HALF:(h + 1) * HALF], part["down"][:, n],
                                           x[:, par, h * HALF:(h + 1) * HALF],
                                           start=(part is w_hi and x is a_hi), stop=(part is w_lo))
                    mm.then_inc(filled["down"], 1)

            def body(j, par):
                for s in ("gate", "up"):
                    pe.wait_ge(lo_ready[s], j + 1)
                    pe.wait_ge(silu_ready if s == "gate" else a_ready, j)
                    for k in range(KD):
                        for part, x in ((w_hi, x_hi), (w_hi, x_lo), (w_lo, x_hi)):
                            for h in range(2):
                                mm = pe.matmul(acc[s][:, h * HALF:(h + 1) * HALF], part[s][:, k],
                                               x[:, k, h * HALF:(h + 1) * HALF],
                                               start=(k == 0 and part is w_hi and x is x_hi),
                                               stop=(k == KD - 1 and part is w_lo))
                    mm.then_inc(filled[s], 1)
                if not (isinstance(j, int) and j == 0):
                    down(j - 1, 1 - par)
            cycles(pe, body)
            down(NF - 1, 1)


def project(core, name, w, x_hi, x_lo, out, load=None):
    def act_epilogue(act, m, r, kind, psum, filled, drained):
        act.wait_ge(filled, m + 1)
        act.copy(tile_of(out, m), psum).then_inc(drained, 1)
    dense(core, name, w, x_hi, x_lo, [(0, KD, None)], act_epilogue, load=load)


def embedding_gate(core, w, h_hi, h_lo, e):
    nc = core.nc
    with ExitStack() as ctx:
        gate = ctx.enter_context(nc.sbuf_tensor("eg_gate", [P, 2, T], F32))
        gated = core.sem("eg_gated")

        def act_epilogue(act, m, r, kind, psum, filled, drained):
            act.wait_ge(filled, m + 1)
            if not (isinstance(m, int) and m < 2):
                act.wait_ge(gated, m - 1)
            act.activation(gate[:, r % 2], psum, ACT.Sigmoid, bias=vec(core, "ple_b", m)).then_inc(drained, 1)

        def dve_epilogue(dve, m, r, kind, drained):
            dve.wait_ge(drained, m + 1)
            dve.tensor_tensor(tile_of(e, m), tile_of(e, m), gate[:, r % 2], ALU.mult).then_inc(gated, 1)

        dense(core, "eg", w, h_hi, h_lo, [(0, KD, None)], act_epilogue, dve_epilogue)


def short_conv(core, w, x_hi, x_lo, y):
    nc = core.nc
    with ExitStack() as ctx:
        cvb = ctx.enter_context(nc.sbuf_tensor("sc_cvb", [P, 3, T], F32))
        u = ctx.enter_context(nc.sbuf_tensor("sc_u", [P, T + 2], F32))
        conv = ctx.enter_context(nc.sbuf_tensor("sc_conv", [P, T], F32))
        padded = core.sem("sc_padded")
        dve_made = Marks(core.sem("sc_dve"), ["u", "tap0", "tap1", "conv", "y"])

        def act_epilogue(act, m, r, jt, psum, filled, drained):
            act.wait_ge(filled, m + 1)
            if not (isinstance(m, int) and m < 3):
                act.wait_ge(*dve_made.by("u" if r % 3 < 2 else "y", jt - 1))
            act.copy(cvb[:, r % 3], psum).then_inc(drained, 1)

        def dve_epilogue(dve, m, r, jt, drained):
            if r % 3 == 1:
                dve.wait_ge(drained, m + 1)
                dve.tensor_tensor(u[:, 2:T + 2], cvb[:, 0], cvb[:, 1], ALU.mult).then_inc(*dve_made("u"))
                dve.wait_ge(*dve_made.by("u", jt))
                dve.tensor_scalar(conv[:, :], u[:, 0:T], vec(core, "conv2", jt), None, ALU.mult
                                  ).then_inc(*dve_made("tap0"))
                dve.wait_ge(*dve_made.by("tap0", jt))
                dve.scalar_tensor_tensor(conv[:, :], u[:, 1:T + 1], vec(core, "conv2", KD + jt), conv[:, :],
                                         ALU.mult, ALU.add).then_inc(*dve_made("tap1"))
                dve.wait_ge(*dve_made.by("tap1", jt))
                dve.scalar_tensor_tensor(conv[:, :], u[:, 2:T + 2], vec(core, "conv2", 2 * KD + jt), conv[:, :],
                                         ALU.mult, ALU.add).then_inc(*dve_made("conv"))
            if r % 3 == 2:
                dve.wait_ge(drained, m + 1)
                dve.wait_ge(*dve_made.by("conv", jt))
                dve.tensor_tensor(tile_of(y, jt), cvb[:, 2], conv[:, :], ALU.mult).then_inc(*dve_made("y"))

        def dve_first(dve):
            dve_made.begin(dve)
            dve.memset(u[:, :], 0.0).then_inc(padded, 1)
            dve.wait_ge(padded, 1)

        dense(core, "sc", w, x_hi, x_lo, [(0, 3 * KD, "third")], act_epilogue, dve_epilogue, unroll=6,
              dve_first=dve_first)


def load_constants(core, d_vec, d_const):
    nc = core.nc
    loaded = core.sem("in_loaded")
    with nc.Block() as block:
        @block.sync
        def _(sp):
            sp.dma_start(core.vec[:, :], d_vec).then_inc(loaded, 16)
            sp.dma_start(core.const[:, :], d_const[:, 0:N_STAY * P]).then_inc(loaded, 16)
            sp.wait_ge(loaded, 32)


def build(nc, a, out):
    with ExitStack() as ctx:
        core = Core(nc, ctx)
        core.vec = ctx.enter_context(nc.sbuf_tensor("vec", [P, NVEC], F32))
        core.const = ctx.enter_context(nc.sbuf_tensor("const", [P, N_STAY * P], F32))
        big = ctx.enter_context(nc.sbuf_tensor("big", [P, 20, T], F32))
        z, y_gla = big[:, 0:16], big[:, 16:20]

        h = z[:, 0:8]
        load_constants(core, a["vec"], a["const"])
        with ExitStack() as scope:
            xn_hi = scope.enter_context(nc.sbuf_tensor("xn_hi", [P, KD, T], F32R))
            xn_lo = scope.enter_context(nc.sbuf_tensor("xn_lo", [P, KD, T], F32R))
            with ExitStack() as weights:
                gp = DenseWeights(core, weights, "gp", a["w_gla"])
                joint(core, "pre", None, None, h, core.vec[:, VEC["norm_mix_pre"]:VEC["norm_mix_pre"] + 8], None,
                      xn_hi, xn_lo, ahead=gp.ahead, source=a["x"])
                gla_project(core, gp, xn_hi, xn_lo, z, z[:, 12])
            with ExitStack() as inner:
                sums = inner.enter_context(nc.sbuf_tensor("gla_sums", [P, 2, 2, T], F32))
                gla_decay(core, a["const"], a["gla_a_up"], z[:, 12], sums)
                gla_mix(core, a["const"], z, sums, y_gla, z[:, 12:16].rearrange("p a t -> p (a t)"))
            rp = DenseWeights(core, scope, "rp", a["w_rwkv"])
            gla_finish(core, z, y_gla, rp.ahead)
            rwkv_project(core, rp, xn_hi, xn_lo, z)
        gains = ctx.enter_context(nc.sbuf_tensor("gains", [P, 6, KD], F32))
        rwkv_mix(core, a["const"], a["lora"], a["ada"], z, gains)
        core.clear_sems()
        x_hi = ctx.enter_context(nc.sbuf_tensor("x_hi", [P, KD, T], F32R))
        x_lo = ctx.enter_context(nc.sbuf_tensor("x_lo", [P, KD, T], F32R))
        y, spare = z[:, 8:16], big[:, 16:20]

        def own(name):
            return core.vec[:, VEC[name]:VEC[name] + KD]

        with ExitStack() as weights:
            wo = DenseWeights(core, weights, "wo", a["w_out"])
            rwkv_finish(core, a["lora"], z, y_gla, x_hi, x_lo, wo.ahead)
            project(core, "wo", wo, x_hi, x_lo, y, load=(h, a["x"]))
        with ExitStack() as weights:
            f1 = SwigluWeights(core, weights, "f1", a["ffn_gate"], a["ffn_up"], a["ffn_down"], spare)
            joint(core, "mix", y, own("norm_mix_post"), h, own("norm_ffn_pre"), None, x_hi, x_lo, ahead=f1.ahead)
            swiglu(core, "f1", f1, x_hi, x_lo, y)
        joint(core, "ffn", y, own("norm_ffn_post"), h, None, None, x_hi, x_lo, load=(spare[:, 0:2], a["p"]))
        with ExitStack() as weights:
            p_hi = weights.enter_context(nc.sbuf_tensor("p_hi", [P, 2, T], F32R))
            p_lo = weights.enter_context(nc.sbuf_tensor("p_lo", [P, 2, T], F32R))
            pe = DenseWeights(core, weights, "pe", a["ple_proj"])
            eg = DenseWeights(core, weights, "eg", a["ple_gate"])
            split_tiles(core, "ps", [spare[:, 0], spare[:, 1]], p_hi, p_lo, Ahead(pe.ahead.tiles + eg.ahead.tiles))
            project(core, "pe", pe, p_hi, p_lo, y)
            embedding_gate(core, eg, x_hi, x_lo, y)
        with ExitStack() as weights:
            sc = DenseWeights(core, weights, "sc", a["conv_in"])
            joint(core, "ple", y, own("norm_ple"), h, gains[:, 0], gains[:, 1], x_hi, x_lo, ahead=sc.ahead)
            short_conv(core, sc, x_hi, x_lo, y)
        with ExitStack() as weights:
            co = DenseWeights(core, weights, "co", a["conv_out"])
            split_tiles(core, "cs", [y[:, n] for n in range(KD)], x_hi, x_lo, co.ahead)
            project(core, "co", co, x_hi, x_lo, y)
        core.clear_sems()
        with ExitStack() as weights:
            f2 = SwigluWeights(core, weights, "f2", a["ffn2_gate"], a["ffn2_up"], a["ffn2_down"], spare)
            joint(core, "conv", y, gains[:, 2], h, gains[:, 3], gains[:, 4], x_hi, x_lo, ahead=f2.ahead)
            swiglu(core, "f2", f2, x_hi, x_lo, y)
        joint(core, "out", y, gains[:, 5], h, None, None, None, None, store=out)


def tiled(w):
    k, n = w.shape
    nt = -(-n // P)
    full = np.zeros((k, nt * P), w.dtype)
    full[:, :n] = w
    return np.ascontiguousarray(full.reshape(k // P, P, nt, P).transpose(2, 1, 0, 3).reshape(nt, P, k))


def by_tile(v):
    return np.ascontiguousarray(np.asarray(v).reshape(-1, P).T)


def channels_first(x):
    t, c = x.shape
    return np.ascontiguousarray(x.T.reshape(c // P, P, t).transpose(1, 0, 2))


def laid_out(i):
    w_in, mu = i["w_in"][0], i["rwkv_mu"][0]
    zero = lambda n: np.zeros((w_in.shape[0], n), w_in.dtype)
    w_rwkv = np.concatenate([w_in[:, :1728], zero(64), w_in[:, 1728:1856]], axis=1)
    g = w_in[:, 1856:]
    w_gla = np.concatenate([g[:, :1536], g[:, 1536:1552], zero(16), g[:, 1552:1568], zero(80)], axis=1)
    a = {"x": channels_first(i["x"][0]), "p": channels_first(i["p"][0, 0]), "const": constants()}
    a["w_rwkv"], a["w_gla"] = tiled(w_rwkv), tiled(w_gla)
    up = np.zeros((P, 256), w_in.dtype)
    up[0:16], up[32:48] = i["gla_a_up"][0, 0], i["gla_a_up"][0, 1]
    a["gla_a_up"] = up
    lora = np.zeros((P, 3, 512), w_in.dtype)
    lora[:, 0] = i["rwkv_w_up"][0].reshape(P, 512)
    lora[0:64, 1] = i["rwkv_a_up"][0]
    lora[:, 2] = i["rwkv_g_up"][0]
    a["lora"] = lora
    a["w_out"] = tiled(i["w_out"][0])
    for n in ("gate", "up"):
        a[f"ffn_{n}"] = tiled(i[f"ffn_{n}"][0])
    a["ffn_down"] = np.ascontiguousarray(i["ffn_down"][0].reshape(NF, P, D))
    a["ple_proj"], a["ple_gate"] = tiled(i["ple_proj"][0]), tiled(i["ple_gate"][0])
    a["ada"] = tiled(i["ada_w_2"][0])
    c_in = i["conv_w_in_2"][0].reshape(D, 3, KD, P)
    a["conv_in"] = tiled(c_in[:, [1, 2, 0]].transpose(0, 2, 1, 3).reshape(D, 3 * D))
    a["conv_out"] = tiled(i["conv_w_out_2"][0])
    gu = i["ffn_w_gate_up_2"][0]
    a["ffn2_gate"], a["ffn2_up"] = tiled(gu[:, :FF]), tiled(gu[:, FF:])
    a["ffn2_down"] = np.ascontiguousarray(i["ffn_w_down_2"][0].reshape(NF, P, D))
    mu_l = np.concatenate([mu[:1728], np.zeros(64, mu.dtype), mu[1728:]])
    fields = {
        "norm_mix_pre": i["norm_mix_pre"], "norm_mix_post": i["norm_mix_post"], "norm_ffn_pre": i["norm_ffn_pre"],
        "norm_ffn_post": i["norm_ffn_post"], "norm_ple": i["norm_ple"], "mu": mu_l, "w0": i["rwkv_w0"],
        "a0": i["rwkv_a0"], "k_k": i["rwkv_k_k"], "k_a": i["rwkv_k_a"], "r_k": i["rwkv_r_k"],
        "ln_w": i["rwkv_ln_w"], "ln_b": i["rwkv_ln_b"], "conv": i["gla_conv"], "a_b": i["gla_a_b"],
        "gla_norm": i["gla_norm"], "ple_b": i["ple_gate_b"], "c": i["c_2"], "ada_b": i["ada_b_2"],
        "gains2": i["norm_gains_2"], "conv2": i["conv_w_2"],
    }
    a["vec"] = np.concatenate([by_tile(fields[n]) for n, _ in VEC_FIELDS], axis=1)
    return a


def kernel(**inputs):
    import concourse.bacc as bacc
    from concourse.bass_utils import run_bass_kernel_spmd

    nc = bacc.Bacc("TRN2", target_bir_lowering=False, num_devices=1)
    arrays = {f"in_{n}": v for n, v in laid_out({n: np.asarray(v) for n, v in inputs.items()}).items()}
    aps = {n[3:]: nc.dram_tensor(n, v.shape, mybir.dt.from_np(v.dtype), kind="ExternalInput").ap()
           for n, v in arrays.items()}
    out = nc.dram_tensor("out", (P, KD, T), F32, kind="ExternalOutput").ap()
    build(nc, aps, out)
    r = run_bass_kernel_spmd(nc, [arrays], core_ids=[0])
    got = r.results[0]["out"]
    return np.ascontiguousarray(got.transpose(2, 1, 0)).reshape(1, T, D)
```
